# Optimizing a Trainium2 kernel written in Bass

```python
import math
import jax
import jax.numpy as jnp
from jax import lax
import numpy as np
import jax, jax.numpy as jnp

D_MODEL = 1024
BATCH = 1
SEQ = 256
DEPTH = 2

CHUNK = 64
QBLK = 128
HEAD_DIM = 64
NORM_EPS = 1e-6

A_HEADS = 4
A_QK_WIDTH = A_HEADS * 2 * HEAD_DIM
A_VDIM = 2 * HEAD_DIM
A_WIDTH = A_HEADS * A_VDIM

B_HEADS = 8
B_WIDTH = B_HEADS * HEAD_DIM

C_HEADS = 8
C_KV_HEADS = 2
C_GROUP = C_HEADS // C_KV_HEADS
C_WIDTH = C_HEADS * HEAD_DIM
C_KV_WIDTH = C_KV_HEADS * HEAD_DIM
WINDOW = 128
WIN_CHUNKS = WINDOW // CHUNK

D_HEADS = 8
D_WIDTH = D_HEADS * HEAD_DIM
D_LEFT_CHUNKS = 8
D_BAND = (D_LEFT_CHUNKS + 1) * CHUNK
REL_MAX = 256
REL_SIZE = REL_MAX + CHUNK

EVEN_SPLITS = (A_QK_WIDTH, A_QK_WIDTH, A_WIDTH, A_WIDTH, B_WIDTH, B_WIDTH, B_WIDTH, B_WIDTH, B_HEADS)
ODD_SPLITS = (C_WIDTH, C_KV_WIDTH, C_KV_WIDTH, C_WIDTH, D_WIDTH, D_WIDTH, D_WIDTH, D_WIDTH)
P_EVEN = sum(EVEN_SPLITS)
P_ODD = sum(ODD_SPLITS)
MIX_EVEN = A_WIDTH + B_WIDTH
MIX_ODD = C_WIDTH + D_WIDTH


def rms_norm(x, g):
    xf = x.astype(jnp.float32)
    y = xf * lax.rsqrt(jnp.mean(xf * xf, axis=-1, keepdims=True) + NORM_EPS)
    return (y * g.astype(jnp.float32)).astype(x.dtype)

def split_cols(z, sizes):
    idx = np.cumsum(np.array(sizes))[:-1].tolist()
    return jnp.split(z, idx, axis=-1)

def alibi_slopes(n_heads):
    return 2.0 ** (-8.0 * jnp.arange(1, n_heads + 1, dtype=jnp.float32) / n_heads)

def sweep_query_blocks(fn, n_blocks):
    out = lax.map(fn, jnp.arange(n_blocks))
    out = jnp.moveaxis(out, 0, 1)
    return out.reshape((out.shape[0], -1) + out.shape[3:])

def diff_attention(q, k, v, lam, lam_init, subln_g):
    bsz, seq = q.shape[:2]
    scale = HEAD_DIM ** -0.5
    slopes = alibi_slopes(A_HEADS)
    tk = jnp.arange(seq)

    def block(b):
        start = b * QBLK
        tq = start + jnp.arange(QBLK)
        qb = lax.dynamic_slice_in_dim(q, start, QBLK, axis=1)
        s = jnp.einsum("bqhcd,bkhcd->bhcqk", qb, k).astype(jnp.float32) * scale
        dist = jnp.abs(tq[:, None] - tk[None, :]).astype(jnp.float32)
        s = s - (slopes[:, None, None] * dist)[None, :, None]
        allowed = (tk[None, :] // CHUNK) <= (tq[:, None] // CHUNK)
        s = jnp.where(allowed, s, -jnp.inf)
        p = jax.nn.softmax(s, axis=-1)
        w = p[:, :, 0] - lam * p[:, :, 1]
        return jnp.einsum("bhqk,bkhe->bqhe", w.astype(v.dtype), v)

    o = sweep_query_blocks(block, seq // QBLK)
    o = rms_norm(o, subln_g) * (1.0 - lam_init)
    return o.reshape(bsz, seq, A_WIDTH)

def forgetting_attention(q, k, v, log_f):
    bsz, seq = q.shape[:2]
    scale = HEAD_DIM ** -0.5
    cum = jnp.transpose(jnp.cumsum(log_f, axis=1), (0, 2, 1))
    tk = jnp.arange(seq)

    def block(b):
        start = b * QBLK
        tq = start + jnp.arange(QBLK)
        qb = lax.dynamic_slice_in_dim(q, start, QBLK, axis=1)
        cq = lax.dynamic_slice_in_dim(cum, start, QBLK, axis=2)
        s = jnp.einsum("bqhd,bkhd->bhqk", qb, k).astype(jnp.float32) * scale
        s = s + cq[..., :, None] - cum[:, :, None, :]
        s = jnp.where(tk[None, :] <= tq[:, None], s, -jnp.inf)
        p = jax.nn.softmax(s, axis=-1)
        return jnp.einsum("bhqk,bkhd->bqhd", p.astype(v.dtype), v)

    o = sweep_query_blocks(block, seq // QBLK)
    return o.reshape(bsz, seq, B_WIDTH)

def sliding_window_sink_attention(q, k, v, sinks):
    bsz, seq = q.shape[:2]
    nb = seq // QBLK
    scale = HEAD_DIM ** -0.5

    def band(t):
        tp = jnp.pad(t, ((0, 0), (QBLK, 0), (0, 0), (0, 0)))
        tb = tp.reshape(bsz, nb + 1, QBLK, C_KV_HEADS, HEAD_DIM)
        return jnp.concatenate([tb[:, :-1], tb[:, 1:]], axis=2)

    kb, vb = band(k), band(v)
    qb = q.reshape(bsz, nb, QBLK, C_KV_HEADS, C_GROUP, HEAD_DIM)
    s = jnp.einsum("bnqkgd,bnskd->bnkgqs", qb, kb).astype(jnp.float32) * scale
    iq = jnp.arange(QBLK)
    ik = jnp.arange(2 * QBLK) - QBLK
    dist = jnp.abs(iq[:, None] - ik[None, :]).astype(jnp.float32)
    slopes = alibi_slopes(C_HEADS).reshape(C_KV_HEADS, C_GROUP, 1, 1)
    s = s - (slopes * dist)[None, None]
    chunk_diff = (iq[:, None] // CHUNK + QBLK // CHUNK) - ((ik[None, :] + QBLK) // CHUNK)
    in_window = (chunk_diff >= 0) & (chunk_diff <= WIN_CHUNKS)
    valid = (jnp.arange(nb)[:, None] * QBLK + ik[None, :]) >= 0
    mask = in_window[None] & valid[:, None, :]
    s = jnp.where(mask[None, :, None, None], s, -jnp.inf)
    sink = jnp.broadcast_to(sinks.astype(jnp.float32).reshape(1, 1, C_KV_HEADS, C_GROUP, 1, 1),
                            s.shape[:-1] + (1,))
    p = jax.nn.softmax(jnp.concatenate([s, sink], axis=-1), axis=-1)[..., :-1]
    o = jnp.einsum("bnkgqs,bnskd->bnqkgd", p.astype(v.dtype), vb)
    return o.reshape(bsz, seq, C_WIDTH)

def chunk_relpos_attention(q, k, v, rel_table):
    bsz, seq = q.shape[:2]
    nc = seq // CHUNK
    scale = HEAD_DIM ** -0.5
    idx = jnp.arange(nc)[:, None] + jnp.arange(D_LEFT_CHUNKS + 1)[None, :]

    def band(t):
        tp = jnp.pad(t, ((0, 0), (D_LEFT_CHUNKS * CHUNK, 0), (0, 0), (0, 0)))
        tp = tp.reshape(bsz, nc + D_LEFT_CHUNKS, CHUNK, D_HEADS, HEAD_DIM)
        return tp[:, idx].reshape(bsz, nc, D_BAND, D_HEADS, HEAD_DIM)

    kb, vb = band(k), band(v)
    qc = q.reshape(bsz, nc, CHUNK, D_HEADS, HEAD_DIM)
    s = jnp.einsum("bnqhd,bnkhd->bnhqk", qc, kb).astype(jnp.float32) * scale
    iq = jnp.arange(CHUNK)
    ik = jnp.arange(D_BAND) - D_LEFT_CHUNKS * CHUNK
    rel = iq[:, None] - ik[None, :]
    ridx = jnp.clip(rel, -(CHUNK - 1), REL_MAX) + (CHUNK - 1)
    bias = rel_table[:, ridx].astype(jnp.float32)
    s = s + bias[None, None]
    valid = (jnp.arange(nc)[:, None] * CHUNK + ik[None, :]) >= 0
    s = jnp.where(valid[None, :, None, None, :], s, -jnp.inf)
    p = jax.nn.softmax(s, axis=-1)
    o = jnp.einsum("bnhqk,bnkhd->bnqhd", p.astype(v.dtype), vb)
    return o.reshape(bsz, seq, D_WIDTH)

def even_layer(x, ln_g, w_in, w_out, a_qn_g, a_kn_g, a_lq1, a_lk1, a_lq2, a_lk2, a_subln_g,
               b_qn_g, b_kn_g, b_f_bias, layer_idx):
    bsz, seq, _ = x.shape
    z = rms_norm(x, ln_g) @ w_in
    aq, ak, av, ag, bq, bk, bv, bg, bf = split_cols(z, EVEN_SPLITS)
    aq = rms_norm(aq.reshape(bsz, seq, A_HEADS, 2, HEAD_DIM), a_qn_g)
    ak = rms_norm(ak.reshape(bsz, seq, A_HEADS, 2, HEAD_DIM), a_kn_g)
    av = av.reshape(bsz, seq, A_HEADS, A_VDIM)
    lam_init = 0.8 - 0.6 * math.exp(-0.3 * layer_idx)
    f32 = jnp.float32
    lam = (jnp.exp(jnp.sum(a_lq1.astype(f32) * a_lk1.astype(f32)))
           - jnp.exp(jnp.sum(a_lq2.astype(f32) * a_lk2.astype(f32))) + lam_init)
    a_out = diff_attention(aq, ak, av, lam, lam_init, a_subln_g)
    bq = rms_norm(bq.reshape(bsz, seq, B_HEADS, HEAD_DIM), b_qn_g)
    bk = rms_norm(bk.reshape(bsz, seq, B_HEADS, HEAD_DIM), b_kn_g)
    bv = bv.reshape(bsz, seq, B_HEADS, HEAD_DIM)
    log_f = jax.nn.log_sigmoid(bf.astype(f32) + b_f_bias.astype(f32))
    b_out = forgetting_attention(bq, bk, bv, log_f)
    mixed = jnp.concatenate([a_out * jax.nn.silu(ag), b_out * jax.nn.silu(bg)], axis=-1)
    return x + mixed @ w_out

def odd_layer(x, ln_g, w_in, w_out, c_qn_g, c_kn_g, c_sinks, d_qn_g, d_kn_g, d_rel_bias):
    bsz, seq, _ = x.shape
    z = rms_norm(x, ln_g) @ w_in
    cq, ck, cv, cg, dq, dk, dv, dg = split_cols(z, ODD_SPLITS)
    cq = rms_norm(cq.reshape(bsz, seq, C_HEADS, HEAD_DIM), c_qn_g)
    ck = rms_norm(ck.reshape(bsz, seq, C_KV_HEADS, HEAD_DIM), c_kn_g)
    cv = cv.reshape(bsz, seq, C_KV_HEADS, HEAD_DIM)
    c_out = sliding_window_sink_attention(cq, ck, cv, c_sinks)
    dq = rms_norm(dq.reshape(bsz, seq, D_HEADS, HEAD_DIM), d_qn_g)
    dk = rms_norm(dk.reshape(bsz, seq, D_HEADS, HEAD_DIM), d_kn_g)
    dv = dv.reshape(bsz, seq, D_HEADS, HEAD_DIM)
    d_out = chunk_relpos_attention(dq, dk, dv, d_rel_bias)
    mixed = jnp.concatenate([c_out * jax.nn.silu(cg), d_out * jax.nn.silu(dg)], axis=-1)
    return x + mixed @ w_out

def first_inputs(seed: int = 0) -> dict:
    key = jax.random.key(seed)
    ne = (DEPTH + 1) // 2
    no = DEPTH // 2
    ks = jax.random.split(key, 23)

    def nrm(k, shape, s):
        return s * jax.random.normal(k, shape, jnp.float32)

    def gain(k, shape):
        return 1.0 + 0.1 * jax.random.normal(k, shape, jnp.float32)

    return {
        "x": jax.random.normal(ks[0], (BATCH, SEQ, D_MODEL), jnp.float32),
        "even_ln_g": gain(ks[1], (ne, D_MODEL)),
        "even_w_in": nrm(ks[2], (ne, D_MODEL, P_EVEN), D_MODEL ** -0.5),
        "even_w_out": nrm(ks[3], (ne, MIX_EVEN, D_MODEL), MIX_EVEN ** -0.5),
        "a_q_norm_g": gain(ks[4], (ne, HEAD_DIM)),
        "a_k_norm_g": gain(ks[5], (ne, HEAD_DIM)),
        "a_lambda_q1": nrm(ks[6], (ne, HEAD_DIM), 0.1),
        "a_lambda_k1": nrm(ks[7], (ne, HEAD_DIM), 0.1),
        "a_lambda_q2": nrm(ks[8], (ne, HEAD_DIM), 0.1),
        "a_lambda_k2": nrm(ks[9], (ne, HEAD_DIM), 0.1),
        "a_subln_g": gain(ks[10], (ne, A_VDIM)),
        "b_q_norm_g": gain(ks[11], (ne, HEAD_DIM)),
        "b_k_norm_g": gain(ks[12], (ne, HEAD_DIM)),
        "b_forget_bias": 3.0 + nrm(ks[13], (ne, B_HEADS), 0.5),
        "odd_ln_g": gain(ks[14], (no, D_MODEL)),
        "odd_w_in": nrm(ks[15], (no, D_MODEL, P_ODD), D_MODEL ** -0.5),
        "odd_w_out": nrm(ks[16], (no, MIX_ODD, D_MODEL), MIX_ODD ** -0.5),
        "c_q_norm_g": gain(ks[17], (no, HEAD_DIM)),
        "c_k_norm_g": gain(ks[18], (no, HEAD_DIM)),
        "c_sinks": nrm(ks[19], (no, C_HEADS), 0.5),
        "d_q_norm_g": gain(ks[20], (no, HEAD_DIM)),
        "d_k_norm_g": gain(ks[21], (no, HEAD_DIM)),
        "d_rel_bias": nrm(ks[22], (no, D_HEADS, REL_SIZE), 0.5),
    }

def first_block(x, even_ln_g, even_w_in, even_w_out, a_q_norm_g, a_k_norm_g, a_lambda_q1,
              a_lambda_k1, a_lambda_q2, a_lambda_k2, a_subln_g, b_q_norm_g, b_k_norm_g,
              b_forget_bias, odd_ln_g, odd_w_in, odd_w_out, c_q_norm_g, c_k_norm_g, c_sinks,
              d_q_norm_g, d_k_norm_g, d_rel_bias):
    for i in range(DEPTH):
        j = i // 2
        if i % 2 == 0:
            x = even_layer(x, even_ln_g[j], even_w_in[j], even_w_out[j], a_q_norm_g[j],
                           a_k_norm_g[j], a_lambda_q1[j], a_lambda_k1[j], a_lambda_q2[j],
                           a_lambda_k2[j], a_subln_g[j], b_q_norm_g[j], b_k_norm_g[j],
                           b_forget_bias[j], i)
        else:
            x = odd_layer(x, odd_ln_g[j], odd_w_in[j], odd_w_out[j], c_q_norm_g[j],
                          c_k_norm_g[j], c_sinks[j], d_q_norm_g[j], d_k_norm_g[j],
                          d_rel_bias[j])
    return x


N_MIXERS = 2
ROPE_THETA = 500000.0
EPS = 1e-6

A_HEADS_2 = 16
A_KV_HEADS = 4
A_HEAD_DIM = 64
A_ROT = A_HEAD_DIM // 4
IDX_HEADS = 8
IDX_DIM = 64
IDX_ROT = IDX_DIM // 4
IDX_TOPK_MAX = 256
IDX_WEIGHT_SCALE = (IDX_HEADS ** -0.5) * (IDX_DIM ** -0.5)
A_QBLK = CHUNK
A_IN = A_HEADS_2 * A_HEAD_DIM + 2 * A_KV_HEADS * A_HEAD_DIM + IDX_HEADS * IDX_DIM + IDX_DIM + IDX_HEADS

B_HEADS_2 = 16
B_NOPE = 64
B_ROPE = 32
B_V = 64
B_Q_LORA = 384
B_KV_LORA = 256
B_QBLK = 128
B_IN = B_Q_LORA + B_KV_LORA + B_ROPE

D_FF = 4 * D_MODEL

N_A = (DEPTH + 1) // 2
N_B = DEPTH // 2


def rms_norm_2(x, g):
    xf = x.astype(jnp.float32)
    y = xf * lax.rsqrt(jnp.mean(xf * xf, axis=-1, keepdims=True) + EPS)
    return (y * g.astype(jnp.float32)).astype(x.dtype)

def rope_angles(positions, rot_dim):
    inv = ROPE_THETA ** (-jnp.arange(0, rot_dim, 2, dtype=jnp.float32) / rot_dim)
    ang = positions.astype(jnp.float32)[..., None] * inv
    return jnp.cos(ang), jnp.sin(ang)

def apply_rope(x, cos, sin):
    half = x.shape[-1] // 2
    x1 = x[..., :half].astype(jnp.float32)
    x2 = x[..., half:].astype(jnp.float32)
    c = cos[:, :, None, :]
    s = sin[:, :, None, :]
    return jnp.concatenate([x1 * c - x2 * s, x2 * c + x1 * s], axis=-1).astype(x.dtype)

def partial_rope(x, cos, sin, rot):
    return jnp.concatenate([apply_rope(x[..., :rot], cos, sin), x[..., rot:]], axis=-1)

def dsa_mixer(h, w_in, w_out, cos_a, sin_a, cos_i, sin_i):
    bsz, seq, _ = h.shape
    f32 = jnp.float32
    n_q = A_HEADS_2 * A_HEAD_DIM
    n_kv = A_KV_HEADS * A_HEAD_DIM
    n_qi = IDX_HEADS * IDX_DIM
    cuts = [n_q, n_q + n_kv, n_q + 2 * n_kv, n_q + 2 * n_kv + n_qi, n_q + 2 * n_kv + n_qi + IDX_DIM]
    proj = h @ w_in
    q, k, v, qi, ki, wi = jnp.split(proj, cuts, axis=-1)
    q = partial_rope(q.reshape(bsz, seq, A_HEADS_2, A_HEAD_DIM), cos_a, sin_a, A_ROT)
    k = partial_rope(k.reshape(bsz, seq, A_KV_HEADS, A_HEAD_DIM), cos_a, sin_a, A_ROT)
    v = v.reshape(bsz, seq, A_KV_HEADS, A_HEAD_DIM)
    qi = partial_rope(qi.reshape(bsz, seq, IDX_HEADS, IDX_DIM), cos_i, sin_i, IDX_ROT)
    ki = partial_rope(ki[:, :, None, :], cos_i, sin_i, IDX_ROT)[:, :, 0, :]
    wi = wi.astype(f32) * IDX_WEIGHT_SCALE

    top_k = min(IDX_TOPK_MAX, seq // 4)
    group = A_HEADS_2 // A_KV_HEADS
    scale = A_HEAD_DIM ** -0.5
    key_pos = jnp.arange(seq)

    def block(i):
        start = i * A_QBLK
        qb = lax.dynamic_slice_in_dim(q, start, A_QBLK, axis=1)
        qib = lax.dynamic_slice_in_dim(qi, start, A_QBLK, axis=1)
        wib = lax.dynamic_slice_in_dim(wi, start, A_QBLK, axis=1)
        q_pos = start + jnp.arange(A_QBLK)
        chunk_end = (q_pos // CHUNK + 1) * CHUNK
        logits = jnp.einsum('bthd,bsd->bths', qib, ki, preferred_element_type=f32)
        score = jnp.einsum('bths,bth->bts', jax.nn.relu(logits), wib)
        visible = key_pos[None, :] < chunk_end[:, None]
        score = jnp.where(visible[None], score, -jnp.inf)
        _, sel = lax.top_k(score, top_k)
        sel_ok = sel < chunk_end[None, :, None]
        flat = sel.reshape(bsz, A_QBLK * top_k)[:, :, None, None]
        kg = jnp.take_along_axis(k, flat, axis=1).reshape(bsz, A_QBLK, top_k, A_KV_HEADS, A_HEAD_DIM)
        vg = jnp.take_along_axis(v, flat, axis=1).reshape(bsz, A_QBLK, top_k, A_KV_HEADS, A_HEAD_DIM)
        qg = qb.reshape(bsz, A_QBLK, A_KV_HEADS, group, A_HEAD_DIM)
        s = jnp.einsum('btgrd,btkgd->btgrk', qg, kg, preferred_element_type=f32) * scale
        s = jnp.where(sel_ok[:, :, None, None, :], s, -jnp.inf)
        p = jax.nn.softmax(s, axis=-1)
        o = jnp.einsum('btgrk,btkgd->btgrd', p.astype(vg.dtype), vg, preferred_element_type=f32)
        return o.reshape(bsz, A_QBLK, A_HEADS_2 * A_HEAD_DIM).astype(h.dtype)

    o = lax.map(block, jnp.arange(seq // A_QBLK))
    o = jnp.moveaxis(o, 0, 1).reshape(bsz, seq, A_HEADS_2 * A_HEAD_DIM)
    return o @ w_out

def mla_mixer(h, w_in, q_norm, kv_norm, w_q_up, w_kv_up, w_out, cos_b, sin_b):
    bsz, seq, _ = h.shape
    f32 = jnp.float32
    proj = h @ w_in
    cq, ckv, kr = jnp.split(proj, [B_Q_LORA, B_Q_LORA + B_KV_LORA], axis=-1)
    cq = rms_norm_2(cq, q_norm)
    ckv = rms_norm_2(ckv, kv_norm)
    qf = (cq @ w_q_up).reshape(bsz, seq, B_HEADS_2, B_NOPE + B_ROPE)
    q_nope, q_rope = qf[..., :B_NOPE], apply_rope(qf[..., B_NOPE:], cos_b, sin_b)
    kr = apply_rope(kr[:, :, None, :], cos_b, sin_b)[:, :, 0, :]
    kv = (ckv @ w_kv_up).reshape(bsz, seq, B_HEADS_2, B_NOPE + B_V)
    k_nope, v = kv[..., :B_NOPE], kv[..., B_NOPE:]
    scale = (B_NOPE + B_ROPE) ** -0.5
    key_pos = jnp.arange(seq)

    def block(i):
        start = i * B_QBLK
        qn = lax.dynamic_slice_in_dim(q_nope, start, B_QBLK, axis=1)
        qr = lax.dynamic_slice_in_dim(q_rope, start, B_QBLK, axis=1)
        s = (jnp.einsum('bthd,bshd->bhts', qn, k_nope, preferred_element_type=f32)
             + jnp.einsum('bthd,bsd->bhts', qr, kr, preferred_element_type=f32)) * scale
        q_pos = start + jnp.arange(B_QBLK)
        chunk_end = (q_pos // CHUNK + 1) * CHUNK
        mask = key_pos[None, :] < chunk_end[:, None]
        s = jnp.where(mask[None, None], s, -jnp.inf)
        p = jax.nn.softmax(s, axis=-1)
        o = jnp.einsum('bhts,bshd->bthd', p.astype(v.dtype), v, preferred_element_type=f32)
        return o.reshape(bsz, B_QBLK, B_HEADS_2 * B_V).astype(h.dtype)

    o = lax.map(block, jnp.arange(seq // B_QBLK))
    o = jnp.moveaxis(o, 0, 1).reshape(bsz, seq, B_HEADS_2 * B_V)
    return o @ w_out

def squared_relu_mlp(h, w_up, w_down):
    a = jax.nn.relu(h @ w_up)
    return (a * a) @ w_down

def second_inputs(seed: int = 0) -> dict:
    key = jax.random.key(seed)
    ks = jax.random.split(key, 20)
    f32 = jnp.float32

    def nrm(k, shape, fan_in):
        return jax.random.normal(k, shape, f32) * (fan_in ** -0.5)

    def gain(k, shape):
        return 1.0 + 0.02 * jax.random.normal(k, shape, f32)

    x = jax.random.normal(ks[0], (BATCH, SEQ, D_MODEL), f32)
    starts = jax.random.randint(ks[1], (BATCH, 1), 0, 64, dtype=jnp.int32) * CHUNK
    positions = (starts + jnp.arange(SEQ, dtype=jnp.int32)[None, :]).astype(jnp.int32)
    return {
        'x': x,
        'positions': positions,
        'attn_norm': gain(ks[2], (DEPTH, D_MODEL)),
        'mlp_norm': gain(ks[3], (DEPTH, D_MODEL)),
        'a_w_in': nrm(ks[4], (N_A, D_MODEL, A_IN), D_MODEL),
        'a_w_out': nrm(ks[5], (N_A, A_HEADS_2 * A_HEAD_DIM, D_MODEL), A_HEADS_2 * A_HEAD_DIM),
        'b_w_in': nrm(ks[6], (N_B, D_MODEL, B_IN), D_MODEL),
        'b_q_norm': gain(ks[7], (N_B, B_Q_LORA)),
        'b_kv_norm': gain(ks[8], (N_B, B_KV_LORA)),
        'b_w_q_up': nrm(ks[9], (N_B, B_Q_LORA, B_HEADS_2 * (B_NOPE + B_ROPE)), B_Q_LORA),
        'b_w_kv_up': nrm(ks[10], (N_B, B_KV_LORA, B_HEADS_2 * (B_NOPE + B_V)), B_KV_LORA),
        'b_w_out': nrm(ks[11], (N_B, B_HEADS_2 * B_V, D_MODEL), B_HEADS_2 * B_V),
        'mlp_w_up': nrm(ks[12], (DEPTH, D_MODEL, D_FF), D_MODEL),
        'mlp_w_down': nrm(ks[13], (DEPTH, D_FF, D_MODEL), D_FF),
        'final_norm': gain(ks[14], (D_MODEL,)),
    }

def second_block(x, positions, attn_norm, mlp_norm, a_w_in, a_w_out, b_w_in, b_q_norm, b_kv_norm,
              b_w_q_up, b_w_kv_up, b_w_out, mlp_w_up, mlp_w_down, final_norm):
    cos_a, sin_a = rope_angles(positions, A_ROT)
    cos_i, sin_i = rope_angles(positions, IDX_ROT)
    cos_b, sin_b = rope_angles(positions, B_ROPE)
    for i in range(DEPTH):
        h = rms_norm_2(x, attn_norm[i])
        j = i // N_MIXERS
        if i % N_MIXERS == 0:
            x = x + dsa_mixer(h, a_w_in[j], a_w_out[j], cos_a, sin_a, cos_i, sin_i)
        else:
            x = x + mla_mixer(h, b_w_in[j], b_q_norm[j], b_kv_norm[j], b_w_q_up[j],
                              b_w_kv_up[j], b_w_out[j], cos_b, sin_b)
        h = rms_norm_2(x, mlp_norm[i])
        x = x + squared_relu_mlp(h, mlp_w_up[i], mlp_w_down[i])
    return rms_norm_2(x, final_norm)


def setup_inputs(seed=0):
    out = dict(first_inputs(seed))
    for name, value in second_inputs(seed + 1).items():
        if name != "x":
            out[name + "_2"] = value
    return out


def reference(
    x, even_ln_g, even_w_in, even_w_out, a_q_norm_g, a_k_norm_g, a_lambda_q1, a_lambda_k1,
    a_lambda_q2, a_lambda_k2, a_subln_g, b_q_norm_g, b_k_norm_g, b_forget_bias, odd_ln_g,
    odd_w_in, odd_w_out, c_q_norm_g, c_k_norm_g, c_sinks, d_q_norm_g, d_k_norm_g, d_rel_bias,
    positions_2, attn_norm_2, mlp_norm_2, a_w_in_2, a_w_out_2, b_w_in_2, b_q_norm_2,
    b_kv_norm_2, b_w_q_up_2, b_w_kv_up_2, b_w_out_2, mlp_w_up_2, mlp_w_down_2, final_norm_2,
):
    x = first_block(
        x, even_ln_g, even_w_in, even_w_out, a_q_norm_g, a_k_norm_g, a_lambda_q1, a_lambda_k1,
        a_lambda_q2, a_lambda_k2, a_subln_g, b_q_norm_g, b_k_norm_g, b_forget_bias, odd_ln_g,
        odd_w_in, odd_w_out, c_q_norm_g, c_k_norm_g, c_sinks, d_q_norm_g, d_k_norm_g,
        d_rel_bias,
    )
    return second_block(
        x, positions_2, attn_norm_2, mlp_norm_2, a_w_in_2, a_w_out_2, b_w_in_2, b_q_norm_2,
        b_kv_norm_2, b_w_q_up_2, b_w_kv_up_2, b_w_out_2, mlp_w_up_2, mlp_w_down_2, final_norm_2,
    )


_drawn_inputs = setup_inputs


def setup_inputs(seed=0):
    import zlib

    import numpy as np

    out = dict(_drawn_inputs(seed))
    spreads = {}
    factors = {'a_lambda_k2': 5.091,
     'c_q_norm_g': 2.712,
     'c_sinks': 5.803,
     'd_q_norm_g': 3.039,
     'd_k_norm_g': 3.623,
     'b_q_norm_2': 8.0,
     'b_kv_norm_2': 8.0,
     'final_norm_2': 2.856}
    for name, (base, spread) in spreads.items():
        noise = np.random.default_rng([zlib.crc32(name.encode()), seed]).standard_normal(out[name].shape)
        drawn = base * np.exp(spread * noise) if base else spread * noise
        out[name] = jnp.asarray(drawn.astype(out[name].dtype))
    for name, factor in factors.items():
        out[name] = (out[name] * factor).astype(out[name].dtype)
    return out
```

```python
import math
from contextlib import ExitStack

import numpy as np

import concourse.bass as bass
from concourse import mybir
from concourse.alu_op_type import AluOpType as ALU

F32 = mybir.dt.float32
F32R = mybir.dt.float32r
I32 = mybir.dt.int32
ACT = mybir.ActivationFunctionType
AX = mybir.AxisListType

P = 128
SEQ = 256
T = SEQ // P
DM = 1024
KC = DM // P
HD = 64
EPS = 1e-6
MASKED = -1e30
HIDDEN = -3e38
TAKEN = -3.3e38
N_EVEN, N_ODD, N_DSA, N_MLA = 4104, 3328, 2120, 672
Q_LORA, KV_LORA, ROPE = 384, 256, 32
Q_UP, KV_UP = 1536, 2048
FF_BLOCKS = 8
TOPK = 64
BLOCK = 512
LAM_INIT = 0.8 - 0.6 * math.exp(0.0)
G_EVEN, G_ODD, G_DSA, G_MLA, G_MLP0, G_MLP1, G_QL, G_KVL, G_SUB, G_HEAD = 0, 8, 16, 24, 32, 40, 48, 51, 53, 54
GAIN_ROWS = G_HEAD + 8
R_LAM, R_FB, R_SINK, R_FREQ = 0, 256, 264, 272
ROW_PARAMS = R_FREQ + 24


def weight_units():
    units, first = [], {}

    def columns(stage, matrix, kind, start, end, width, kc=KC, split=1, row=0):
        first.setdefault(stage, len(units))
        for c in range(start, end, width):
            w = min(width, end - c)
            units.append((matrix, kind, row, kc, c, w, [(i * (w // split), w // split) for i in range(split)]))

    columns("even_in_rest", "even_in", "z", 4096, N_EVEN, BLOCK)
    columns("even_in", "even_in", "z", 0, 4096, BLOCK)
    columns("even_out", "even_out", "x", 0, DM, BLOCK)
    columns("odd_in_rest", "odd_in", "z", 3072, N_ODD, BLOCK)
    columns("odd_in", "odd_in", "z", 0, 3072, BLOCK)
    columns("odd_out", "odd_out", "x", 0, DM, BLOCK)
    columns("dsa_in_rest", "dsa_in", "z", 2048, N_DSA, BLOCK)
    columns("dsa_in", "dsa_in", "z", 0, 2048, BLOCK)
    columns("dsa_out", "dsa_out", "x", 0, DM, BLOCK)

    def mlp(m):
        first[f"mlp{m}"] = len(units)
        for b in range(FF_BLOCKS + 1):
            if b < FF_BLOCKS:
                units.append((f"up{m}", "up", 0, KC, b * BLOCK, BLOCK, [(0, 256), (256, 256)]))
            if b:
                units.append((f"down{m}", "down", 4 * (b - 1), 4, 0, DM, [(0, DM)]))

    mlp(0)
    columns("mla_in_rest", "mla_in", "z", 512, N_MLA, BLOCK)
    columns("mla_in", "mla_in", "z", 0, 512, BLOCK)
    columns("q_up", "q_up", "z", 0, Q_UP, 768, Q_LORA // P, split=2)
    columns("kv_up", "kv_up", "z", 0, KV_UP, KV_UP, KV_LORA // P, split=4)
    columns("mla_out", "mla_out", "x", 0, DM, BLOCK)
    mlp(1)
    return units, first


def program(nc, w, x_in, gain_rows, row_params, positions, rel_band, final_gain, out, upto=99):
    units, first = weight_units()
    mm_after, act_after, dve_after, pair_of = [], [], [], []
    mm = act_n = dve_n = blocks = 0
    block_evacs = []
    for _, kind, _, _, _, _, parts in units:
        pair_of.append(blocks)
        if kind == "down":
            mm += 1
        else:
            mm += len(parts)
        if kind in ("z", "x"):
            for _ in parts:
                act_n += kind == "z"
                dve_n += 1
                blocks += 1
                block_evacs.append((act_n, dve_n))
        mm_after.append(mm)
        act_after.append(act_n)
        dve_after.append(dve_n)

    def w_view(u):
        matrix, _, row, kc, c, n, _ = units[u]
        return w[matrix][row * P:(row + kc) * P, c:c + n].rearrange("(k p) n -> p k n", p=P)

    ctx = ExitStack()
    with ctx:
        def sb(name, shape, dt=F32):
            return ctx.enter_context(nc.sbuf_tensor(name, shape, dt))

        def sem(name):
            return ctx.enter_context(nc.semaphore(name))

        x = sb("x", [P, T, DM])
        raw = [sb(f"raw{i}", [P, 4096]) for i in range(2)]
        w_hi = [sb(f"w_hi{i}", [P, 4096], F32R) for i in range(2)]
        w_lo = [sb(f"w_lo{i}", [P, 4096], F32R) for i in range(2)]
        h_hi = sb("h_hi", [P, KC, SEQ], F32R)
        h_lo = sb("h_lo", [P, KC, SEQ], F32R)
        mix = sb("mix", [P, T, DM])
        ident = sb("ident", [P, P])
        chunked = sb("chunked", [P, SEQ])
        gcols = sb("gcols", [P, GAIN_ROWS])
        g_mix = sb("g_mix", [P, KC])
        g_qk = sb("g_qk", [P, 4])
        rowp = sb("rowp", [P, ROW_PARAMS])
        lam4 = sb("lam4", [P, 4])
        wait_carrier = sb("wait_carrier", [P, 1])
        lam_diff = sb("lam_diff", [P, 1])
        lam_dot = sb("lam_dot", [P, 2])
        eps = sb("eps", [P, 1])
        pos_i = sb("pos_i", [P, T], I32)
        pos = sb("pos", [P, T])
        angle = sb("angle", [P, T, 24])
        turns = sb("turns", [P, T, 24])
        cosine = sb("cosine", [P, T, 24])
        sine = sb("sine", [P, T, 24])
        R_WIDTH = [2, 64, 8, 2, 52, 2, 2, 2, 4, 2, 2]
        ms = [sb(f"ms{i}", [P, n]) for i, n in enumerate(R_WIDTH)]
        rstd = [sb(f"rstd{i}", [P, n]) for i, n in enumerate(R_WIDTH)]
        r_tmp = sb("r_tmp", [P, 64])
        r_log = sb("r_log", [P, 64])
        rstd_sq = [sb(f"rstd_sq{i}", [P, T]) for i in range(2)]

        both = ExitStack()
        with both:
            def sa(name, shape, dt=F32):
                return both.enter_context(nc.sbuf_tensor(name, shape, dt))
            z = sa("z", [P, T * N_EVEN])
            tab = sa("tab", [P, 4096])
            qs = [sa(f"qs{i}", [P, 256]) for i in range(2)]
            ks = [sa(f"ks{i}", [P, 256]) for i in range(2)]
            qkT = [sa(f"qkT{i}", [P, 1024]) for i in range(2)]
            sc = [[sa(f"sc{i}{c}", [P, 384]) for c in range(2)] for i in range(2)]
            pT = [sa(f"pT{i}", [P, 2, 384]) for i in range(2)]
            row_max = [sa(f"row_max{i}", [P, 4]) for i in range(2)]
            neg_max = [sa(f"neg_max{i}", [P, 4]) for i in range(2)]
            row_sum = [sa(f"row_sum{i}", [P, 4]) for i in range(2)]
            inv_sum = [sa(f"inv_sum{i}", [P, 4]) for i in range(2)]
            sink_e = [sa(f"sink_e{i}", [P, 4]) for i in range(2)]
            logf = sa("logf", [P, 4, T, 8])
            cum = sa("cum", [P, T, 8])
            wi = sa("wi", [P, T, 8])
            best = sa("best", [P, T, 8])
        upper = pT[0][:, :, 0:SEQ]
        causal = sc[1][0][:, 0:SEQ]
        mlpb = ExitStack()
        with mlpb:
            def sm(name, shape, dt=F32):
                return mlpb.enter_context(nc.sbuf_tensor(name, shape, dt))
            relu = [sm(f"relu{i}", [P, BLOCK]) for i in range(2)]
            sq = [sm(f"sq{i}", [P, BLOCK]) for i in range(2)]
            u_hi = [sm(f"u_hi{i}", [P, 4, SEQ], F32R) for i in range(2)]
            u_lo = [sm(f"u_lo{i}", [P, 4, SEQ], F32R) for i in range(2)]
            g_final = sm("g_final", [P, DM])

        bank = [ctx.enter_context(nc.psum_tensor(f"bank{i}", [P, BLOCK], F32)) for i in range(8)]

        x_loaded, rows_loaded, params_loaded = sem("x_loaded"), sem("rows_loaded"), sem("params_loaded")
        pos_loaded, band_loaded, final_loaded = sem("pos_loaded"), sem("band_loaded"), sem("final_loaded")
        stored = sem("stored")
        raw_loaded = [sem(f"raw_loaded{i}") for i in range(2)]
        hi_split, lo_split = sem("hi_split"), sem("lo_split")
        mm_done, evac_act, evac_dve = sem("mm_done"), sem("evac_act"), sem("evac_dve")
        consts = sem("consts")
        tables, even_tables = sem("tables"), sem("even_tables")
        gains_turned, gains_ready = sem("gains_turned"), sem("gains_ready")
        trig_in, trig_ready = sem("trig_in"), sem("trig_ready")
        lam_in, lam_exp, lam_ready = sem("lam_in"), sem("lam_exp"), sem("lam_ready")
        turned, hi_turned, lo_turned = sem("turned"), sem("hi_turned"), sem("lo_turned")
        x_ready, mix_ready = sem("x_ready"), sem("mix_ready")
        ms_ready = [sem(f"ms_ready{i}") for i in range(11)]
        guess_ready = [sem(f"guess_ready{i}") for i in range(11)]
        rstd_ready = [sem(f"rstd_ready{i}") for i in range(11)]
        squares_ready, squares_read = sem("squares_ready"), sem("squares_read")
        act_order, dve_order, pool_order = sem("act_order"), sem("dve_order"), sem("pool_order")
        relu_done, sq_done, u_hi_done, u_lo_done = sem("relu_done"), sem("sq_done"), sem("u_hi_done"), sem("u_lo_done")
        staged, qk_turned, qk_ready = sem("staged"), sem("qk_turned"), sem("qk_ready")
        scores_done, max_done, probs_done = sem("scores_done"), sem("max_done"), sem("probs_done")
        diff_done, probs_turned, pt_act, pt_dve = sem("diff_done"), sem("probs_turned"), sem("pt_act"), sem("pt_dve")
        attended, heads_out = sem("attended"), sem("heads_out")
        raw_max_done, inv_done = sem("raw_max_done"), sem("inv_done")
        forget_in, forget_log, forget_ready = sem("forget_in"), sem("forget_log"), sem("forget_ready")
        cum_done, cum_ready, bias_ready = sem("cum_done"), sem("cum_ready"), sem("bias_ready")
        gate_exp = sem("gate_exp")
        roped, ki_staged, index_turned, index_ready = sem("roped"), sem("ki_staged"), sem("index_turned"), sem("index_ready")
        logits_done, logits_relu, logits_added = sem("logits_done"), sem("logits_relu"), sem("logits_added")
        mla_roped, kr_staged = sem("mla_roped"), sem("kr_staged")
        final_done = sem("final_done")

        TURNS = {"even": (8, gcols, G_EVEN), "even_mix": (8, g_mix, 0), "odd": (8, gcols, G_ODD), "odd_mix": (8, None, 0),
                 "dsa": (8, gcols, G_DSA), "dsa_mix": (8, None, 0), "mlp0": (8, gcols, G_MLP0), "mla": (8, gcols, G_MLA),
                 "latent": (5, gcols, G_QL), "mla_mix": (8, None, 0), "mlp1": (8, gcols, G_MLP1)}
        turn_base, n = {}, 0
        for name, (chunks, _, _) in TURNS.items():
            turn_base[name] = n
            n += (chunks + 1) // 2
        X_READY = {"odd": (evac_dve, dve_after[first["even_out"] + 1]), "dsa": (evac_dve, dve_after[first["odd_out"] + 1]),
                   "mlp0": (evac_dve, dve_after[first["dsa_out"] + 1]), "mla": (x_ready, 1),
                   "mlp1": (evac_dve, dve_after[first["mla_out"] + 1]), "final": (x_ready, 2)}
        PAIRS = {"A": 0, "B": 4, "C": 8, "D": 12, "S": 16, "L": 24}

        z_even = z[:, 0:T * N_EVEN].rearrange("p (t n) -> p t n", t=T)
        z_odd = z[:, 0:T * N_ODD].rearrange("p (t n) -> p t n", t=T)
        z_dsa = z[:, 0:T * N_DSA].rearrange("p (t n) -> p t n", t=T)
        z_mla = tab[:, 0:T * N_MLA].rearrange("p (t n) -> p t n", t=T)
        q_full = z[:, 0:T * Q_UP].rearrange("p (t n) -> p t n", t=T)
        kv_full = z[:, T * Q_UP:T * (Q_UP + KV_UP)].rearrange("p (t n) -> p t n", t=T)
        qs_mla = [tab[:, 1536 + 768 * i:1920 + 768 * i] for i in range(2)]
        ks_mla = [tab[:, 1920 + 768 * i:2304 + 768 * i] for i in range(2)]
        bias_a = tab[:, 0:1024].rearrange("p (h j) -> p h j", h=4)
        bias_b = tab[:, 1024:4096].rearrange("p (h j) -> p h j", h=8)
        bias_c = tab[:, 0:2048].rearrange("p (h j) -> p h j", h=8)
        bias_d = tab[:, 2048:4096].rearrange("p (h j) -> p h j", h=8)
        bias_s = tab[:, 0:384]
        qiT = tab[:, 512:1536].rearrange("p (i q) -> p i q", i=4)
        kiT = tab[:, 1536:1792]
        score = tab[:, 1792:2176]
        rl = tab[:, 2304:3072].rearrange("p (i q) -> p i q", i=2)

        def wait_from(e, s, value):
            if not isinstance(value, int) or value > 0:
                e.wait_ge(s, value)

        def load_unit(e, u, i=None, per=0):
            matrix, kind, row, kc, c, n, _ = units[u]
            slot = u % 2
            dst = raw[slot][:, 0:kc * n].rearrange("p (k n) -> p k n", k=kc)
            if i is None:
                if u >= 2:
                    e.wait_ge(lo_split, u - 1)
                e.dma_start(dst, w_view(u)).then_inc(raw_loaded[slot], 16)
                return
            e.wait_ge(lo_split, i * per + (u - 1))
            if kind == "down":
                rows = w[matrix][bass.ds(i * (per // 2 * 4 * P) + row * P, kc * P), :]
                e.dma_start(dst, rows.rearrange("(k p) n -> p k n", p=P)).then_inc(raw_loaded[slot], 16)
            else:
                step = per // 2 if kind == "up" else per
                cols = w[matrix][:, bass.ds(i * (step * n) + c, n)]
                e.dma_start(dst, cols.rearrange("(k p) n -> p k n", p=P)).then_inc(raw_loaded[slot], 16)

        def split_hi(e, u, i=None, per=0):
            if u >= len(units):
                return
            slot, size = u % 2, units[u][3] * units[u][5]
            if i is None:
                e.wait_ge(raw_loaded[slot], 16 * (u // 2 + 1))
                if u >= 2:
                    e.wait_ge(mm_done, mm_after[u - 2])
            else:
                e.wait_ge(raw_loaded[slot], i * (8 * per) + 16 * (u // 2 + 1))
                e.wait_ge(mm_done, i * (mm_after[u - 2 + per] - mm_after[u - 2]) + mm_after[u - 2])
            e.activation(w_hi[slot][:, 0:size], raw[slot][:, 0:size], ACT.Copy).then_inc(hi_split, 1)

        def split_lo(e, u, i=None, per=0):
            if u >= len(units):
                return
            slot, size = u % 2, units[u][3] * units[u][5]
            e.wait_ge(hi_split, u + 1 if i is None else i * per + (u + 1))
            e.tensor_tensor(w_lo[slot][:, 0:size], raw[slot][:, 0:size], w_hi[slot][:, 0:size].bitcast(F32),
                            ALU.subtract).then_inc(lo_split, 1)

        def turn_pe(e, name, src):
            chunks = TURNS[name][0]
            for c in range(chunks):
                for t in range(T):
                    last = e.transpose(bank[4 + c // 2][:, (c % 2) * SEQ + t * P:(c % 2) * SEQ + (t + 1) * P],
                                       src[:, t, c * P:(c + 1) * P], ident[:, :])
                if c % 2 or c == chunks - 1:
                    last.then_inc(turned, 1)

        def turn_act(e, name):
            chunks, gain, g0 = TURNS[name]
            for c in range(chunks):
                if c % 2 == 0:
                    e.wait_ge(turned, turn_base[name] + c // 2 + 1)
                scale = 1.0 if gain is None else gain[:, g0 + c:g0 + c + 1]
                ins = e.activation(h_hi[:, c, :], bank[4 + c // 2][:, (c % 2) * SEQ:(c % 2 + 1) * SEQ], ACT.Copy, scale=scale)
                if c % 2 or c == chunks - 1:
                    ins.then_inc(hi_turned, 1)

        def turn_dve(e, name):
            chunks, gain, g0 = TURNS[name]
            for c in range(chunks):
                if c % 2 == 0:
                    e.wait_ge(hi_turned, turn_base[name] + c // 2 + 1)
                scale = 1.0 if gain is None else gain[:, g0 + c:g0 + c + 1]
                ins = e.scalar_tensor_tensor(out=h_lo[:, c, :], in0=bank[4 + c // 2][:, (c % 2) * SEQ:(c % 2 + 1) * SEQ],
                                             scalar=scale, in1=h_hi[:, c, :].bitcast(F32), op0=ALU.mult, op1=ALU.subtract)
                if c % 2 or c == chunks - 1:
                    ins.then_inc(lo_turned, 1)

        def wait_turned(e, name):
            e.wait_ge(lo_turned, turn_base[name] + (TURNS[name][0] + 1) // 2)

        def unit_pe(e, u, i=None, per=0, chunk0=0):
            _, kind, _, kc, _, n, parts = units[u]
            slot = u % 2
            hi = w_hi[slot][:, 0:kc * n].rearrange("p (k n) -> p k n", k=kc)
            lo = w_lo[slot][:, 0:kc * n].rearrange("p (k n) -> p k n", k=kc)
            e.wait_ge(lo_split, u + 1 if i is None else i * per + (u + 1))
            for b, (c0, cn) in enumerate(parts):
                j = pair_of[u] + b
                if j >= 2:
                    a, d = block_evacs[j - 2]
                    if i is None:
                        wait_from(e, evac_act, a)
                        wait_from(e, evac_dve, d)
                    else:
                        a1, d1 = block_evacs[j - 2 + per]
                        assert a1 - a in (0, per) and d1 - d == per
                        e.wait_ge(evac_act, i * per + a)
                        e.wait_ge(evac_dve, i * per + d)
                for t in range(T):
                    dst = bank[2 * (j % 2) + t][:, 0:cn]
                    for k in range(kc):
                        h, l = h_hi[:, chunk0 + k, t * P:(t + 1) * P], h_lo[:, chunk0 + k, t * P:(t + 1) * P]
                        e.matmul(dst, h, hi[:, k, c0:c0 + cn], start=(k == 0), stop=False)
                        e.matmul(dst, h, lo[:, k, c0:c0 + cn], start=False, stop=False)
                        last = e.matmul(dst, l, hi[:, k, c0:c0 + cn], start=False, stop=(k == kc - 1))
                last.then_inc(mm_done, 1)

        def mm_value(u, b, i, per):
            v = mm_after[u] - len(units[u][6]) + b + 1
            return v if i is None else i * (mm_after[u + per] - mm_after[u]) + v

        def unit_z_act(e, u, dst, scale, i=None, per=0):
            for b, (c0, cn) in enumerate(units[u][6]):
                j = pair_of[u] + b
                e.wait_ge(mm_done, mm_value(u, b, i, per))
                c = units[u][4] + c0 if i is None else i * (per * units[u][5]) + (units[u][4] + c0)
                e.activation(dst[:, 0, bass.ds(c, cn)], bank[2 * (j % 2)][:, 0:cn], ACT.Copy, scale=scale).then_inc(evac_act, 1)

        def unit_z_dve(e, u, dst, scale, i=None, per=0):
            for b, (c0, cn) in enumerate(units[u][6]):
                j = pair_of[u] + b
                e.wait_ge(mm_done, mm_value(u, b, i, per))
                c = units[u][4] + c0 if i is None else i * (per * units[u][5]) + (units[u][4] + c0)
                e.tensor_scalar(dst[:, 1, bass.ds(c, cn)], bank[2 * (j % 2) + 1][:, 0:cn], scale, None, ALU.mult).then_inc(evac_dve, 1)

        def unit_x_dve(e, u):
            j, c = pair_of[u], units[u][4]
            e.wait_ge(mm_done, mm_after[u])
            e.tensor_tensor(x[:, 0, c:c + BLOCK], bank[2 * (j % 2)][:, :], x[:, 0, c:c + BLOCK], ALU.add)
            e.tensor_tensor(x[:, 1, c:c + BLOCK], bank[2 * (j % 2) + 1][:, :], x[:, 1, c:c + BLOCK], ALU.add).then_inc(evac_dve, 1)

        class Order:
            def __init__(self, e, s):
                self.e, self.s, self.n = e, s, 0

            def after(self, ins):
                ins.then_inc(self.s, 1)
                self.n += 1
                self.e.wait_ge(self.s, self.n)

        def x_squares_act(e, r):
            for t in range(T):
                ins = e.activation(mix[:, t, :], x[:, t, :], ACT.Square, scale=DM ** -0.5, accum_out=ms[r][:, t:t + 1])
            ins.then_inc(ms_ready[r], 1)

        def guess_act(e, order, r, count=1):
            n = R_WIDTH[r]
            e.wait_ge(ms_ready[r], count)
            order.after(e.activation(r_log[:, 0:n], ms[r][:, :], ACT.Ln, bias=eps[:, 0:1]))
            e.activation(rstd[r][:, :], r_log[:, 0:n], ACT.Exp, scale=-0.5).then_inc(guess_ready[r], 1)

        def newton_dve(e, order, r, square=None):
            n = R_WIDTH[r]
            y, tmp = rstd[r][:, :], r_tmp[:, 0:n]
            e.wait_ge(guess_ready[r], 1)
            order.after(e.tensor_scalar(ms[r][:, :], ms[r][:, :], EPS, None, ALU.add))
            order.after(e.tensor_tensor(tmp, y, y, ALU.mult))
            order.after(e.tensor_tensor(tmp, tmp, ms[r][:, :], ALU.mult))
            order.after(e.tensor_scalar(tmp, tmp, -0.5, 1.5, ALU.mult, ALU.add))
            if square is None:
                e.tensor_tensor(y, y, tmp, ALU.mult).then_inc(rstd_ready[r], 1)
            else:
                order.after(e.tensor_tensor(y, y, tmp, ALU.mult))
                e.tensor_tensor(square, y, y, ALU.mult).then_inc(rstd_ready[r], 1)

        def plus(g, n):
            return g + n

        def stage_wait_pool(e, g):
            wait_from(e, qk_turned, plus(g, -1))

        def turn_qk_pe(e, g, p):
            e.wait_ge(staged, plus(g, 1))
            wait_from(e, qk_ready, plus(g, -1))
            for j, src in enumerate((qs[p], ks[p])):
                for t in range(T):
                    last = e.transpose(bank[p][:, (2 * j + t) * P:(2 * j + t + 1) * P], src[:, t * P:(t + 1) * P], ident[:, :])
            last.then_inc(qk_turned, 1)

        def turn_qk_mla_pe(e, g, p):
            e.wait_ge(staged, plus(g, 1))
            e.wait_ge(qk_ready, plus(g, 0))
            for j, src in enumerate((qs_mla[p], ks_mla[p])):
                for m in range(4):
                    last = e.transpose(bank[j][0:96, m * P:(m + 1) * P], src[:, m * 96:(m + 1) * 96], ident[:, :])
            last.then_inc(qk_turned, 1)

        def qk_evac_act(e, g, p, scale):
            e.wait_ge(qk_turned, plus(g, 1))
            wait_from(e, scores_done, plus(g, -1))
            e.activation(qkT[p][:, 0:256], bank[p][:, 0:256], ACT.Copy, scale=scale)
            e.activation(qkT[p][:, 256:512], bank[p][:, 256:512], ACT.Copy).then_inc(qk_ready, 1)

        def qk_evac_mla_act(e, g, p):
            e.wait_ge(qk_turned, plus(g, 1))
            wait_from(e, scores_done, plus(g, -1))
            e.activation(qkT[p][0:96, 0:512], bank[0][0:96, :], ACT.Copy)
            e.activation(qkT[p][0:96, 512:1024], bank[1][0:96, :], ACT.Copy).then_inc(qk_ready, 1)

        def scores_pe(e, g, p, mla=False):
            e.wait_ge(qk_ready, plus(g, 1))
            for c in range(2):
                dst = bank[2 + 2 * p + c]
                if mla:
                    q, k = qkT[p][0:96, c * 256:(c + 1) * 256], qkT[p][0:96, 512 + c * 256:512 + (c + 1) * 256]
                else:
                    q, k = qkT[p][c * HD:(c + 1) * HD, 0:256], qkT[p][c * HD:(c + 1) * HD, 256:512]
                e.matmul(dst[:, 0:256], q[:, P:2 * P], k, start=True, stop=True)
                last = e.matmul(dst[:, 256:384], q[:, 0:P], k[:, 0:P], start=True, stop=True)
            last.then_inc(scores_done, 1)

        def row_max_dve(e, g, p, biases, scale=1.0, sink=None):
            e.wait_ge(scores_done, plus(g, 1))
            wait_from(e, probs_turned, plus(g, -1))
            if not isinstance(g, int):
                e.memset(wait_carrier[:, :], 0.0)
            for c in range(2):
                b1, b0 = biases[c]
                s = bank[2 + 2 * p + c]
                for t, cols, b in ((1, slice(0, 256), b1), (0, slice(256, 384), b0)):
                    last = e.tensor_tensor_reduce(sc[p][c][:, cols], s[:, cols], b, 1.0, MASKED, ALU.add, ALU.max,
                                                  row_max[p][:, 2 * c + t:2 * c + t + 1])
            last.then_inc(raw_max_done, 1)
            e.wait_ge(raw_max_done, plus(g, 1))
            if sink is not None:
                e.scalar_tensor_tensor(out=neg_max[p][:, :].rearrange("p (c t) -> p c t", c=2), in0=row_max[p][:, :].rearrange("p (c t) -> p c t", c=2), scalar=1.0, in1=sink, op0=ALU.mult, op1=ALU.max)\
                    .then_inc(sink_max, 1)
                e.wait_ge(sink_max, 2 * (g - PAIRS["C"]) + 1)
                e.tensor_scalar(neg_max[p][:, :], neg_max[p][:, :], -scale, None, ALU.mult).then_inc(sink_max, 1)
                e.wait_ge(sink_max, 2 * (g - PAIRS["C"]) + 2)
                e.tensor_tensor(sink_e[p][:, :].rearrange("p (c t) -> p c t", c=2), neg_max[p][:, :].rearrange("p (c t) -> p c t", c=2),
                                sink, ALU.add).then_inc(max_done, 1)
            else:
                e.tensor_scalar(neg_max[p][:, :], row_max[p][:, :], -scale, None, ALU.mult).then_inc(max_done, 1)

        def probs_act(e, g, p, scale=1.0, sink=False):
            e.wait_ge(max_done, plus(g, 1))
            wait_from(e, heads_out, plus(g, -1))
            for c in range(2):
                for t, cols in ((1, slice(0, 256)), (0, slice(256, 384))):
                    j = 2 * c + t
                    last = e.activation(sc[p][c][:, cols], sc[p][c][:, cols], ACT.Exp, bias=neg_max[p][:, j:j + 1],
                                        scale=scale, accum_out=row_sum[p][:, j:j + 1])
            if sink:
                last = e.activation(sink_e[p][:, :], sink_e[p][:, :], ACT.Exp)
            last.then_inc(probs_done, 1)

        def turn_probs_pe(e, g, p, ready, value, comps=2):
            e.wait_ge(ready, value)
            for c in range(comps):
                for m in range(3):
                    last = e.transpose(bank[2 + 2 * p + c][:, m * P:(m + 1) * P], sc[p][c][:, m * P:(m + 1) * P], ident[:, :])
            last.then_inc(probs_turned, 1)

        def pt_evac_dve(e, g, p):
            e.wait_ge(probs_turned, plus(g, 1))
            wait_from(e, attended, plus(g, -1))
            e.tensor_copy(pT[p][:, 0, :], bank[2 + 2 * p][:, 0:384]).then_inc(pt_dve, 1)

        def pt_evac_act(e, g, p):
            e.wait_ge(probs_turned, plus(g, 1))
            wait_from(e, attended, plus(g, -1))
            e.activation(pT[p][:, 1, :], bank[3 + 2 * p][:, 0:384], ACT.Copy).then_inc(pt_act, 1)

        def attend_pe(e, g, p, value, width=HD, comps=2):
            e.wait_ge(pt_dve, plus(g, 1))
            if comps == 2:
                e.wait_ge(pt_act, plus(g, 1) - PAIRS["B"])
            wait_from(e, heads_out, plus(g, -1))
            for c in range(comps):
                for t in range(T):
                    dst = bank[6 + p][:, (2 * c + t) * width:(2 * c + t + 1) * width]
                    if t == 0:
                        last = e.matmul(dst, pT[p][:, c, 256:384], value(c, 0), start=True, stop=True)
                    else:
                        e.matmul(dst, pT[p][:, c, 0:P], value(c, 0), start=True, stop=False)
                        last = e.matmul(dst, pT[p][:, c, P:2 * P], value(c, 1), start=False, stop=True)
            last.then_inc(attended, 1)

        def heads_out_dve(e, g, p, dst, sink=False):
            e.wait_ge(probs_done, plus(g, 1))
            if sink:
                e.tensor_tensor(row_sum[p][:, :], row_sum[p][:, :], sink_e[p][:, :], ALU.add).then_inc(sink_sum, 1)
                e.wait_ge(sink_sum, g - PAIRS["C"] + 1)
            e.reciprocal(inv_sum[p][:, :], row_sum[p][:, :]).then_inc(inv_done, 1)
            e.wait_ge(inv_done, plus(g, 1) - PAIRS["B"])
            e.wait_ge(attended, plus(g, 1))
            e.tensor_tensor(dst, bank[6 + p][:, 0:256].rearrange("p (c t d) -> p c t d", c=2, t=T),
                            inv_sum[p][:, :].rearrange("p (c t) -> p c t", c=2).unsqueeze(3).to_broadcast([P, 2, T, HD]),
                            ALU.mult).then_inc(heads_out, 1)

        sink_max, sink_sum = sem("sink_max"), sem("sink_sum")

        def staging(buf):
            return buf[:, 0:256].rearrange("p (t c d) -> p t c d", t=T, c=2)

        def heads2(v, c0, step):
            if step == HD:
                return v[:, :, bass.ds(c0, 2 * HD)].rearrange("p t (c d) -> p t c d", c=2)
            return v[:, :, bass.ds(c0, 2 * step)].rearrange("p t (c s) -> p t c s", c=2)[:, :, :, 0:HD]

        def bcast64(a):
            return a.unsqueeze(3).to_broadcast([P, T, 2, HD])

        def static_pair(kind, i):
            if kind in ("A", "B"):
                o, r = (0, 0) if kind == "A" else (2048, 32)
                st = rstd[1][:, r:r + 32].rearrange("p (t g) -> p t g", t=T)
                return (heads2(z_even, o + 128 * i, HD), st[:, :, 2 * i:2 * i + 2],
                        heads2(z_even, o + 512 + 128 * i, HD), st[:, :, 8 + 2 * i:10 + 2 * i])
            if kind == "C":
                st = rstd[4][:, 0:20].rearrange("p (t g) -> p t g", t=T)
                return (heads2(z_odd, 64 * i, 256), st[:, :, i:i + 5:4], heads2(z_odd, 512, HD), st[:, :, 8:10])
            st = rstd[4][:, 20:52].rearrange("p (t g) -> p t g", t=T)
            return (heads2(z_odd, 1280 + 128 * i, HD), st[:, :, 2 * i:2 * i + 2],
                    heads2(z_odd, 1792 + 128 * i, HD), st[:, :, 8 + 2 * i:10 + 2 * i])

        def static_biases(kind, i):
            if kind == "A":
                return [(bias_a[:, i, :], bias_a[:, i, P:])] * 2
            if kind == "B":
                return [(bias_b[:, 2 * i + c, 0:256], bias_b[:, 2 * i + c, 256:384]) for c in range(2)]
            if kind == "C":
                return [(bias_c[:, i + 4 * c, :], bias_c[:, i + 4 * c, P:]) for c in range(2)]
            return [(bias_d[:, 2 * i + c, :], bias_d[:, 2 * i + c, P:]) for c in range(2)]

        def static_value(kind, i):
            if kind == "A":
                return lambda c, t: z_even[:, t, 1024 + 128 * i:1152 + 128 * i]
            if kind == "B":
                return lambda c, t: z_even[:, t, 3072 + 128 * i + 64 * c:3136 + 128 * i + 64 * c]
            if kind == "C":
                return lambda c, t: z_odd[:, t, 640 + 64 * c:704 + 64 * c]
            return lambda c, t: z_odd[:, t, 2304 + 128 * i + 64 * c:2368 + 128 * i + 64 * c]

        def static_out(kind, i):
            if kind == "B":
                v = mix[:, :, 512 + 128 * i:640 + 128 * i].rearrange("p t (c d) -> p c t d", c=2)
            elif kind == "C":
                v = mix[:, :, 0:512].rearrange("p t (c s) -> p c t s", c=2)[:, :, :, 64 * i:64 * i + 64]
            else:
                v = mix[:, :, 512 + 128 * i:640 + 128 * i].rearrange("p t (c d) -> p c t d", c=2)
            return v

        def static_pairs(kinds):
            return [(k, i, PAIRS[k] + i) for k in kinds for i in range(4)]

        def sparse_value(i):
            return lambda c, t: z_dsa[:, t, bass.ds((i >> 2) * HD + (1280 + 128 * c), HD)]

        def latent_value(i):
            return lambda c, t: kv_full[:, t, bass.ds(i * 256 + (128 * c + 64), HD)]

        block = ctx.enter_context(nc.Block())

        @block.sync
        def _(sp):
            sp.dma_start(x[:, :, :], x_in.rearrange("(t p) n -> p t n", p=P)).then_inc(x_loaded, 16)
            sp.dma_start(mix[0:GAIN_ROWS, 0, 0:P], gain_rows).then_inc(rows_loaded, 16)
            sp.dma_start(rowp[:, :], row_params.partition_broadcast(P)).then_inc(params_loaded, 16)
            load_unit(sp, 0)
            load_unit(sp, 1)
            sp.dma_start(pos_i[:, :], positions).then_inc(pos_loaded, 16)

            def stream(u0, count, trips=0, per=2):
                if trips:
                    with sp.Fori(0, trips) as i:
                        for j in range(per):
                            load_unit(sp, u0 + j, i, per)
                else:
                    for j in range(count):
                        load_unit(sp, u0 + j)

            stream(2, 1)
            stream(3, 6, trips=3)
            stream(first["even_out"], 3)
            if upto >= 2:
                stream(first["odd_in"], 6, trips=3)
                sp.wait_ge(max_done, PAIRS["B"] + 4)
                sp.dma_start(tab[:, 2048:4096], rel_band.rearrange("p h j -> p (h j)")).then_inc(band_loaded, 16)
                stream(first["odd_out"], 3)
            if upto >= 3:
                stream(first["dsa_in"], 4, trips=2)
                stream(first["dsa_out"], 3)
            for m, done in ((0, 4), (1, 6)):
                if upto < done:
                    break
                u = first[f"mlp{m}"]
                stream(u + 1, 12, trips=3, per=4)
                stream(u + 13, 3)
                if m == 0:
                    stream(u + 16, 1)
                    if upto >= 5:
                        stream(first["mla_in"], first["mlp1"] + 1 - first["mla_in"])
            if upto >= 6:
                sp.wait_ge(heads_out, PAIRS["L"] + 8)
                sp.dma_start(g_final[:, :], final_gain.partition_broadcast(P)).then_inc(final_loaded, 16)
                for t in range(T):
                    sp.wait_ge(final_done, t + 1)
                    sp.dma_start(out[t * P:(t + 1) * P, :], mix[:, t, :]).then_inc(stored, 16)
            else:
                sp.wait_ge(*X_READY[{1: "odd", 2: "dsa", 3: "mlp0", 4: "mla", 5: "mlp1"}[upto]])
                for t in range(T):
                    sp.dma_start(out[t * P:(t + 1) * P, :], x[:, t, :]).then_inc(stored, 16)
            sp.wait_ge(stored, 32)

        @block.gpsimd
        def _(pool):
            order = Order(pool, pool_order)
            order.after(pool.memset(ident[:, :], 0.0))
            pool.affine_select(out=ident[:, :], in_=ident[:, :], compare_op=ALU.not_equal, fill=1.0, base=0,
                               pattern=[[-1, P]], channel_multiplier=1).then_inc(consts, 1)
            pool.memset(eps[:, :], EPS).then_inc(consts, 1)
            order.after(pool.memset(upper, 1.0))
            for t in range(T):
                order.after(pool.affine_select(out=upper[:, t, :], in_=upper[:, t, :], compare_op=ALU.is_ge, fill=0.0,
                                               base=-P * t, pattern=[[1, SEQ]], channel_multiplier=-1))
            order.after(pool.memset(causal, 0.0))
            order.after(pool.affine_select(out=causal, in_=causal, compare_op=ALU.is_ge, fill=MASKED, base=P,
                                           pattern=[[-1, SEQ]], channel_multiplier=1))
            order.after(pool.memset(chunked[:, :], 0.0))
            order.after(pool.memset(chunked[0:64, 192:256], MASKED))
            nd = sc[0][0][:, 0:256]
            order.after(pool.iota(nd, pattern=[[-1, SEQ]], base=P, channel_multiplier=1, allow_small_or_imprecise_dtypes=True))
            nd2 = sc[0][1][:, 0:256]
            order.after(pool.tensor_scalar(nd2, nd, 0.0, None, ALU.max))
            order.after(pool.tensor_scalar(nd, nd, 0.0, None, ALU.min))
            order.after(pool.tensor_tensor(nd, nd, nd2, ALU.subtract))
            order.after(pool.memset(nd[0:64, 192:256], MASKED))
            for h in range(4):
                pool.tensor_scalar(bias_a[:, h, :], nd, 2.0 ** (-8.0 * (h + 1) / 4), None, ALU.mult).then_inc(even_tables, 1)
            pool.memset(g_mix[:, 4:KC], 1.0).then_inc(consts, 1)

            def stage_static(kinds):
                for kind, i, g in static_pairs(kinds):
                    q, rq, k, rk = static_pair(kind, i)
                    if i == 0:
                        pool.wait_ge(rstd_ready[1 if kind in "AB" else 4], 1)
                    stage_wait_pool(pool, g)
                    pool.tensor_tensor(staging(qs[g % 2]), q, bcast64(rq), ALU.mult)
                    pool.tensor_tensor(staging(ks[g % 2]), k, bcast64(rk), ALU.mult).then_inc(staged, 1)

            stage_static("AB")
            if upto < 2:
                return
            pool.wait_ge(max_done, PAIRS["B"] + 4)
            pool.wait_ge(heads_out, PAIRS["B"] + 4)
            order.after(pool.iota(nd, pattern=[[-1, SEQ]], base=P, channel_multiplier=1, allow_small_or_imprecise_dtypes=True))
            order.after(pool.tensor_scalar(nd2, nd, 0.0, None, ALU.max))
            order.after(pool.tensor_scalar(nd, nd, 0.0, None, ALU.min))
            order.after(pool.tensor_tensor(nd, nd, nd2, ALU.subtract))
            order.after(pool.memset(nd[0:64, 192:256], MASKED))
            order.after(pool.memset(nd[64:128, 0:64], MASKED))
            for h in range(8):
                pool.tensor_scalar(bias_c[:, h, :], nd, 2.0 ** -(h + 1), None, ALU.mult).then_inc(tables, 1)
            pool.wait_ge(band_loaded, 16)
            pool.tensor_tensor(bias_d[:, :, :], bias_d[:, :, :], chunked[:, :].unsqueeze(1).to_broadcast([P, 8, SEQ]),
                               ALU.add).then_inc(tables, 1)
            stage_static("CD")
            if upto < 3:
                return
            pool.wait_ge(roped, 1)
            pool.wait_ge(qk_turned, PAIRS["S"])
            pool.tensor_copy(staging(ks[0]), z_dsa[:, :, 2048:2112].unsqueeze(2).to_broadcast([P, T, 2, HD])).then_inc(ki_staged, 1)
            pool.wait_ge(index_turned, 1)
            pool.wait_ge(roped, 2)

            def stage_sparse(g, p, i):
                stage_wait_pool(pool, g)
                pool.tensor_copy(staging(qs[p]), heads2(z_dsa, i * HD, 512))
                pool.tensor_copy(staging(ks[p]), heads2(z_dsa, (i >> 2) * HD + 1024, P)).then_inc(staged, 1)

            with pool.Fori(0, 4) as i:
                for j in range(2):
                    stage_sparse(i * 2 + (PAIRS["S"] + j), j, i * 2 + j)
            if upto < 5:
                return
            pool.wait_ge(mla_roped, 1)
            for p in range(2):
                kbuf = ks_mla[p].rearrange("p (c t d) -> p c t d", c=2, t=T)
                for c in range(2):
                    ins = pool.tensor_copy(kbuf[:, c, :, HD:96], z_mla[:, :, 640:672])
            ins.then_inc(kr_staged, 1)

            def stage_latent(g, p, i):
                stage_wait_pool(pool, g)
                for buf, full, step, n in ((qs_mla[p], q_full, 96, 96), (ks_mla[p], kv_full, 128, 64)):
                    dst = buf.rearrange("p (c t d) -> p c t d", c=2, t=T)[:, :, :, 0:n]
                    src = full[:, :, bass.ds(i * (2 * step), 2 * step)].rearrange("p t (c s) -> p c t s", c=2)[:, :, :, 0:n]
                    last = pool.tensor_copy(dst, src)
                last.then_inc(staged, 1)

            with pool.Fori(0, 4) as i:
                for j in range(2):
                    stage_latent(i * 2 + (PAIRS["L"] + j), j, i * 2 + j)

        @block.tensor
        def _(pe):
            pe.wait_ge(consts, 1)
            pe.wait_ge(rows_loaded, 16)
            pe.transpose(bank[0][:, 0:GAIN_ROWS], mix[0:GAIN_ROWS, 0, 0:P], ident[0:GAIN_ROWS, 0:GAIN_ROWS]).then_inc(gains_turned, 1)
            pe.wait_ge(x_loaded, 16)
            turn_pe(pe, "even", x)

            def project(u0, count, trips=0, chunk0=0):
                if trips:
                    with pe.Fori(0, trips) as i:
                        for j in range(2):
                            unit_pe(pe, u0 + j, i, 2, chunk0)
                else:
                    for j in range(count):
                        unit_pe(pe, u0 + j, chunk0=chunk0)

            def static_attention(kinds):
                pairs = static_pairs(kinds)

                def back(kind, i, g):
                    p = g % 2
                    if kind == "A":
                        turn_probs_pe(pe, g, p, diff_done, g + 1, comps=1)
                        attend_pe(pe, g, p, static_value(kind, i), width=P, comps=1)
                    else:
                        turn_probs_pe(pe, g, p, probs_done, g + 1)
                        attend_pe(pe, g, p, static_value(kind, i))

                turn_qk_pe(pe, pairs[0][2], 0)
                turn_qk_pe(pe, pairs[1][2], 1)
                scores_pe(pe, pairs[0][2], 0)
                for n, (kind, i, g) in enumerate(pairs):
                    if n + 1 < len(pairs):
                        scores_pe(pe, g + 1, (g + 1) % 2)
                    if n + 2 < len(pairs):
                        turn_qk_pe(pe, g + 2, g % 2)
                    back(kind, i, g)

            wait_turned(pe, "even")
            project(0, 2)
            u = first["even_in"]
            unit_pe(pe, 2)
            with pe.Fori(0, 3) as i:
                for j in range(2):
                    unit_pe(pe, 3 + j, i, 2)
            pe.wait_ge(forget_ready, 1)
            pe.wait_ge(even_tables, 4)
            for t in range(T):
                for s in range(t + 1):
                    last = pe.matmul(bank[0][:, 8 * t:8 * t + 8], upper[:, s, t * P:(t + 1) * P], logf[:, 3, s, :],
                                     start=(s == 0), stop=(s == t))
            last.then_inc(cum_done, 1)
            for h in range(8):
                for s in range(T):
                    last = pe.matmul(bank[4 + h // 2][:, (h % 2) * SEQ:(h % 2 + 1) * SEQ], qkT[s][:, h * P:(h + 1) * P],
                                     upper[:, s, :], start=(s == 0), stop=(s == 1))
            last.then_inc(cum_done, 1)
            pe.wait_ge(bias_ready, 1)
            static_attention("AB")
            pe.wait_ge(mix_ready, 1)
            turn_pe(pe, "even_mix", mix)
            wait_turned(pe, "even_mix")
            project(first["even_out"], 2)
            if upto < 2:
                return
            pe.wait_ge(*X_READY["odd"])
            turn_pe(pe, "odd", x)
            wait_turned(pe, "odd")
            project(first["odd_in_rest"], 1)
            project(first["odd_in"], 6, trips=3)
            static_attention("CD")
            pe.wait_ge(mix_ready, 2)
            turn_pe(pe, "odd_mix", mix)
            wait_turned(pe, "odd_mix")
            project(first["odd_out"], 2)
            if upto < 3:
                return
            pe.wait_ge(*X_READY["dsa"])
            turn_pe(pe, "dsa", x)
            wait_turned(pe, "dsa")
            project(first["dsa_in_rest"], 1)
            project(first["dsa_in"], 4, trips=2)
            pe.wait_ge(roped, 1)
            for i in range(4):
                for t in range(T):
                    pe.transpose(bank[4 + i // 2][:, (i % 2) * SEQ + t * P:(i % 2) * SEQ + (t + 1) * P],
                                 z_dsa[:, t, 1536 + P * i:1536 + P * (i + 1)], ident[:, :])
            pe.wait_ge(ki_staged, 1)
            for t in range(T):
                last = pe.transpose(bank[6][:, t * P:(t + 1) * P], ks[0][:, t * P:(t + 1) * P], ident[:, :])
            last.then_inc(index_turned, 1)
            pe.wait_ge(index_ready, 1)
            for h in range(8):
                if h >= 4:
                    pe.wait_ge(logits_relu, h - 3)
                q = qiT[(h % 2) * HD:(h % 2 + 1) * HD, h // 2, :]
                k = kiT[(h % 2) * HD:(h % 2 + 1) * HD, :]
                pe.matmul(bank[h % 4][:, 0:256], q[:, P:2 * P], k, start=True, stop=True)
                pe.matmul(bank[h % 4][:, 256:384], q[:, 0:P], k[:, 0:P], start=True, stop=True).then_inc(logits_done, 1)
            pe.wait_ge(logits_relu, 8)

            def looped_attention(first_pair, value, mla):
                turn = turn_qk_mla_pe if mla else turn_qk_pe
                turn(pe, first_pair, 0)
                turn(pe, first_pair + 1, 1)
                scores_pe(pe, first_pair, 0, mla)

                def step(g, i, p, scores=True, turns=True):
                    if scores:
                        scores_pe(pe, plus(g, 1), 1 - p, mla)
                    if turns:
                        turn(pe, plus(g, 2), p)
                    turn_probs_pe(pe, g, p, probs_done, plus(g, 1))
                    attend_pe(pe, g, p, value(i))

                with pe.Fori(0, 3) as i:
                    for j in range(2):
                        step(i * 2 + (first_pair + j), i * 2 + j, j)
                step(first_pair + 6, 6, 0, turns=False)
                step(first_pair + 7, 7, 1, scores=False, turns=False)

            looped_attention(PAIRS["S"], sparse_value, False)
            pe.wait_ge(heads_out, PAIRS["S"] + 8)
            turn_pe(pe, "dsa_mix", mix)
            wait_turned(pe, "dsa_mix")
            project(first["dsa_out"], 2)
            if upto < 4:
                return

            def mlp(m):
                name, u = f"mlp{m}", first[f"mlp{m}"]
                pe.wait_ge(*X_READY[name])
                turn_pe(pe, name, x)
                wait_turned(pe, name)

                def up(v, b, i=None):
                    slot = v % 2
                    hi = w_hi[slot][:, :].rearrange("p (k n) -> p k n", k=KC)
                    lo = w_lo[slot][:, :].rearrange("p (k n) -> p k n", k=KC)
                    pe.wait_ge(lo_split, v + 1 if i is None else i * 4 + (v + 1))
                    relus = 2 * FF_BLOCKS * m + 2 * (b - 1)
                    if i is not None or b >= 2:
                        pe.wait_ge(relu_done, relus if i is None else i * 4 + relus)
                    for f in range(4):
                        dst = bank[2 * (b % 2) + f // 2][:, (f % 2) * SEQ:(f % 2 + 1) * SEQ]
                        for k in range(KC):
                            wh, wl = hi[:, k, f * P:(f + 1) * P], lo[:, k, f * P:(f + 1) * P]
                            pe.matmul(dst, wh, h_hi[:, k, :], start=(k == 0), stop=False)
                            pe.matmul(dst, wh, h_lo[:, k, :], start=False, stop=False)
                            last = pe.matmul(dst, wl, h_hi[:, k, :], start=False, stop=(k == KC - 1))
                        if f % 2:
                            last.then_inc(mm_done, 1)

                def down(v, b, i=None, begins=False, ends=False):
                    slot = v % 2
                    hi = w_hi[slot][:, :].rearrange("p (k n) -> p k n", k=4)
                    lo = w_lo[slot][:, :].rearrange("p (k n) -> p k n", k=4)
                    pe.wait_ge(lo_split, v + 1 if i is None else i * 4 + (v + 1))
                    blocks_done = 2 * FF_BLOCKS * m + 2 * (b + 1)
                    pe.wait_ge(u_lo_done, blocks_done if i is None else i * 4 + blocks_done)
                    for c in range(4):
                        for t in range(T):
                            uh, ul = u_hi[b % 2][:, c, t * P:(t + 1) * P], u_lo[b % 2][:, c, t * P:(t + 1) * P]
                            for half in range(2):
                                dst = bank[4 + 2 * t + half][:, :]
                                cols = slice(half * BLOCK, (half + 1) * BLOCK)
                                a, z_ = begins and c == 0, ends and c == 3
                                pe.matmul(dst, uh, hi[:, c, cols], start=a, stop=False, skip_group_check=True)
                                pe.matmul(dst, uh, lo[:, c, cols], start=False, stop=False, skip_group_check=True)
                                last = pe.matmul(dst, ul, hi[:, c, cols], start=False, stop=z_, skip_group_check=True)
                    last.then_inc(mm_done, 1)

                up(u, 0)
                up(u + 1, 1)
                down(u + 2, 0, begins=True)
                up(u + 3, 2)
                down(u + 4, 1)
                with pe.Fori(0, 2) as i:
                    up(u + 5, 3, i)
                    down(u + 6, 2, i)
                    up(u + 7, 4, i)
                    down(u + 8, 3, i)
                up(u + 13, 7)
                down(u + 14, 6)
                down(u + 15, 7, ends=True)

            mlp(0)
            if upto < 5:
                return
            pe.wait_ge(*X_READY["mla"])
            turn_pe(pe, "mla", x)
            wait_turned(pe, "mla")
            project(first["mla_in_rest"], 2)
            u = first["q_up"]
            pe.wait_ge(evac_act, act_after[u - 1])
            pe.wait_ge(evac_dve, dve_after[u - 1])
            turn_pe(pe, "latent", z_mla)
            wait_turned(pe, "latent")
            project(u, 2)
            project(first["kv_up"], 1, chunk0=Q_LORA // P)
            pe.wait_ge(kr_staged, 1)
            looped_attention(PAIRS["L"], latent_value, True)
            pe.wait_ge(heads_out, PAIRS["L"] + 8)
            turn_pe(pe, "mla_mix", mix)
            wait_turned(pe, "mla_mix")
            project(first["mla_out"], 2)
            if upto < 6:
                return
            mlp(1)

        @block.scalar
        def _(act):
            order = Order(act, act_order)
            act.wait_ge(pos_loaded, 16)
            act.wait_ge(trig_in, 1)
            act.activation(sine[:, :, :], angle[:, :, :], ACT.Sin)
            act.activation(cosine[:, :, :], turns[:, :, :], ACT.Sin).then_inc(trig_ready, 1)
            act.wait_ge(lam_in, 1)
            act.activation(lam_dot[:, :], lam_dot[:, :], ACT.Exp).then_inc(lam_exp, 1)
            split_hi(act, 0)
            act.wait_ge(gains_ready, 1)
            turn_act(act, "even")
            act.wait_ge(x_loaded, 16)
            act.wait_ge(gains_turned, 1)
            x_squares_act(act, 0)
            act.wait_ge(consts, 2)
            guess_act(act, order, 0)

            def project(u0, count, dst, scale, trips=0):
                if trips:
                    with act.Fori(0, trips) as i:
                        for j in range(2):
                            split_hi(act, u0 + j + 1, i, 2)
                            unit_z_act(act, u0 + j, dst, scale, i, 2)
                else:
                    for j in range(count):
                        split_hi(act, u0 + j + 1)
                        unit_z_act(act, u0 + j, dst, scale)

            def project_x(u0):
                for j in range(2):
                    split_hi(act, u0 + j + 1)

            def static_attention(kinds, scales):
                pairs = static_pairs(kinds)

                def out(kind, i, g):
                    if kind != "A":
                        pt_evac_act(act, g, g % 2)

                qk_evac_act(act, pairs[0][2], 0, scales(pairs[0][0]))
                qk_evac_act(act, pairs[1][2], 1, scales(pairs[1][0]))
                probs_act(act, pairs[0][2], 0, sink=pairs[0][0] == "C")
                for n, (kind, i, g) in enumerate(pairs):
                    if n + 2 < len(pairs):
                        qk_evac_act(act, g + 2, g % 2, scales(pairs[n + 2][0]))
                    out(kind, i, g)
                    if n + 1 < len(pairs):
                        probs_act(act, g + 1, (g + 1) % 2, sink=pairs[n + 1][0] == "C")

            act.wait_ge(rstd_ready[0], 1)
            project(0, 2, z_even, rstd[0][:, 0:1])
            split_hi(act, 3)
            unit_z_act(act, 2, z_even, rstd[0][:, 0:1])
            with act.Fori(0, 3) as i:
                for j in range(2):
                    split_hi(act, 4 + j, i, 2)
                    unit_z_act(act, 3 + j, z_even, rstd[0][:, 0:1], i, 2)
            act.wait_ge(evac_act, act_after[8])
            act.wait_ge(evac_dve, dve_after[8])
            act.activation(mix[:, :, :], z_even[:, :, 0:1024], ACT.Square, scale=HD ** -0.5).then_inc(squares_ready, 1)
            act.wait_ge(forget_in, 1)
            order.after(act.activation(logf[:, 2, :, :], logf[:, 1, :, :], ACT.Exp))
            act.activation(logf[:, 2, :, :], logf[:, 2, :, :], ACT.Ln, bias=1.0).then_inc(forget_log, 1)
            act.wait_ge(squares_read, 1)
            act.activation(mix[:, :, :], z_even[:, :, 2048:3072], ACT.Square, scale=HD ** -0.5).then_inc(squares_ready, 1)
            guess_act(act, order, 1)
            act.wait_ge(gains_ready, 2)
            act.wait_ge(consts, 3)
            static_attention("AB", lambda kind: g_qk[:, "ABCD".index(kind):"ABCD".index(kind) + 1])

            act.wait_ge(heads_out, PAIRS["B"] + 4)
            act.activation(z_even[:, :, 0:512], mix[:, :, 0:512], ACT.Square, scale=P ** -0.5).then_inc(squares_ready, 1)
            act.activation(z_even[:, :, 512:1024], z_even[:, :, 1536:2048], ACT.Exp, scale=-1.0)
            act.activation(z_even[:, :, 2560:3072], z_even[:, :, 3584:4096], ACT.Exp, scale=-1.0).then_inc(gate_exp, 1)
            guess_act(act, order, 2)
            turn_act(act, "even_mix")
            project_x(first["even_out"])
            if upto < 2:
                return
            turn_act(act, "odd")
            act.wait_ge(*X_READY["odd"])
            x_squares_act(act, 3)
            guess_act(act, order, 3)
            act.wait_ge(rstd_ready[3], 1)
            project(first["odd_in_rest"], 1, z_odd, rstd[3][:, 0:1])
            project(first["odd_in"], 6, z_odd, rstd[3][:, 0:1], trips=3)
            act.wait_ge(evac_act, act_after[first["odd_out"] - 1])
            act.wait_ge(evac_dve, dve_after[first["odd_out"] - 1])
            act.activation(mix[:, :, 0:640], z_odd[:, :, 0:640], ACT.Square, scale=HD ** -0.5).then_inc(squares_ready, 1)
            act.wait_ge(squares_read, 2)
            act.activation(mix[:, :, :], z_odd[:, :, 1280:2304], ACT.Square, scale=HD ** -0.5).then_inc(squares_ready, 1)
            guess_act(act, order, 4)
            static_attention("CD", lambda kind: g_qk[:, "ABCD".index(kind):"ABCD".index(kind) + 1])
            act.wait_ge(probs_turned, PAIRS["D"] + 4)
            act.activation(z_odd[:, :, 0:512], z_odd[:, :, 768:1280], ACT.Exp, scale=-1.0)
            act.activation(z_odd[:, :, 1280:1792], z_odd[:, :, 2816:3328], ACT.Exp, scale=-1.0).then_inc(gate_exp, 1)
            turn_act(act, "odd_mix")
            project_x(first["odd_out"])
            if upto < 3:
                return
            turn_act(act, "dsa")
            act.wait_ge(*X_READY["dsa"])
            x_squares_act(act, 5)
            guess_act(act, order, 5)
            act.wait_ge(rstd_ready[5], 1)
            project(first["dsa_in_rest"], 1, z_dsa, rstd[5][:, 0:1])
            project(first["dsa_in"], 4, z_dsa, rstd[5][:, 0:1], trips=2)
            act.wait_ge(index_turned, 1)
            act.activation(qiT[:, 0:2, :], bank[4][:, :].rearrange("p (i q) -> p i q", i=2), ACT.Copy)
            act.activation(qiT[:, 2:4, :], bank[5][:, :].rearrange("p (i q) -> p i q", i=2), ACT.Copy)
            act.activation(kiT, bank[6][:, 0:256], ACT.Copy).then_inc(index_ready, 1)
            for h in range(8):
                act.wait_ge(logits_done, h + 1)
                if h >= 2:
                    act.wait_ge(logits_added, h - 1)
                act.activation(rl[:, h % 2, :], bank[h % 4][:, 0:384], ACT.Relu).then_inc(logits_relu, 1)

            def looped_attention(first_pair, mla, scale):
                evac = (lambda g, p: qk_evac_mla_act(act, g, p)) if mla else (lambda g, p: qk_evac_act(act, g, p, HD ** -0.5))
                evac(first_pair, 0)
                evac(first_pair + 1, 1)
                probs_act(act, first_pair, 0, scale)

                def step(g, p, turns=True, probs=True):
                    if turns:
                        evac(plus(g, 2), p)
                    pt_evac_act(act, g, p)
                    if probs:
                        probs_act(act, plus(g, 1), 1 - p, scale)

                with act.Fori(0, 3) as i:
                    for j in range(2):
                        step(i * 2 + (first_pair + j), j)
                step(first_pair + 6, 0, turns=False)
                step(first_pair + 7, 1, turns=False, probs=False)

            looped_attention(PAIRS["S"], False, 1.0)
            turn_act(act, "dsa_mix")
            project_x(first["dsa_out"])
            if upto < 4:
                return

            def mlp(m):
                r, u = (6, 9)[m], first[f"mlp{m}"]
                turn_act(act, f"mlp{m}")
                act.wait_ge(*X_READY[f"mlp{m}"])
                x_squares_act(act, r)
                guess_act(act, order, r)

                def up(v, b, i=None):
                    split_hi(act, v + 1, i, 4)
                    for j in range(2):
                        act.wait_ge(mm_done, mm_value(v, j, i, 4))
                        act.activation(relu[j][:, :], bank[2 * (b % 2) + j][:, :], ACT.Relu).then_inc(relu_done, 1)
                    for j in range(2):
                        done = 2 * FF_BLOCKS * m + 2 * b + j + 1
                        act.wait_ge(sq_done, done if i is None else i * 4 + done)
                        act.activation(u_hi[b % 2][:, 2 * j:2 * j + 2, :], sq[j][:, :].rearrange("p (f q) -> p f q", f=2),
                                       ACT.Copy).then_inc(u_hi_done, 1)

                up(u, 0)
                up(u + 1, 1)
                split_hi(act, u + 3)
                up(u + 3, 2)
                split_hi(act, u + 5)
                with act.Fori(0, 2) as i:
                    up(u + 5, 3, i)
                    split_hi(act, u + 7, i, 4)
                    up(u + 7, 4, i)
                    split_hi(act, u + 9, i, 4)
                up(u + 13, 7)
                split_hi(act, u + 15)
                split_hi(act, u + 16)

            mlp(0)
            if upto < 5:
                return
            turn_act(act, "mla")
            act.wait_ge(*X_READY["mla"])
            x_squares_act(act, 7)
            guess_act(act, order, 7)
            act.wait_ge(rstd_ready[7], 1)
            project(first["mla_in_rest"], 2, z_mla, rstd[7][:, 0:1])
            act.wait_ge(evac_dve, dve_after[first["q_up"] - 1])
            act.wait_ge(evac_act, act_after[first["q_up"] - 1])
            turn_act(act, "latent")
            for t in range(T):
                act.activation(mix[:, t, 0:Q_LORA], z_mla[:, t, 0:Q_LORA], ACT.Square, scale=Q_LORA ** -0.5,
                               accum_out=ms[8][:, t:t + 1])
                ins = act.activation(mix[:, t, Q_LORA:640], z_mla[:, t, Q_LORA:640], ACT.Square, scale=KV_LORA ** -0.5,
                                     accum_out=ms[8][:, 2 + t:3 + t])
            ins.then_inc(ms_ready[8], 1)
            guess_act(act, order, 8)
            act.wait_ge(rstd_ready[8], 1)
            project(first["q_up"], 2, q_full, rstd[8][:, 0:1])
            project(first["kv_up"], 1, kv_full, rstd[8][:, 2:3])
            looped_attention(PAIRS["L"], True, 96 ** -0.5)
            turn_act(act, "mla_mix")
            project_x(first["mla_out"])
            if upto < 6:
                return
            mlp(1)
            act.wait_ge(*X_READY["final"])
            x_squares_act(act, 10)
            guess_act(act, order, 10)

        @block.vector
        def _(dve):
            order = Order(dve, dve_order)
            dve.wait_ge(params_loaded, 16)
            dve.wait_ge(pos_loaded, 16)
            order.after(dve.tensor_copy(pos[:, :], pos_i[:, :]))
            for t in range(T):
                ins = dve.tensor_scalar(angle[:, t, :], rowp[:, R_FREQ:R_FREQ + 24], pos[:, t:t + 1], None, ALU.mult)
            order.after(ins)
            magic = 1.5 * 2.0 ** 23
            order.after(dve.tensor_scalar(turns[:, :, :], angle[:, :, :], 1.0 / (2.0 * math.pi), magic, ALU.mult, ALU.add))
            order.after(dve.tensor_scalar(turns[:, :, :], turns[:, :, :], magic, None, ALU.subtract))
            c1 = 6.28125
            c2 = float(np.float32(round((2 * math.pi - c1) * 2 ** 20) / 2 ** 20))
            c3 = float(np.float32(2 * math.pi - c1 - c2))
            for c in (c1, c2, c3):
                order.after(dve.scalar_tensor_tensor(out=angle[:, :, :], in0=turns[:, :, :], scalar=-c, in1=angle[:, :, :],
                                                     op0=ALU.mult, op1=ALU.add))
            pi_below = 3.1415925
            order.after(dve.tensor_scalar(angle[:, :, :], angle[:, :, :], pi_below, -pi_below, ALU.min, ALU.max))
            order.after(dve.scalar_tensor_tensor(out=turns[:, :, :], in0=angle[:, :, :], scalar=-1.0, in1=angle[:, :, :],
                                                 op0=ALU.mult, op1=ALU.min))
            dve.tensor_scalar(turns[:, :, :], turns[:, :, :], math.pi / 2, None, ALU.add).then_inc(trig_in, 1)
            for j in range(2):
                ins = dve.tensor_tensor_reduce(r_tmp[:, 0:HD], rowp[:, R_LAM + 128 * j:R_LAM + 128 * j + HD],
                                               rowp[:, R_LAM + 128 * j + HD:R_LAM + 128 * j + 2 * HD], 1.0, 0.0,
                                               ALU.mult, ALU.add, lam_dot[:, j:j + 1])
                if j == 0:
                    order.after(ins)
            ins.then_inc(lam_in, 1)
            dve.wait_ge(gains_turned, 1)
            dve.tensor_copy(gcols[:, :], bank[0][:, 0:GAIN_ROWS]).then_inc(gains_ready, 1)
            dve.wait_ge(gains_ready, 1)
            dve.tensor_scalar(g_mix[:, 0:4], gcols[:, G_SUB:G_SUB + 1].to_broadcast([P, 4]), 1.0 - LAM_INIT, None, ALU.mult)
            for j in range(4):
                ins = dve.tensor_scalar(g_qk[:, j:j + 1], gcols[:, G_HEAD + 2 * j:G_HEAD + 2 * j + 1],
                                        gcols[:, G_HEAD + 2 * j + 1:G_HEAD + 2 * j + 2], HD ** -0.5, ALU.mult, ALU.mult)
            ins.then_inc(gains_ready, 1)
            split_lo(dve, 0)
            turn_dve(dve, "even")
            dve.wait_ge(lam_exp, 1)
            order.after(dve.tensor_tensor(lam_diff[:, :], lam_dot[:, 1:2], lam_dot[:, 0:1], ALU.subtract))
            dve.memset(lam4[:, 0:2], 1.0)
            dve.tensor_scalar(lam4[:, 2:4], lam_diff[:, 0:1].to_broadcast([P, 2]), -LAM_INIT, None, ALU.add).then_inc(lam_ready, 1)
            newton_dve(dve, order, 0)

            def project(u0, count, dst, scale, trips=0):
                if trips:
                    with dve.Fori(0, trips) as i:
                        for j in range(2):
                            split_lo(dve, u0 + j + 1, i, 2)
                            unit_z_dve(dve, u0 + j, dst, scale, i, 2)
                else:
                    for j in range(count):
                        split_lo(dve, u0 + j + 1)
                        unit_z_dve(dve, u0 + j, dst, scale)

            def project_x(u0):
                for j in range(2):
                    split_lo(dve, u0 + j + 1)
                    unit_x_dve(dve, u0 + j)

            def static_attention(kinds):
                pairs = static_pairs(kinds)

                def maxima(kind, i, g):
                    sink = None
                    if kind == "C":
                        sink = rowp[:, R_SINK + i:R_SINK + i + 5:4].unsqueeze(2).to_broadcast([P, 2, T])
                    row_max_dve(dve, g, g % 2, static_biases(kind, i), sink=sink)

                def difference(i, g):
                    p = g % 2
                    dve.wait_ge(probs_done, g + 1)
                    order.after(dve.reciprocal(inv_sum[p][:, :], row_sum[p][:, :]))
                    order.after(dve.tensor_tensor(inv_sum[p][:, :], inv_sum[p][:, :], lam4[:, :], ALU.mult))
                    for t, cols in ((1, slice(0, 256)), (0, slice(256, 384))):
                        ins = dve.tensor_scalar(sc[p][1][:, cols], sc[p][1][:, cols], inv_sum[p][:, 2 + t:3 + t], None, ALU.mult)
                    order.after(ins)
                    for t, cols in ((1, slice(0, 256)), (0, slice(256, 384))):
                        ins = dve.scalar_tensor_tensor(out=sc[p][0][:, cols], in0=sc[p][0][:, cols], scalar=inv_sum[p][:, t:t + 1],
                                                       in1=sc[p][1][:, cols], op0=ALU.mult, op1=ALU.add)
                    ins.then_inc(diff_done, 1)

                def out(kind, i, g):
                    p = g % 2
                    if kind == "A":
                        difference(i, g)
                        pt_evac_dve(dve, g, p)
                        dve.wait_ge(attended, g + 1)
                        dve.tensor_copy(mix[:, :, 128 * i:128 * (i + 1)],
                                        bank[6 + p][:, 0:256].rearrange("p (t e) -> p t e", t=T)).then_inc(heads_out, 1)
                        return
                    pt_evac_dve(dve, g, p)
                    heads_out_dve(dve, g, p, static_out(kind, i), sink=kind == "C")

                maxima(*pairs[0])
                for n, (kind, i, g) in enumerate(pairs):
                    if n + 1 < len(pairs):
                        maxima(*pairs[n + 1])
                    out(kind, i, g)

            project(0, 2, z_even, rstd[0][:, 1:2])
            split_lo(dve, 3)
            unit_z_dve(dve, 2, z_even, rstd[0][:, 1:2])
            with dve.Fori(0, 3) as i:
                for j in range(2):
                    split_lo(dve, 4 + j, i, 2)
                    unit_z_dve(dve, 3 + j, z_even, rstd[0][:, 1:2], i, 2)
            dve.wait_ge(evac_act, act_after[0])
            dve.wait_ge(evac_dve, dve_after[0])
            order.after(dve.tensor_tensor(logf[:, 0, :, :], z_even[:, :, 4096:4104],
                                          rowp[:, R_FB:R_FB + 8].unsqueeze(1).to_broadcast([P, T, 8]), ALU.add))
            dve.scalar_tensor_tensor(out=logf[:, 1, :, :], in0=logf[:, 0, :, :], scalar=-1.0, in1=logf[:, 0, :, :],
                                     op0=ALU.mult, op1=ALU.min).then_inc(forget_in, 1)
            dve.wait_ge(forget_log, 1)
            order.after(dve.scalar_tensor_tensor(out=logf[:, 3, :, :], in0=logf[:, 0, :, :], scalar=0.0, in1=logf[:, 2, :, :],
                                                 op0=ALU.min, op1=ALU.subtract))
            for s in range(T):
                ins = dve.tensor_scalar(qkT[s][:, :].rearrange("p (h m) -> p h m", h=8),
                                        logf[:, 3, s, :].unsqueeze(2).to_broadcast([P, 8, P]), -1.0, None, ALU.mult)
            ins.then_inc(forget_ready, 1)

            def group_sums(r, at, src, groups, width, squares):
                dve.wait_ge(squares_ready, squares)
                return dve.tensor_reduce(ms[r][:, at:at + T * groups].rearrange("p (t g) -> p t g", t=T),
                                         src.rearrange("p t (g d) -> p t g d", d=width), AX.X, ALU.add)

            group_sums(1, 0, mix[:, :, :], 16, HD, 1).then_inc(squares_read, 1)
            dve.wait_ge(cum_done, 1)
            order.after(dve.tensor_copy(cum[:, :, :], bank[0][:, 0:16].rearrange("p (t h) -> p t h", t=T)))
            dve.wait_ge(cum_done, 2)
            dve.wait_ge(even_tables, 4)
            for h in range(8):
                b = bank[4 + h // 2][:, (h % 2) * SEQ:(h % 2 + 1) * SEQ]
                dve.scalar_tensor_tensor(out=bias_b[:, h, 0:256], in0=b, scalar=cum[:, 1, h:h + 1], in1=causal,
                                         op0=ALU.add, op1=ALU.add)
                ins = dve.scalar_tensor_tensor(out=bias_b[:, h, 256:384], in0=b[:, 0:P], scalar=cum[:, 0, h:h + 1],
                                               in1=causal[:, P:], op0=ALU.add, op1=ALU.add)
            ins.then_inc(bias_ready, 1)
            group_sums(1, 32, mix[:, :, :], 16, HD, 2).then_inc(ms_ready[1], 1)
            newton_dve(dve, order, 1)
            dve.wait_ge(lam_ready, 1)
            static_attention("AB")
            group_sums(2, 0, z_even[:, :, 0:512], 4, P, 3).then_inc(ms_ready[2], 1)

            def gates(v, e0, g0, out_cols):
                e, gt = v[:, :, e0:e0 + 512], v[:, :, g0:g0 + 512]
                order.after(dve.tensor_scalar(e, e, 1.0, None, ALU.add))
                order.after(dve.reciprocal(e, e))
                order.after(dve.tensor_tensor(e, e, gt, ALU.mult))
                return dve.tensor_tensor(mix[:, :, out_cols], mix[:, :, out_cols], e, ALU.mult)

            dve.wait_ge(gate_exp, 1)
            order.after(gates(z_even, 512, 1536, slice(0, 512)))
            order.after(gates(z_even, 2560, 3584, slice(512, 1024)))
            newton_dve(dve, order, 2)
            dve.wait_ge(rstd_ready[2], 1)
            heads = mix[:, :, 0:512].rearrange("p t (h d) -> p t h d", h=4)
            dve.tensor_tensor(heads, heads, rstd[2][:, :].rearrange("p (t h) -> p t h", t=T).unsqueeze(3).to_broadcast([P, T, 4, P]),
                              ALU.mult).then_inc(mix_ready, 1)
            turn_dve(dve, "even_mix")
            project_x(first["even_out"])
            if upto < 2:
                return
            turn_dve(dve, "odd")
            newton_dve(dve, order, 3)
            dve.wait_ge(rstd_ready[3], 1)
            project(first["odd_in_rest"], 1, z_odd, rstd[3][:, 1:2])
            project(first["odd_in"], 6, z_odd, rstd[3][:, 1:2], trips=3)
            group_sums(4, 0, mix[:, :, 0:640], 10, HD, 4).then_inc(squares_read, 1)
            group_sums(4, 20, mix[:, :, :], 16, HD, 5).then_inc(ms_ready[4], 1)
            newton_dve(dve, order, 4)
            dve.wait_ge(tables, 9)
            static_attention("CD")
            dve.wait_ge(gate_exp, 2)
            order.after(gates(z_odd, 0, 768, slice(0, 512)))
            gates(z_odd, 1280, 2816, slice(512, 1024)).then_inc(mix_ready, 1)
            turn_dve(dve, "odd_mix")
            project_x(first["odd_out"])
            if upto < 3:
                return
            turn_dve(dve, "dsa")
            newton_dve(dve, order, 5)
            dve.wait_ge(rstd_ready[5], 1)
            project(first["dsa_in_rest"], 1, z_dsa, rstd[5][:, 1:2])
            project(first["dsa_in"], 4, z_dsa, rstd[5][:, 1:2], trips=2)

            def rope(groups):
                parts = []
                for v, f0, half, at in groups:
                    heads = v.shape[2]
                    cos = cosine[:, :, f0:f0 + half].unsqueeze(2).to_broadcast([P, T, heads, half])
                    sin = sine[:, :, f0:f0 + half].unsqueeze(2).to_broadcast([P, T, heads, half])
                    a, b = v[:, :, :, 0:half], v[:, :, :, half:2 * half]
                    n = T * heads * half
                    flat = mix[:, :, :].rearrange("p t n -> p (t n)")
                    tmp = [flat[:, at + n * m:at + n * (m + 1)].rearrange("p (t h d) -> p t h d", t=T, h=heads) for m in range(4)]
                    dve.tensor_tensor(tmp[0], a, cos, ALU.mult)
                    dve.tensor_tensor(tmp[1], b, sin, ALU.mult)
                    dve.tensor_tensor(tmp[2], b, cos, ALU.mult)
                    last = dve.tensor_tensor(tmp[3], a, sin, ALU.mult)
                    parts.append((a, b, tmp))
                order.after(last)
                for a, b, tmp in parts:
                    dve.tensor_tensor(a, tmp[0], tmp[1], ALU.subtract)
                    last = dve.tensor_tensor(b, tmp[2], tmp[3], ALU.add)
                return last

            dve.wait_ge(evac_act, act_after[first["dsa_out"] - 1])
            dve.wait_ge(evac_dve, dve_after[first["dsa_out"] - 1])
            dve.wait_ge(trig_ready, 1)

            def rotated(v, lo, hi, width, at, rot):
                return v[:, :, lo:hi].rearrange("p t (h d) -> p t h d", d=width)[:, :, :, at:at + rot]

            rope([(rotated(z_dsa, 1536, 2112, HD, 0, 16), 0, 8, 0)]).then_inc(roped, 1)
            dve.tensor_scalar(wi[:, :, :], z_dsa[:, :, 2112:2120], (8 ** -0.5) * (HD ** -0.5), None, ALU.mult)
            rope([(rotated(z_dsa, 0, 1280, HD, 0, 16), 0, 8, 576)]).then_inc(roped, 1)
            halves = ((1, slice(0, 256)), (0, slice(256, 384)))
            for h in range(8):
                dve.wait_ge(logits_relu, h + 1)
                for t, cols in halves:
                    if h == 0:
                        ins = dve.tensor_scalar(score[:, cols], rl[:, 0, cols], wi[:, t, 0:1], None, ALU.mult)
                    else:
                        ins = dve.scalar_tensor_tensor(out=score[:, cols], in0=rl[:, h % 2, cols], scalar=wi[:, t, h:h + 1],
                                                       in1=score[:, cols], op0=ALU.mult, op1=ALU.add)
                ins.then_inc(logits_added, 1)
                dve.wait_ge(logits_added, h + 1)
            for t, cols in halves:
                ins = dve.scalar_tensor_tensor(out=score[:, cols], in0=chunked[:, SEQ - (cols.stop - cols.start):],
                                               scalar=HIDDEN / MASKED, in1=score[:, cols], op0=ALU.mult, op1=ALU.add)
            order.after(ins)
            for _ in range(TOPK // 8):
                for t, cols in halves:
                    ins = dve.max(best[:, t, :], score[:, cols])
                order.after(ins)
                for t, cols in halves:
                    ins = dve.match_replace(score[:, cols], best[:, t, :], score[:, cols], TAKEN)
                order.after(ins)
            order.after(dve.tensor_scalar(bias_s, score, (HIDDEN + TAKEN) / 2, MASKED, ALU.is_gt, ALU.mult))

            def looped_attention(first_pair, biases, scale, dst):
                row_max_dve(dve, first_pair, 0, biases, scale)

                def step(g, i, p, maxima=True):
                    if maxima:
                        row_max_dve(dve, plus(g, 1), 1 - p, biases, scale)
                    pt_evac_dve(dve, g, p)
                    heads_out_dve(dve, g, p, dst(i))

                with dve.Fori(0, 3) as i:
                    for j in range(2):
                        step(i * 2 + (first_pair + j), i * 2 + j, j)
                step(first_pair + 6, 6, 0)
                step(first_pair + 7, 7, 1, maxima=False)

            def sparse_out(i):
                return mix[:, :, :].rearrange("p t (c s) -> p c t s", c=2)[:, :, :, bass.ds(i * HD, HD)]

            def latent_out(i):
                return mix[:, :, bass.ds(i * P, P)].rearrange("p t (c d) -> p c t d", c=2)

            looped_attention(PAIRS["S"], [(bias_s[:, 0:256], bias_s[:, 256:384])] * 2, 1.0, sparse_out)
            turn_dve(dve, "dsa_mix")
            project_x(first["dsa_out"])
            if upto < 4:
                return

            def mlp(m):
                r, u = (6, 9)[m], first[f"mlp{m}"]
                turn_dve(dve, f"mlp{m}")
                newton_dve(dve, order, r, square=rstd_sq[m][:, :])

                def up(v, b, i=None):
                    split_lo(dve, v + 1, i, 4)
                    base = 2 * FF_BLOCKS * m + 2 * b
                    if base > 0:
                        dve.wait_ge(u_lo_done, base if i is None else i * 4 + base)
                    for j in range(2):
                        dve.wait_ge(relu_done, base + j + 1 if i is None else i * 4 + (base + j + 1))
                        dve.tensor_tensor(sq[j][:, :], relu[j][:, :], relu[j][:, :], ALU.mult).then_inc(sq_done, 1)
                    for j in range(2):
                        dve.wait_ge(u_hi_done, base + j + 1 if i is None else i * 4 + (base + j + 1))
                        dve.tensor_tensor(u_lo[b % 2][:, 2 * j:2 * j + 2, :], sq[j][:, :].rearrange("p (f q) -> p f q", f=2),
                                          u_hi[b % 2][:, 2 * j:2 * j + 2, :].bitcast(F32), ALU.subtract).then_inc(u_lo_done, 1)

                up(u, 0)
                up(u + 1, 1)
                split_lo(dve, u + 3)
                up(u + 3, 2)
                split_lo(dve, u + 5)
                with dve.Fori(0, 2) as i:
                    up(u + 5, 3, i)
                    split_lo(dve, u + 7, i, 4)
                    up(u + 7, 4, i)
                    split_lo(dve, u + 9, i, 4)
                up(u + 13, 7)
                split_lo(dve, u + 15)
                split_lo(dve, u + 16)
                dve.wait_ge(mm_done, mm_after[u + 15])
                dve.wait_ge(rstd_ready[r], 1)
                for t in range(T):
                    for half in range(2):
                        cols = slice(half * BLOCK, (half + 1) * BLOCK)
                        ins = dve.scalar_tensor_tensor(out=x[:, t, cols], in0=bank[4 + 2 * t + half][:, :],
                                                       scalar=rstd_sq[m][:, t:t + 1], in1=x[:, t, cols], op0=ALU.mult, op1=ALU.add)
                ins.then_inc(x_ready, 1)

            mlp(0)
            if upto < 5:
                return
            turn_dve(dve, "mla")
            newton_dve(dve, order, 7)
            dve.wait_ge(rstd_ready[7], 1)
            project(first["mla_in_rest"], 2, z_mla, rstd[7][:, 1:2])
            turn_dve(dve, "latent")
            newton_dve(dve, order, 8)
            dve.wait_ge(rstd_ready[8], 1)
            project(first["q_up"], 2, q_full, rstd[8][:, 1:2])
            project(first["kv_up"], 1, kv_full, rstd[8][:, 3:4])
            dve.wait_ge(evac_act, act_after[first["kv_up"]])
            dve.wait_ge(evac_dve, dve_after[first["kv_up"]])
            rope([(rotated(z_mla, 640, 672, 32, 0, 32), 8, 16, 0)])
            dve.wait_ge(dve_order, order.n)
            q_rope = rotated(q_full, 0, Q_UP, 96, 64, 32)
            for hh in range(2):
                last = rope([(q_rope[:, :, 4 * m + 8 * hh:4 * m + 8 * hh + 4, :], 8, 16, 256 + 512 * m) for m in range(2)])
                if hh == 0:
                    order.after(last)
            last.then_inc(mla_roped, 1)
            looped_attention(PAIRS["L"], [(chunked[:, :], chunked[:, P:])] * 2, 96 ** -0.5, latent_out)
            turn_dve(dve, "mla_mix")
            project_x(first["mla_out"])
            if upto < 6:
                return
            mlp(1)
            newton_dve(dve, order, 10)
            dve.wait_ge(rstd_ready[10], 1)
            dve.wait_ge(final_loaded, 16)
            for t in range(T):
                dve.scalar_tensor_tensor(out=mix[:, t, :], in0=x[:, t, :], scalar=rstd[10][:, t:t + 1], in1=g_final[:, :],
                                         op0=ALU.mult, op1=ALU.mult).then_inc(final_done, 1)


WEIGHTS = {"even_in": "even_w_in", "even_out": "even_w_out", "odd_in": "odd_w_in", "odd_out": "odd_w_out",
           "dsa_in": "a_w_in_2", "dsa_out": "a_w_out_2", "mla_in": "b_w_in_2", "q_up": "b_w_q_up_2",
           "kv_up": "b_w_kv_up_2", "mla_out": "b_w_out_2"}


def kernel(**inputs):
    import concourse.bacc as bacc
    from concourse.bass_utils import run_bass_kernel_spmd

    a = {k: np.ascontiguousarray(v) for k, v in inputs.items()}
    arrays = {name: a[key][0] for name, key in WEIGHTS.items()}
    for m in range(2):
        arrays[f"up{m}"] = a["mlp_w_up_2"][m]
        arrays[f"down{m}"] = a["mlp_w_down_2"][m]
    rows = [a["even_ln_g"], a["odd_ln_g"], a["attn_norm_2"], a["mlp_norm_2"], a["b_q_norm_2"], a["b_kv_norm_2"], a["a_subln_g"]]
    for k in ("a", "b", "c", "d"):
        for which in ("q", "k"):
            rows += [a[f"{k}_{which}_norm_g"]] * 2
    arrays["gain_rows"] = np.concatenate([r.reshape(-1) for r in rows]).reshape(GAIN_ROWS, P)
    freq = [500000.0 ** (-np.arange(0, rot, 2) / rot) for rot in (16, 32)]
    params = [a["a_lambda_q1"], a["a_lambda_k1"], a["a_lambda_q2"], a["a_lambda_k2"], a["b_forget_bias"], a["c_sinks"]]
    arrays["row_params"] = np.concatenate([r.reshape(-1) for r in params] + [f.astype(np.float32) for f in freq])
    table = a["d_rel_bias"][0]
    entry = np.clip(np.arange(P)[:, None] + P - np.arange(SEQ)[None, :] + 63, 0, table.shape[1] - 1)
    arrays["rel_band"] = np.ascontiguousarray(table[:, entry].transpose(1, 0, 2))
    arrays["x"] = a["x"][0]
    arrays["positions"] = np.ascontiguousarray(a["positions_2"][0].reshape(T, P).T)
    arrays["final_gain"] = a["final_norm_2"]

    nc = bacc.Bacc("TRN2", target_bir_lowering=False, num_devices=1)
    aps = {k: nc.dram_tensor(f"in_{k}", v.shape, mybir.dt.from_np(v.dtype), kind="ExternalInput").ap() for k, v in arrays.items()}
    out = nc.dram_tensor("out", (SEQ, DM), F32, kind="ExternalOutput").ap()
    program(nc, aps, aps["x"], aps["gain_rows"], aps["row_params"], aps["positions"], aps["rel_band"], aps["final_gain"], out)
    r = run_bass_kernel_spmd(nc, [{f"in_{k}": v for k, v in arrays.items()}], core_ids=[0])
    return r.results[0]["out"].reshape(1, SEQ, DM)
```

```python
import math
from contextlib import ExitStack

import numpy as np

import concourse.bass as bass
from concourse import mybir
from concourse.alu_op_type import AluOpType as ALU

F32 = mybir.dt.float32
F32R = mybir.dt.float32r
I32 = mybir.dt.int32
ACT = mybir.ActivationFunctionType
AX = mybir.AxisListType

P = 128
SEQ = 256
T = SEQ // P
DM = 1024
KC = DM // P
HD = 64
EPS = 1e-6
MASKED = -1e30
HIDDEN = -3e38
TAKEN = -3.3e38
N_EVEN, N_ODD, N_DSA, N_MLA = 4104, 3328, 2120, 672
Q_LORA, KV_LORA, ROPE = 384, 256, 32
Q_UP, KV_UP = 1536, 2048
FF_BLOCKS = 8
TOPK = 64
BLOCK = 512
LAM_INIT = 0.8 - 0.6 * math.exp(0.0)
G_EVEN, G_ODD, G_DSA, G_MLA, G_MLP0, G_MLP1, G_QL, G_KVL, G_SUB, G_HEAD = 0, 8, 16, 24, 32, 40, 48, 51, 53, 54
GAIN_ROWS = G_HEAD + 8
R_LAM, R_FB, R_SINK, R_FREQ = 0, 256, 264, 272
ROW_PARAMS = R_FREQ + 24


def weight_units():
    units, first = [], {}

    def columns(stage, matrix, kind, start, end, width, kc=KC, split=1, row=0):
        first.setdefault(stage, len(units))
        for c in range(start, end, width):
            w = min(width, end - c)
            units.append((matrix, kind, row, kc, c, w, [(i * (w // split), w // split) for i in range(split)]))

    for start, end in ((4096, N_EVEN), (0, 512), (512, 1024), (1024, 1536), (2048, 2560), (2560, 3072), (3072, 3584),
                       (1536, 2048), (3584, 4096)):
        columns("even_in", "even_in", "z", start, end, BLOCK)
    columns("even_out", "even_out", "x", 0, DM, BLOCK)
    for start, end in ((512, 768), (0, 512), (1280, 1792), (1792, 2304), (2304, 2816), (768, 1280), (2816, 3328)):
        columns("odd_in", "odd_in", "z", start, end, BLOCK)
    columns("odd_out", "odd_out", "x", 0, DM, BLOCK)
    for start, end in ((2048, N_DSA), (1536, 2048), (1024, 1536), (0, 512), (512, 1024)):
        columns("dsa_in", "dsa_in", "z", start, end, BLOCK)
    columns("dsa_out", "dsa_out", "x", 0, DM, BLOCK)

    def mlp(m):
        first[f"mlp{m}"] = len(units)
        for b in range(FF_BLOCKS + 1):
            if b < FF_BLOCKS:
                units.append((f"up{m}", "up", 0, KC, b * BLOCK, BLOCK, [(0, 256), (256, 256)]))
            if b:
                units.append((f"down{m}", "down", 4 * (b - 1), 4, 0, DM, [(0, DM)]))

    mlp(0)
    columns("mla_in_rest", "mla_in", "z", 512, N_MLA, BLOCK)
    columns("mla_in", "mla_in", "z", 0, 512, BLOCK)
    columns("q_up", "q_up", "z", 0, Q_UP, 768, Q_LORA // P, split=2)
    columns("kv_up", "kv_up", "z", 0, KV_UP, KV_UP, KV_LORA // P, split=4)
    columns("mla_out", "mla_out", "x", 0, DM, BLOCK)
    mlp(1)
    return units, first


def program(nc, w, x_in, gain_rows, row_params, positions, rel_band, final_gain, out, upto=99):
    units, first = weight_units()
    mm_after, act_after, dve_after, pair_of = [], [], [], []
    mm = act_n = dve_n = blocks = 0
    block_evacs = []
    for _, kind, _, _, _, _, parts in units:
        pair_of.append(blocks)
        if kind == "down":
            mm += 1
        else:
            mm += len(parts)
        if kind in ("z", "x"):
            for _ in parts:
                act_n += kind == "z"
                dve_n += 1
                blocks += 1
                block_evacs.append((act_n, dve_n))
        mm_after.append(mm)
        act_after.append(act_n)
        dve_after.append(dve_n)

    def w_view(u):
        matrix, _, row, kc, c, n, _ = units[u]
        return w[matrix][row * P:(row + kc) * P, c:c + n].rearrange("(k p) n -> p k n", p=P)

    ctx = ExitStack()
    with ctx:
        def sb(name, shape, dt=F32):
            return ctx.enter_context(nc.sbuf_tensor(name, shape, dt))

        def sem(name):
            return ctx.enter_context(nc.semaphore(name))

        x = sb("x", [P, T, DM])
        raw = [sb(f"raw{i}", [P, 4096]) for i in range(2)]
        w_hi = [sb(f"w_hi{i}", [P, 4096], F32R) for i in range(2)]
        w_lo = [sb(f"w_lo{i}", [P, 4096], F32R) for i in range(2)]
        h_hi = sb("h_hi", [P, KC, SEQ], F32R)
        h_lo = sb("h_lo", [P, KC, SEQ], F32R)
        mix = sb("mix", [P, T, DM])
        ident = sb("ident", [P, P])
        chunked = sb("chunked", [P, SEQ])
        gcols = sb("gcols", [P, GAIN_ROWS])
        g_mix = sb("g_mix", [P, KC])
        g_qk = sb("g_qk", [P, 4])
        rowp = sb("rowp", [P, ROW_PARAMS])
        lam4 = sb("lam4", [P, 4])
        wait_carrier = sb("wait_carrier", [P, 1])
        lam_diff = sb("lam_diff", [P, 1])
        lam_dot = sb("lam_dot", [P, 2])
        eps = sb("eps", [P, 1])
        pos_i = sb("pos_i", [P, T], I32)
        pos = sb("pos", [P, T])
        angle = sb("angle", [P, T, 24])
        turns = sb("turns", [P, T, 24])
        cosine = sb("cosine", [P, T, 24])
        sine = sb("sine", [P, T, 24])
        R_WIDTH = [2, 32, 8, 2, 20, 2, 2, 2, 4, 2, 2, 32, 32]
        ms = [sb(f"ms{i}", [P, n]) for i, n in enumerate(R_WIDTH)]
        rstd = [sb(f"rstd{i}", [P, n]) for i, n in enumerate(R_WIDTH)]
        r_tmp = sb("r_tmp", [P, 64])
        r_log = sb("r_log", [P, 64])
        rstd_sq = [sb(f"rstd_sq{i}", [P, T]) for i in range(2)]

        both = ExitStack()
        with both:
            def sa(name, shape, dt=F32):
                return both.enter_context(nc.sbuf_tensor(name, shape, dt))
            z = sa("z", [P, T * N_EVEN])
            tab = sa("tab", [P, 4096])
            qs = [sa(f"qs{i}", [P, 256]) for i in range(2)]
            ks = [sa(f"ks{i}", [P, 256]) for i in range(2)]
            qkT = [sa(f"qkT{i}", [P, 1024]) for i in range(2)]
            sc = [[sa(f"sc{i}{c}", [P, 384]) for c in range(2)] for i in range(2)]
            pT = [sa(f"pT{i}", [P, 2, 384]) for i in range(2)]
            row_max = [sa(f"row_max{i}", [P, 4]) for i in range(2)]
            neg_max = [sa(f"neg_max{i}", [P, 4]) for i in range(2)]
            row_sum = [sa(f"row_sum{i}", [P, 4]) for i in range(2)]
            inv_sum = [sa(f"inv_sum{i}", [P, 4]) for i in range(2)]
            sink_e = [sa(f"sink_e{i}", [P, 4]) for i in range(2)]
            logf = sa("logf", [P, 4, T, 8])
            cum = sa("cum", [P, T, 8])
            wi = sa("wi", [P, T, 8])
            best = sa("best", [P, T, 8])
        upper = pT[0][:, :, 0:SEQ]
        causal = sc[1][0][:, 0:SEQ]
        mlpb = ExitStack()
        with mlpb:
            def sm(name, shape, dt=F32):
                return mlpb.enter_context(nc.sbuf_tensor(name, shape, dt))
            relu = [sm(f"relu{i}", [P, BLOCK]) for i in range(2)]
            sq = [sm(f"sq{i}", [P, BLOCK]) for i in range(2)]
            u_hi = [sm(f"u_hi{i}", [P, 4, SEQ], F32R) for i in range(2)]
            u_lo = [sm(f"u_lo{i}", [P, 4, SEQ], F32R) for i in range(2)]
            g_final = sm("g_final", [P, DM])

        bank = [ctx.enter_context(nc.psum_tensor(f"bank{i}", [P, BLOCK], F32)) for i in range(8)]

        x_loaded, rows_loaded, params_loaded = sem("x_loaded"), sem("rows_loaded"), sem("params_loaded")
        pos_loaded, band_loaded, final_loaded = sem("pos_loaded"), sem("band_loaded"), sem("final_loaded")
        stored = sem("stored")
        raw_loaded = [sem(f"raw_loaded{i}") for i in range(2)]
        hi_split, lo_split = sem("hi_split"), sem("lo_split")
        mm_done, evac_act, evac_dve = sem("mm_done"), sem("evac_act"), sem("evac_dve")
        consts = sem("consts")
        tables, even_tables = sem("tables"), sem("even_tables")
        gains_turned, gains_ready = sem("gains_turned"), sem("gains_ready")
        trig_in, trig_ready = sem("trig_in"), sem("trig_ready")
        lam_in, lam_exp, lam_ready = sem("lam_in"), sem("lam_exp"), sem("lam_ready")
        turned, hi_turned, lo_turned = sem("turned"), sem("hi_turned"), sem("lo_turned")
        x_ready, mix_ready = sem("x_ready"), sem("mix_ready")
        ms_ready = [sem(f"ms_ready{i}") for i in range(13)]
        guess_ready = [sem(f"guess_ready{i}") for i in range(13)]
        rstd_ready = [sem(f"rstd_ready{i}") for i in range(13)]
        squares_ready, squares_read = sem("squares_ready"), sem("squares_read")
        act_order, dve_order, pool_order = sem("act_order"), sem("dve_order"), sem("pool_order")
        relu_done, sq_done, u_hi_done, u_lo_done = sem("relu_done"), sem("sq_done"), sem("u_hi_done"), sem("u_lo_done")
        staged, qk_turned, qk_ready = sem("staged"), sem("qk_turned"), sem("qk_ready")
        scores_done, max_done, probs_done = sem("scores_done"), sem("max_done"), sem("probs_done")
        diff_done, probs_turned, pt_act, pt_dve = sem("diff_done"), sem("probs_turned"), sem("pt_act"), sem("pt_dve")
        attended, heads_out = sem("attended"), sem("heads_out")
        raw_max_done, inv_done = sem("raw_max_done"), sem("inv_done")
        forget_in, forget_log, forget_ready = sem("forget_in"), sem("forget_log"), sem("forget_ready")
        cum_done, cum_ready, bias_ready = sem("cum_done"), sem("cum_ready"), sem("bias_ready")
        tanh_first, tanh_second = sem("tanh_first"), sem("tanh_second")
        first_gated = sem("first_gated")
        roped, ki_staged, index_turned, index_ready = sem("roped"), sem("ki_staged"), sem("index_turned"), sem("index_ready")
        logits_done, logits_relu, logits_added = sem("logits_done"), sem("logits_relu"), sem("logits_added")
        mla_roped, kr_staged = sem("mla_roped"), sem("kr_staged")
        final_done = sem("final_done")

        TURNS = {"even": (8, gcols, G_EVEN), "even_mix": (8, g_mix, 0), "odd": (8, gcols, G_ODD), "odd_mix": (8, 0.5, 0),
                 "dsa": (8, gcols, G_DSA), "dsa_mix": (8, None, 0), "mlp0": (8, gcols, G_MLP0), "mla": (8, gcols, G_MLA),
                 "latent": (5, gcols, G_QL), "mla_mix": (8, None, 0), "mlp1": (8, gcols, G_MLP1)}
        turn_base, n = {}, 0
        for name, (chunks, _, _) in TURNS.items():
            turn_base[name] = n
            n += (chunks + 1) // 2
        X_READY = {"odd": (evac_dve, dve_after[first["even_out"] + 1]), "dsa": (evac_dve, dve_after[first["odd_out"] + 1]),
                   "mlp0": (evac_dve, dve_after[first["dsa_out"] + 1]), "mla": (x_ready, 1),
                   "mlp1": (evac_dve, dve_after[first["mla_out"] + 1]), "final": (x_ready, 2)}
        STATS = {"A": 1, "B": 11, "C": 4, "D": 12}
        PAIRS = {"A": 0, "B": 4, "C": 8, "D": 12, "S": 16, "L": 24}

        z_even = z[:, 0:T * N_EVEN].rearrange("p (t n) -> p t n", t=T)
        z_odd = z[:, 0:T * N_ODD].rearrange("p (t n) -> p t n", t=T)
        z_dsa = z[:, 0:T * N_DSA].rearrange("p (t n) -> p t n", t=T)
        z_mla = tab[:, 0:T * N_MLA].rearrange("p (t n) -> p t n", t=T)
        q_full = z[:, 0:T * Q_UP].rearrange("p (t n) -> p t n", t=T)
        kv_full = z[:, T * Q_UP:T * (Q_UP + KV_UP)].rearrange("p (t n) -> p t n", t=T)
        qs_mla = [tab[:, 1536 + 768 * i:1920 + 768 * i] for i in range(2)]
        ks_mla = [tab[:, 1920 + 768 * i:2304 + 768 * i] for i in range(2)]
        bias_a = tab[:, 0:1024].rearrange("p (h j) -> p h j", h=4)
        bias_b = tab[:, 1024:4096].rearrange("p (h j) -> p h j", h=8)
        bias_c = tab[:, 0:2048].rearrange("p (h j) -> p h j", h=8)
        bias_d = tab[:, 2048:4096].rearrange("p (h j) -> p h j", h=8)
        bias_s = tab[:, 0:384]
        qiT = tab[:, 512:1536].rearrange("p (i q) -> p i q", i=4)
        kiT = tab[:, 1536:1792]
        score = tab[:, 1792:2176]
        rl = tab[:, 2304:3072].rearrange("p (i q) -> p i q", i=2)

        def wait_from(e, s, value):
            if not isinstance(value, int) or value > 0:
                e.wait_ge(s, value)

        def load_unit(e, u, i=None, per=0):
            matrix, kind, row, kc, c, n, _ = units[u]
            slot = u % 2
            dst = raw[slot][:, 0:kc * n].rearrange("p (k n) -> p k n", k=kc)
            if i is None:
                if u >= 2:
                    e.wait_ge(lo_split, u - 1)
                e.dma_start(dst, w_view(u)).then_inc(raw_loaded[slot], 16)
                return
            e.wait_ge(lo_split, i * per + (u - 1))
            if kind == "down":
                rows = w[matrix][bass.ds(i * (per // 2 * 4 * P) + row * P, kc * P), :]
                e.dma_start(dst, rows.rearrange("(k p) n -> p k n", p=P)).then_inc(raw_loaded[slot], 16)
            else:
                step = per // 2 if kind == "up" else per
                cols = w[matrix][:, bass.ds(i * (step * n) + c, n)]
                e.dma_start(dst, cols.rearrange("(k p) n -> p k n", p=P)).then_inc(raw_loaded[slot], 16)

        def split_hi(e, u, i=None, per=0):
            if u >= len(units):
                return
            slot, size = u % 2, units[u][3] * units[u][5]
            if i is None:
                e.wait_ge(raw_loaded[slot], 16 * (u // 2 + 1))
                if u >= 2:
                    e.wait_ge(mm_done, mm_after[u - 2])
            else:
                e.wait_ge(raw_loaded[slot], i * (8 * per) + 16 * (u // 2 + 1))
                e.wait_ge(mm_done, i * (mm_after[u - 2 + per] - mm_after[u - 2]) + mm_after[u - 2])
            e.activation(w_hi[slot][:, 0:size], raw[slot][:, 0:size], ACT.Copy).then_inc(hi_split, 1)

        def split_lo_half(e, u, half):
            slot, size = u % 2, units[u][3] * units[u][5] // 2
            cols = slice(half * size, (half + 1) * size)
            e.wait_ge(hi_split, u + 1)
            ins = e.tensor_tensor(w_lo[slot][:, cols], raw[slot][:, cols], w_hi[slot][:, cols].bitcast(F32), ALU.subtract)
            if half:
                ins.then_inc(lo_split, 1)

        def split_lo(e, u, i=None, per=0):
            if u >= len(units):
                return
            slot, size = u % 2, units[u][3] * units[u][5]
            e.wait_ge(hi_split, u + 1 if i is None else i * per + (u + 1))
            e.tensor_tensor(w_lo[slot][:, 0:size], raw[slot][:, 0:size], w_hi[slot][:, 0:size].bitcast(F32),
                            ALU.subtract).then_inc(lo_split, 1)

        def turn_scale(gain, column):
            if gain is None:
                return 1.0
            return gain if isinstance(gain, float) else gain[:, column:column + 1]

        def turn_pe(e, name, src, c0=0, c1=None):
            chunks = TURNS[name][0]
            for c in range(c0, chunks if c1 is None else c1):
                for t in range(T):
                    last = e.transpose(bank[4 + c // 2][:, (c % 2) * SEQ + t * P:(c % 2) * SEQ + (t + 1) * P],
                                       src[:, t, c * P:(c + 1) * P], ident[:, :])
                if c % 2 or c == chunks - 1:
                    last.then_inc(turned, 1)

        def x_mm_done(name):
            return mm_after[first[{"odd": "even_out", "dsa": "odd_out", "mlp0": "dsa_out", "mlp1": "mla_out"}[name]] + 1]

        def turn_act(e, name):
            chunks, gain, g0 = TURNS[name]
            if X_READY.get(name, (None,))[0] is evac_dve:
                e.wait_ge(mm_done, x_mm_done(name))
            for c in range(chunks):
                if c % 2 == 0:
                    e.wait_ge(turned, turn_base[name] + c // 2 + 1)
                scale = turn_scale(gain, g0 + c)
                ins = e.activation(h_hi[:, c, :], bank[4 + c // 2][:, (c % 2) * SEQ:(c % 2 + 1) * SEQ], ACT.Copy, scale=scale)
                if c % 2 or c == chunks - 1:
                    ins.then_inc(hi_turned, 1)

        def turn_dve(e, name):
            chunks, gain, g0 = TURNS[name]
            for c in range(chunks):
                if c % 2 == 0:
                    e.wait_ge(hi_turned, turn_base[name] + c // 2 + 1)
                scale = turn_scale(gain, g0 + c)
                ins = e.scalar_tensor_tensor(out=h_lo[:, c, :], in0=bank[4 + c // 2][:, (c % 2) * SEQ:(c % 2 + 1) * SEQ],
                                             scalar=scale, in1=h_hi[:, c, :].bitcast(F32), op0=ALU.mult, op1=ALU.subtract)
                if c % 2 or c == chunks - 1:
                    ins.then_inc(lo_turned, 1)

        def wait_turned(e, name):
            e.wait_ge(lo_turned, turn_base[name] + (TURNS[name][0] + 1) // 2)

        def unit_pe(e, u, i=None, per=0, chunk0=0, fresh=None):
            _, kind, _, kc, _, n, parts = units[u]
            slot = u % 2
            hi = w_hi[slot][:, 0:kc * n].rearrange("p (k n) -> p k n", k=kc)
            lo = w_lo[slot][:, 0:kc * n].rearrange("p (k n) -> p k n", k=kc)
            e.wait_ge(lo_split, u + 1 if i is None else i * per + (u + 1))
            for b, (c0, cn) in enumerate(parts):
                j = pair_of[u] + b
                if j >= 2:
                    a, d = block_evacs[j - 2]
                    if i is None:
                        wait_from(e, evac_act, a)
                        wait_from(e, evac_dve, d)
                    else:
                        a1, d1 = block_evacs[j - 2 + per]
                        assert a1 - a in (0, per) and d1 - d == per
                        e.wait_ge(evac_act, i * per + a)
                        e.wait_ge(evac_dve, i * per + d)
                for t in range(T):
                    dst = bank[2 * (j % 2) + t][:, 0:cn]
                    for k in range(kc):
                        if fresh and t == 0 and b == 0:
                            e.wait_ge(lo_turned, turn_base[fresh] + (chunk0 + k) // 2 + 1)
                        h, l = h_hi[:, chunk0 + k, t * P:(t + 1) * P], h_lo[:, chunk0 + k, t * P:(t + 1) * P]
                        e.matmul(dst, h, hi[:, k, c0:c0 + cn], start=(k == 0), stop=False)
                        e.matmul(dst, h, lo[:, k, c0:c0 + cn], start=False, stop=False)
                        last = e.matmul(dst, l, hi[:, k, c0:c0 + cn], start=False, stop=(k == kc - 1))
                last.then_inc(mm_done, 1)

        def unit_eighths_pe(e, u, e0, e1):
            n, j = units[u][5], pair_of[u]
            hi = w_hi[u % 2][:, 0:KC * n].rearrange("p (k n) -> p k n", k=KC)
            lo = w_lo[u % 2][:, 0:KC * n].rearrange("p (k n) -> p k n", k=KC)
            if e0 == 0:
                e.wait_ge(lo_split, u + 1)
                a, d = block_evacs[j - 2]
                wait_from(e, evac_act, a)
                wait_from(e, evac_dve, d)
            for piece in range(e0, e1):
                t = piece // 4
                dst = bank[2 * (j % 2) + t][:, 0:n]
                for k in range(2 * (piece % 4), 2 * (piece % 4) + 2):
                    h, l = h_hi[:, k, t * P:(t + 1) * P], h_lo[:, k, t * P:(t + 1) * P]
                    e.matmul(dst, h, hi[:, k, :], start=(k == 0), stop=False)
                    e.matmul(dst, h, lo[:, k, :], start=False, stop=False)
                    last = e.matmul(dst, l, hi[:, k, :], start=False, stop=(k == KC - 1))
            if e1 == 8:
                last.then_inc(mm_done, 1)

        def mm_value(u, b, i, per):
            v = mm_after[u] - len(units[u][6]) + b + 1
            return v if i is None else i * (mm_after[u + per] - mm_after[u]) + v

        def unit_z_act(e, u, dst, scale, i=None, per=0):
            for b, (c0, cn) in enumerate(units[u][6]):
                j = pair_of[u] + b
                e.wait_ge(mm_done, mm_value(u, b, i, per))
                c = units[u][4] + c0 if i is None else i * (per * units[u][5]) + (units[u][4] + c0)
                e.activation(dst[:, 0, bass.ds(c, cn)], bank[2 * (j % 2)][:, 0:cn], ACT.Copy, scale=scale).then_inc(evac_act, 1)

        def unit_z_dve(e, u, dst, scale, i=None, per=0):
            for b, (c0, cn) in enumerate(units[u][6]):
                j = pair_of[u] + b
                e.wait_ge(mm_done, mm_value(u, b, i, per))
                c = units[u][4] + c0 if i is None else i * (per * units[u][5]) + (units[u][4] + c0)
                e.tensor_scalar(dst[:, 1, bass.ds(c, cn)], bank[2 * (j % 2) + 1][:, 0:cn], scale, None, ALU.mult).then_inc(evac_dve, 1)

        def unit_x_dve(e, u):
            j, c = pair_of[u], units[u][4]
            e.wait_ge(mm_done, mm_after[u])
            e.tensor_tensor(x[:, 0, c:c + BLOCK], bank[2 * (j % 2)][:, :], x[:, 0, c:c + BLOCK], ALU.add)
            e.tensor_tensor(x[:, 1, c:c + BLOCK], bank[2 * (j % 2) + 1][:, :], x[:, 1, c:c + BLOCK], ALU.add).then_inc(evac_dve, 1)

        class Order:
            def __init__(self, e, s):
                self.e, self.s, self.n = e, s, 0

            def after(self, ins):
                ins.then_inc(self.s, 1)
                self.n += 1
                self.e.wait_ge(self.s, self.n)

        def x_squares_act(e, r):
            for t in range(T):
                ins = e.activation(mix[:, t, :], x[:, t, :], ACT.Square, scale=DM ** -0.5, accum_out=ms[r][:, t:t + 1])
            ins.then_inc(ms_ready[r], 1)

        def guess_act(e, order, r, count=1):
            n = R_WIDTH[r]
            e.wait_ge(ms_ready[r], count)
            order.after(e.activation(r_log[:, 0:n], ms[r][:, :], ACT.Ln, bias=eps[:, 0:1]))
            e.activation(rstd[r][:, :], r_log[:, 0:n], ACT.Exp, scale=-0.5).then_inc(guess_ready[r], 1)

        def newton_dve(e, order, r, square=None):
            n = R_WIDTH[r]
            y, tmp = rstd[r][:, :], r_tmp[:, 0:n]
            e.wait_ge(guess_ready[r], 1)
            order.after(e.tensor_scalar(ms[r][:, :], ms[r][:, :], EPS, None, ALU.add))
            order.after(e.tensor_tensor(tmp, y, y, ALU.mult))
            order.after(e.tensor_tensor(tmp, tmp, ms[r][:, :], ALU.mult))
            order.after(e.tensor_scalar(tmp, tmp, -0.5, 1.5, ALU.mult, ALU.add))
            if square is None:
                e.tensor_tensor(y, y, tmp, ALU.mult).then_inc(rstd_ready[r], 1)
            else:
                order.after(e.tensor_tensor(y, y, tmp, ALU.mult))
                e.tensor_tensor(square, y, y, ALU.mult).then_inc(rstd_ready[r], 1)

        def is_static(g):
            return isinstance(g, int) and g < PAIRS["S"]

        def turn_bank(g, p):
            return bank[4] if is_static(g) else bank[p]

        def score_bank(g, p, c):
            return bank[5 + c] if is_static(g) else bank[2 + 2 * p + c]

        def out_bank(g, p):
            return bank[7] if is_static(g) else bank[6 + p]

        def before(g):
            return g if is_static(g) else plus(g, -1)

        def plus(g, n):
            return g + n

        def stage_wait_pool(e, g):
            wait_from(e, qk_turned, plus(g, -1))

        def turn_qk_pe(e, g, p):
            e.wait_ge(staged, plus(g, 1))
            wait_from(e, qk_ready, before(g))
            for j, src in enumerate((qs[p], ks[p])):
                for t in range(T):
                    last = e.transpose(turn_bank(g, p)[:, (2 * j + t) * P:(2 * j + t + 1) * P], src[:, t * P:(t + 1) * P], ident[:, :])
            last.then_inc(qk_turned, 1)

        def turn_qk_mla_pe(e, g, p):
            e.wait_ge(staged, plus(g, 1))
            e.wait_ge(qk_ready, plus(g, 0))
            for j, src in enumerate((qs_mla[p], ks_mla[p])):
                for m in range(4):
                    last = e.transpose(bank[j][0:96, m * P:(m + 1) * P], src[:, m * 96:(m + 1) * 96], ident[:, :])
            last.then_inc(qk_turned, 1)

        def qk_evac_act(e, g, p, scale):
            e.wait_ge(qk_turned, plus(g, 1))
            wait_from(e, scores_done, plus(g, -1))
            e.activation(qkT[p][:, 0:256], turn_bank(g, p)[:, 0:256], ACT.Copy, scale=scale)
            e.activation(qkT[p][:, 256:512], turn_bank(g, p)[:, 256:512], ACT.Copy).then_inc(qk_ready, 1)

        def qk_evac_mla_act(e, g, p):
            e.wait_ge(qk_turned, plus(g, 1))
            wait_from(e, scores_done, plus(g, -1))
            e.activation(qkT[p][0:96, 0:512], bank[0][0:96, :], ACT.Copy)
            e.activation(qkT[p][0:96, 512:1024], bank[1][0:96, :], ACT.Copy).then_inc(qk_ready, 1)

        def scores_pe(e, g, p, mla=False):
            e.wait_ge(qk_ready, plus(g, 1))
            wait_from(e, pt_dve, before(g))
            wait_from(e, pt_act, before(g) - PAIRS["B"])
            for c in range(2):
                dst = score_bank(g, p, c)
                if mla:
                    q, k = qkT[p][0:96, c * 256:(c + 1) * 256], qkT[p][0:96, 512 + c * 256:512 + (c + 1) * 256]
                else:
                    q, k = qkT[p][c * HD:(c + 1) * HD, 0:256], qkT[p][c * HD:(c + 1) * HD, 256:512]
                e.matmul(dst[:, 0:256], q[:, P:2 * P], k, start=True, stop=True)
                last = e.matmul(dst[:, 256:384], q[:, 0:P], k[:, 0:P], start=True, stop=True)
            last.then_inc(scores_done, 1)

        def row_max_dve(e, g, p, biases, scale=1.0, sink=None):
            e.wait_ge(scores_done, plus(g, 1))
            wait_from(e, probs_turned, plus(g, -1))
            if not isinstance(g, int):
                e.memset(wait_carrier[:, :], 0.0)
            for c in range(2):
                b1, b0 = biases[c]
                s = score_bank(g, p, c)
                for t, cols, b in ((1, slice(0, 256), b1), (0, slice(256, 384), b0)):
                    last = e.tensor_tensor_reduce(sc[p][c][:, cols], s[:, cols], b, 1.0, MASKED, ALU.add, ALU.max,
                                                  row_max[p][:, 2 * c + t:2 * c + t + 1])
            last.then_inc(raw_max_done, 1)
            e.wait_ge(raw_max_done, plus(g, 1))
            if sink is not None:
                e.scalar_tensor_tensor(out=neg_max[p][:, :].rearrange("p (c t) -> p c t", c=2), in0=row_max[p][:, :].rearrange("p (c t) -> p c t", c=2), scalar=1.0, in1=sink, op0=ALU.mult, op1=ALU.max)\
                    .then_inc(sink_max, 1)
                e.wait_ge(sink_max, 2 * (g - PAIRS["C"]) + 1)
                e.tensor_scalar(neg_max[p][:, :], neg_max[p][:, :], -scale, None, ALU.mult).then_inc(sink_max, 1)
                e.wait_ge(sink_max, 2 * (g - PAIRS["C"]) + 2)
                e.tensor_tensor(sink_e[p][:, :].rearrange("p (c t) -> p c t", c=2), neg_max[p][:, :].rearrange("p (c t) -> p c t", c=2),
                                sink, ALU.add).then_inc(max_done, 1)
            else:
                e.tensor_scalar(neg_max[p][:, :], row_max[p][:, :], -scale, None, ALU.mult).then_inc(max_done, 1)

        def probs_act(e, g, p, scale=1.0, sink=False):
            e.wait_ge(max_done, plus(g, 1))
            if isinstance(g, int) and g < PAIRS["B"] + 2:
                wait_from(e, diff_done, g - 1)
            else:
                e.wait_ge(inv_done, plus(g, -1) - PAIRS["B"])
            for c in range(2):
                for t, cols in ((1, slice(0, 256)), (0, slice(256, 384))):
                    j = 2 * c + t
                    last = e.activation(sc[p][c][:, cols], sc[p][c][:, cols], ACT.Exp, bias=neg_max[p][:, j:j + 1],
                                        scale=scale, accum_out=row_sum[p][:, j:j + 1])
            if sink:
                last = e.activation(sink_e[p][:, :], sink_e[p][:, :], ACT.Exp)
            last.then_inc(probs_done, 1)

        def turn_probs_pe(e, g, p, ready, value, comps=2):
            e.wait_ge(ready, value)
            for c in range(comps):
                for m in range(3):
                    last = e.transpose(score_bank(g, p, c)[:, m * P:(m + 1) * P], sc[p][c][:, m * P:(m + 1) * P], ident[:, :])
            last.then_inc(probs_turned, 1)

        def pt_evac_dve(e, g, p):
            e.wait_ge(probs_turned, plus(g, 1))
            wait_from(e, attended, plus(g, -1))
            e.tensor_copy(pT[p][:, 0, :], score_bank(g, p, 0)[:, 0:384]).then_inc(pt_dve, 1)

        def pt_evac_act(e, g, p):
            e.wait_ge(probs_turned, plus(g, 1))
            wait_from(e, attended, plus(g, -1))
            e.activation(pT[p][:, 1, :], score_bank(g, p, 1)[:, 0:384], ACT.Copy).then_inc(pt_act, 1)

        def attend_pe(e, g, p, value, width=HD, comps=2):
            e.wait_ge(pt_dve, plus(g, 1))
            if comps == 2:
                e.wait_ge(pt_act, plus(g, 1) - PAIRS["B"])
            wait_from(e, heads_out, before(g))
            for c in range(comps):
                for t in range(T):
                    dst = out_bank(g, p)[:, (2 * c + t) * width:(2 * c + t + 1) * width]
                    if t == 0:
                        last = e.matmul(dst, pT[p][:, c, 256:384], value(c, 0), start=True, stop=True)
                    else:
                        e.matmul(dst, pT[p][:, c, 0:P], value(c, 0), start=True, stop=False)
                        last = e.matmul(dst, pT[p][:, c, P:2 * P], value(c, 1), start=False, stop=True)
            last.then_inc(attended, 1)

        def inv_sum_dve(e, g, p, sink=False):
            e.wait_ge(probs_done, plus(g, 1))
            wait_from(e, heads_out, plus(g, -1))
            if sink:
                e.tensor_tensor(row_sum[p][:, :], row_sum[p][:, :], sink_e[p][:, :], ALU.add).then_inc(sink_sum, 1)
                e.wait_ge(sink_sum, g - PAIRS["C"] + 1)
            e.reciprocal(inv_sum[p][:, :], row_sum[p][:, :]).then_inc(inv_done, 1)

        def heads_out_dve(e, g, p, dst):
            e.wait_ge(inv_done, plus(g, 1) - PAIRS["B"])
            e.wait_ge(attended, plus(g, 1))
            e.tensor_tensor(dst, out_bank(g, p)[:, 0:256].rearrange("p (c t d) -> p c t d", c=2, t=T),
                            inv_sum[p][:, :].rearrange("p (c t) -> p c t", c=2).unsqueeze(3).to_broadcast([P, 2, T, HD]),
                            ALU.mult).then_inc(heads_out, 1)

        sink_max, sink_sum = sem("sink_max"), sem("sink_sum")

        def staging(buf):
            return buf[:, 0:256].rearrange("p (t c d) -> p t c d", t=T, c=2)

        def heads2(v, c0, step):
            if step == HD:
                return v[:, :, bass.ds(c0, 2 * HD)].rearrange("p t (c d) -> p t c d", c=2)
            return v[:, :, bass.ds(c0, 2 * step)].rearrange("p t (c s) -> p t c s", c=2)[:, :, :, 0:HD]

        def bcast64(a):
            return a.unsqueeze(3).to_broadcast([P, T, 2, HD])

        def static_pair(kind, i):
            if kind in ("A", "B"):
                o = 0 if kind == "A" else 2048
                st = rstd[STATS[kind]][:, :].rearrange("p (t g) -> p t g", t=T)
                return (heads2(z_even, o + 128 * i, HD), st[:, :, 2 * i:2 * i + 2],
                        heads2(z_even, o + 512 + 128 * i, HD), st[:, :, 8 + 2 * i:10 + 2 * i])
            st = rstd[STATS[kind]][:, :].rearrange("p (t g) -> p t g", t=T)
            if kind == "C":
                return (heads2(z_odd, 64 * i, 256), st[:, :, i:i + 5:4], heads2(z_odd, 512, HD), st[:, :, 8:10])
            return (heads2(z_odd, 1280 + 128 * i, HD), st[:, :, 2 * i:2 * i + 2],
                    heads2(z_odd, 1792 + 128 * i, HD), st[:, :, 8 + 2 * i:10 + 2 * i])

        def static_biases(kind, i):
            if kind == "A":
                return [(bias_a[:, i, :], bias_a[:, i, P:])] * 2
            if kind == "B":
                return [(bias_b[:, 2 * i + c, 0:256], bias_b[:, 2 * i + c, 256:384]) for c in range(2)]
            if kind == "C":
                return [(bias_c[:, i + 4 * c, :], bias_c[:, i + 4 * c, P:]) for c in range(2)]
            return [(bias_d[:, 2 * i + c, :], bias_d[:, 2 * i + c, P:]) for c in range(2)]

        def static_value(kind, i):
            if kind == "A":
                return lambda c, t: z_even[:, t, 1024 + 128 * i:1152 + 128 * i]
            if kind == "B":
                return lambda c, t: z_even[:, t, 3072 + 128 * i + 64 * c:3136 + 128 * i + 64 * c]
            if kind == "C":
                return lambda c, t: z_odd[:, t, 640 + 64 * c:704 + 64 * c]
            return lambda c, t: z_odd[:, t, 2304 + 128 * i + 64 * c:2368 + 128 * i + 64 * c]

        def static_out(kind, i):
            if kind == "B":
                v = mix[:, :, 512 + 128 * i:640 + 128 * i].rearrange("p t (c d) -> p c t d", c=2)
            elif kind == "C":
                v = mix[:, :, 0:512].rearrange("p t (c s) -> p c t s", c=2)[:, :, :, 64 * i:64 * i + 64]
            else:
                v = mix[:, :, 512 + 128 * i:640 + 128 * i].rearrange("p t (c d) -> p c t d", c=2)
            return v

        def static_pairs(kinds):
            return [(k, i, PAIRS[k] + i) for k in kinds for i in range(4)]

        FIRST_FILL = {"AB": first["even_in"] + 4, "CD": first["odd_in"] + 3}
        SLOTS = {"AB": [(4, 2)] * 4 + [(3, 1)] * 3 + [(4, 0)], "CD": [(3, 1)] * 7 + [(4, 0)]}
        SPLITS = {"AB": {0: 1, 2: 2, 3: 3, 4: 4, 6: 5}, "CD": {0: 1, 2: 2, 4: 3, 6: 4}}

        def slot_pieces(kinds, n, which):
            at = sum(sum(s) for s in SLOTS[kinds][:n]) + (SLOTS[kinds][n][0] if which else 0)
            end, pieces = at + SLOTS[kinds][n][which], []
            while at < end:
                stop = min(end, (at // 8 + 1) * 8)
                pieces.append((FIRST_FILL[kinds] + at // 8, at % 8, at % 8 + stop - at))
                at = stop
            return pieces

        def slot_ends(kinds, n, which):
            return [u for u, _, e1 in slot_pieces(kinds, n, which) if e1 == 8]

        def sparse_value(i):
            return lambda c, t: z_dsa[:, t, bass.ds((i >> 2) * HD + (1280 + 128 * c), HD)]

        def latent_value(i):
            return lambda c, t: kv_full[:, t, bass.ds(i * 256 + (128 * c + 64), HD)]

        block = ctx.enter_context(nc.Block())

        @block.sync
        def _(sp):
            sp.dma_start(x[:, :, :], x_in.rearrange("(t p) n -> p t n", p=P)).then_inc(x_loaded, 16)
            sp.dma_start(mix[0:GAIN_ROWS, 0, 0:P], gain_rows).then_inc(rows_loaded, 16)
            sp.dma_start(rowp[:, :], row_params.partition_broadcast(P)).then_inc(params_loaded, 16)
            load_unit(sp, 0)
            load_unit(sp, 1)
            sp.dma_start(pos_i[:, :], positions).then_inc(pos_loaded, 16)

            def stream(u0, count, trips=0, per=2):
                if trips:
                    with sp.Fori(0, trips) as i:
                        for j in range(per):
                            load_unit(sp, u0 + j, i, per)
                else:
                    for j in range(count):
                        load_unit(sp, u0 + j)

            stream(2, first["even_out"] + 2 - 2)
            if upto >= 2:
                stream(first["odd_in"], 2)
                sp.wait_ge(max_done, PAIRS["B"] + 4)
                sp.dma_start(tab[:, 2048:4096], rel_band.rearrange("p h j -> p (h j)")).then_inc(band_loaded, 16)
                stream(first["odd_in"] + 2, 8)
            elif upto == 1:
                stream(first["odd_in"], 1)
            if upto >= 3:
                stream(first["dsa_in"] + 1, 7)
            for m, done in ((0, 4), (1, 6)):
                if upto < done:
                    break
                u = first[f"mlp{m}"]
                stream(u + 1, 12, trips=3, per=4)
                stream(u + 13, 3)
                if m == 0:
                    stream(u + 16, 1)
                    if upto >= 5:
                        stream(first["mla_in"], first["mlp1"] + 1 - first["mla_in"])
            if upto >= 6:
                sp.wait_ge(heads_out, PAIRS["L"] + 8)
                sp.dma_start(g_final[:, :], final_gain.partition_broadcast(P)).then_inc(final_loaded, 16)
                for t in range(T):
                    sp.wait_ge(final_done, t + 1)
                    sp.dma_start(out[t * P:(t + 1) * P, :], mix[:, t, :]).then_inc(stored, 16)
            else:
                sp.wait_ge(*X_READY[{1: "odd", 2: "dsa", 3: "mlp0", 4: "mla", 5: "mlp1"}[upto]])
                for t in range(T):
                    sp.dma_start(out[t * P:(t + 1) * P, :], x[:, t, :]).then_inc(stored, 16)
            sp.wait_ge(stored, 32)

        @block.gpsimd
        def _(pool):
            order = Order(pool, pool_order)
            order.after(pool.memset(ident[:, :], 0.0))
            pool.affine_select(out=ident[:, :], in_=ident[:, :], compare_op=ALU.not_equal, fill=1.0, base=0,
                               pattern=[[-1, P]], channel_multiplier=1).then_inc(consts, 1)
            pool.memset(eps[:, :], EPS).then_inc(consts, 1)
            order.after(pool.memset(upper, 1.0))
            for t in range(T):
                order.after(pool.affine_select(out=upper[:, t, :], in_=upper[:, t, :], compare_op=ALU.is_ge, fill=0.0,
                                               base=-P * t, pattern=[[1, SEQ]], channel_multiplier=-1))
            order.after(pool.memset(causal, 0.0))
            order.after(pool.affine_select(out=causal, in_=causal, compare_op=ALU.is_ge, fill=MASKED, base=P,
                                           pattern=[[-1, SEQ]], channel_multiplier=1))
            order.after(pool.memset(chunked[:, :], 0.0))
            order.after(pool.memset(chunked[0:64, 192:256], MASKED))
            nd = sc[0][0][:, 0:256]
            order.after(pool.iota(nd, pattern=[[-1, SEQ]], base=P, channel_multiplier=1, allow_small_or_imprecise_dtypes=True))
            nd2 = sc[0][1][:, 0:256]
            order.after(pool.tensor_scalar(nd2, nd, 0.0, None, ALU.max))
            order.after(pool.tensor_scalar(nd, nd, 0.0, None, ALU.min))
            order.after(pool.tensor_tensor(nd, nd, nd2, ALU.subtract))
            order.after(pool.memset(nd[0:64, 192:256], MASKED))
            for h in range(4):
                pool.tensor_scalar(bias_a[:, h, :], nd, 2.0 ** (-8.0 * (h + 1) / 4), None, ALU.mult).then_inc(even_tables, 1)
            pool.memset(g_mix[:, 4:KC], 0.5).then_inc(consts, 1)

            def stage_static(kinds):
                for kind, i, g in static_pairs(kinds):
                    q, rq, k, rk = static_pair(kind, i)
                    if i == 0:
                        pool.wait_ge(rstd_ready[STATS[kind]], 1)
                    stage_wait_pool(pool, g)
                    pool.tensor_tensor(staging(qs[g % 2]), q, bcast64(rq), ALU.mult)
                    pool.tensor_tensor(staging(ks[g % 2]), k, bcast64(rk), ALU.mult).then_inc(staged, 1)

            def gate_first(v, gate_unit, g0, heads_done, count, gain=None):
                th, gt = v[:, :, 0:512], v[:, :, g0:g0 + 512]
                pool.wait_ge(tanh_first, count)
                pool.wait_ge(evac_dve, dve_after[gate_unit])
                order.after(pool.tensor_scalar(th, th, 1.0, None, ALU.add))
                order.after(pool.tensor_tensor(th, th, gt, ALU.mult))
                if gain is not None:
                    heads = th.rearrange("p t (h d) -> p t h d", h=4)
                    pool.wait_ge(rstd_ready[gain], 1)
                    order.after(pool.tensor_tensor(heads, heads, rstd[gain][:, :].rearrange("p (t h) -> p t h", t=T)
                                                   .unsqueeze(3).to_broadcast([P, T, 4, P]), ALU.mult))
                pool.wait_ge(heads_out, heads_done)
                pool.tensor_tensor(mix[:, :, 0:512], mix[:, :, 0:512], th, ALU.mult).then_inc(first_gated, 1)

            stage_static("AB")
            gate_first(z_even, first["even_in"] + 7, 1536, PAIRS["A"] + 4, 1, gain=2)
            if upto < 2:
                return
            pool.wait_ge(max_done, PAIRS["B"] + 4)
            pool.wait_ge(heads_out, PAIRS["B"] + 4)
            order.after(pool.iota(nd, pattern=[[-1, SEQ]], base=P, channel_multiplier=1, allow_small_or_imprecise_dtypes=True))
            order.after(pool.tensor_scalar(nd2, nd, 0.0, None, ALU.max))
            order.after(pool.tensor_scalar(nd, nd, 0.0, None, ALU.min))
            order.after(pool.tensor_tensor(nd, nd, nd2, ALU.subtract))
            order.after(pool.memset(nd[0:64, 192:256], MASKED))
            order.after(pool.memset(nd[64:128, 0:64], MASKED))
            for h in range(8):
                pool.tensor_scalar(bias_c[:, h, :], nd, 2.0 ** -(h + 1), None, ALU.mult).then_inc(tables, 1)
            pool.wait_ge(band_loaded, 16)
            pool.tensor_tensor(bias_d[:, :, :], bias_d[:, :, :], chunked[:, :].unsqueeze(1).to_broadcast([P, 8, SEQ]),
                               ALU.add).then_inc(tables, 1)
            stage_static("CD")
            gate_first(z_odd, first["odd_in"] + 5, 768, PAIRS["C"] + 4, 2)
            if upto < 3:
                return
            pool.wait_ge(roped, 1)
            pool.wait_ge(qk_turned, PAIRS["S"])
            pool.tensor_copy(staging(ks[0]), z_dsa[:, :, 2048:2112].unsqueeze(2).to_broadcast([P, T, 2, HD])).then_inc(ki_staged, 1)
            pool.wait_ge(index_turned, 1)
            pool.wait_ge(roped, 2)

            def stage_sparse(g, p, i):
                stage_wait_pool(pool, g)
                pool.tensor_copy(staging(qs[p]), heads2(z_dsa, i * HD, 512))
                pool.tensor_copy(staging(ks[p]), heads2(z_dsa, (i >> 2) * HD + 1024, P)).then_inc(staged, 1)

            with pool.Fori(0, 4) as i:
                for j in range(2):
                    stage_sparse(i * 2 + (PAIRS["S"] + j), j, i * 2 + j)
            if upto < 5:
                return
            pool.wait_ge(mla_roped, 1)
            for p in range(2):
                kbuf = ks_mla[p].rearrange("p (c t d) -> p c t d", c=2, t=T)
                for c in range(2):
                    ins = pool.tensor_copy(kbuf[:, c, :, HD:96], z_mla[:, :, 640:672])
            ins.then_inc(kr_staged, 1)

            pool.wait_ge(evac_act, act_after[first["kv_up"]])
            pool.wait_ge(evac_dve, dve_after[first["kv_up"]])

            def stage_latent(g, p, i):
                stage_wait_pool(pool, g)
                for buf, full, step, n in ((qs_mla[p], q_full, 96, 96), (ks_mla[p], kv_full, 128, 64)):
                    dst = buf.rearrange("p (c t d) -> p c t d", c=2, t=T)[:, :, :, 0:n]
                    src = full[:, :, bass.ds(i * (2 * step), 2 * step)].rearrange("p t (c s) -> p c t s", c=2)[:, :, :, 0:n]
                    last = pool.tensor_copy(dst, src)
                last.then_inc(staged, 1)

            with pool.Fori(0, 4) as i:
                for j in range(2):
                    stage_latent(i * 2 + (PAIRS["L"] + j), j, i * 2 + j)

        @block.tensor
        def _(pe):
            pe.wait_ge(consts, 1)
            pe.wait_ge(rows_loaded, 16)
            pe.transpose(bank[0][:, 0:GAIN_ROWS], mix[0:GAIN_ROWS, 0, 0:P], ident[0:GAIN_ROWS, 0:GAIN_ROWS]).then_inc(gains_turned, 1)
            pe.wait_ge(x_loaded, 16)
            turn_pe(pe, "even", x)

            def project(u0, count, trips=0, chunk0=0, fresh=None):
                if trips:
                    with pe.Fori(0, trips) as i:
                        for j in range(2):
                            unit_pe(pe, u0 + j, i, 2, chunk0)
                else:
                    for j in range(count):
                        unit_pe(pe, u0 + j, chunk0=chunk0, fresh=None if j else fresh)

            def turn_x(e, name):
                s, value = X_READY[name]
                if s is evac_dve:
                    e.wait_ge(s, value - 1)
                    turn_pe(e, name, x, 0, 4)
                    e.wait_ge(s, value)
                    turn_pe(e, name, x, 4, 8)
                else:
                    e.wait_ge(s, value)
                    turn_pe(e, name, x)

            def static_attention(kinds):
                pairs = static_pairs(kinds)

                def turn_probs(kind, i, g):
                    if kind == "A":
                        turn_probs_pe(pe, g, g % 2, diff_done, g + 1, comps=1)
                    else:
                        turn_probs_pe(pe, g, g % 2, probs_done, g + 1)

                def attend(kind, i, g):
                    if kind == "A":
                        attend_pe(pe, g, g % 2, static_value(kind, i), width=P, comps=1)
                    else:
                        attend_pe(pe, g, g % 2, static_value(kind, i))

                def fill(n, which):
                    for u, e0, e1 in slot_pieces(kinds, n, which):
                        unit_eighths_pe(pe, u, e0, e1)

                turn_qk_pe(pe, pairs[0][2], 0)
                for n, (kind, i, g) in enumerate(pairs):
                    scores_pe(pe, g, g % 2)
                    if n:
                        attend(*pairs[n - 1])
                    fill(n, 0)
                    if n + 1 < len(pairs):
                        turn_qk_pe(pe, g + 1, (g + 1) % 2)
                    turn_probs(kind, i, g)
                    fill(n, 1)

                name, g = {"AB": "even_mix", "CD": "odd_mix"}[kinds], pairs[-1][2]
                layer = 1 if kinds == "AB" else 2
                pe.wait_ge(first_gated, layer)
                turn_pe(pe, name, mix, 0, 2)
                attend(*pairs[-1])
                turn_pe(pe, name, mix, 2, 4)
                pe.wait_ge(mix_ready, 2 * layer - 1)
                turn_pe(pe, name, mix, 4, 6)
                pe.wait_ge(mix_ready, 2 * layer)
                turn_pe(pe, name, mix, 6, 8)

            unit_pe(pe, 0, fresh="even")
            unit_pe(pe, 1)
            pe.wait_ge(forget_ready, 1)
            pe.wait_ge(even_tables, 4)
            for t in range(T):
                for s in range(t + 1):
                    last = pe.matmul(bank[4][:, 8 * t:8 * t + 8], upper[:, s, t * P:(t + 1) * P], logf[:, 3, s, :],
                                     start=(s == 0), stop=(s == t))
            last.then_inc(cum_done, 1)
            unit_pe(pe, 2)
            pe.wait_ge(cum_ready, 1)
            for h in range(8):
                for s in range(T):
                    last = pe.matmul(bank[4 + h // 2][:, (h % 2) * SEQ:(h % 2 + 1) * SEQ], qkT[s][:, h * P:(h + 1) * P],
                                     upper[:, s, :], start=(s == 0), stop=(s == 1))
            last.then_inc(cum_done, 1)
            unit_pe(pe, 3)
            pe.wait_ge(bias_ready, 1)
            static_attention("AB")
            unit_pe(pe, first["even_out"], fresh="even_mix")
            unit_pe(pe, first["even_out"] + 1)
            if upto < 2:
                return
            turn_x(pe, "odd")
            unit_pe(pe, first["odd_in"], fresh="odd")
            unit_pe(pe, first["odd_in"] + 1)
            unit_pe(pe, first["odd_in"] + 2)
            static_attention("CD")
            unit_pe(pe, first["odd_out"], fresh="odd_mix")
            unit_pe(pe, first["odd_out"] + 1)
            if upto < 3:
                return
            turn_x(pe, "dsa")
            u = first["dsa_in"]
            project(u, 1, fresh="dsa")
            project(u + 1, 1)
            unit_eighths_pe(pe, u + 2, 0, 4)
            pe.wait_ge(roped, 1)
            for i in range(4):
                for t in range(T):
                    pe.transpose(bank[4 + i // 2][:, (i % 2) * SEQ + t * P:(i % 2) * SEQ + (t + 1) * P],
                                 z_dsa[:, t, 1536 + P * i:1536 + P * (i + 1)], ident[:, :])
            pe.wait_ge(ki_staged, 1)
            for t in range(T):
                last = pe.transpose(bank[6][:, t * P:(t + 1) * P], ks[0][:, t * P:(t + 1) * P], ident[:, :])
            last.then_inc(index_turned, 1)
            unit_eighths_pe(pe, u + 2, 4, 8)

            def logits(heads):
                for h in heads:
                    if h >= 4:
                        pe.wait_ge(logits_relu, h - 3)
                    q = qiT[(h % 2) * HD:(h % 2 + 1) * HD, h // 2, :]
                    k = kiT[(h % 2) * HD:(h % 2 + 1) * HD, :]
                    pe.matmul(bank[4 + h % 4][:, 0:256], q[:, P:2 * P], k, start=True, stop=True)
                    pe.matmul(bank[4 + h % 4][:, 256:384], q[:, 0:P], k[:, 0:P], start=True, stop=True).then_inc(logits_done, 1)

            pe.wait_ge(index_ready, 1)
            logits(range(4))
            unit_eighths_pe(pe, u + 3, 0, 3)
            logits(range(4, 8))
            unit_eighths_pe(pe, u + 3, 3, 8)
            project(u + 4, 1)
            pe.wait_ge(logits_relu, 8)

            def looped_attention(first_pair, value, mla):
                turn = turn_qk_mla_pe if mla else turn_qk_pe
                turn(pe, first_pair, 0)
                turn(pe, first_pair + 1, 1)
                scores_pe(pe, first_pair, 0, mla)

                def step(g, p, value_before, scores=True, turns=True):
                    if scores:
                        scores_pe(pe, plus(g, 1), 1 - p, mla)
                    turn_probs_pe(pe, g, p, probs_done, plus(g, 1))
                    if turns:
                        turn(pe, plus(g, 2), p)
                    if value_before is not None:
                        attend_pe(pe, plus(g, -1), 1 - p, value_before)

                step(first_pair, 0, None)
                step(first_pair + 1, 1, value(0))
                with pe.Fori(0, 2) as i:
                    for j in range(2):
                        step(i * 2 + (first_pair + 2 + j), j, value(i * 2 + (1 + j)))
                step(first_pair + 6, 0, value(5), turns=False)
                step(first_pair + 7, 1, value(6), scores=False, turns=False)
                attend_pe(pe, first_pair + 7, 1, value(7))

            looped_attention(PAIRS["S"], sparse_value, False)
            pe.wait_ge(heads_out, PAIRS["S"] + 8)
            turn_pe(pe, "dsa_mix", mix)
            project(first["dsa_out"], 2, fresh="dsa_mix")
            if upto < 4:
                return

            def mlp(m):
                name, u = f"mlp{m}", first[f"mlp{m}"]
                turn_x(pe, name)

                def up(v, b, i=None):
                    slot = v % 2
                    hi = w_hi[slot][:, :].rearrange("p (k n) -> p k n", k=KC)
                    lo = w_lo[slot][:, :].rearrange("p (k n) -> p k n", k=KC)
                    pe.wait_ge(lo_split, v + 1 if i is None else i * 4 + (v + 1))
                    relus = 2 * FF_BLOCKS * m + 2 * (b - 1)
                    if i is not None or b >= 2:
                        pe.wait_ge(relu_done, relus if i is None else i * 4 + relus)
                    for f in range(4):
                        dst = bank[2 * (b % 2) + f // 2][:, (f % 2) * SEQ:(f % 2 + 1) * SEQ]
                        for k in range(KC):
                            if b == 0 and f == 0:
                                pe.wait_ge(lo_turned, turn_base[name] + k // 2 + 1)
                            wh, wl = hi[:, k, f * P:(f + 1) * P], lo[:, k, f * P:(f + 1) * P]
                            pe.matmul(dst, wh, h_hi[:, k, :], start=(k == 0), stop=False)
                            pe.matmul(dst, wh, h_lo[:, k, :], start=False, stop=False)
                            last = pe.matmul(dst, wl, h_hi[:, k, :], start=False, stop=(k == KC - 1))
                        if f % 2:
                            last.then_inc(mm_done, 1)

                def down(v, b, i=None, begins=False, ends=False):
                    slot = v % 2
                    hi = w_hi[slot][:, :].rearrange("p (k n) -> p k n", k=4)
                    lo = w_lo[slot][:, :].rearrange("p (k n) -> p k n", k=4)
                    pe.wait_ge(lo_split, v + 1 if i is None else i * 4 + (v + 1))
                    blocks_done = 2 * FF_BLOCKS * m + 2 * (b + 1)
                    pe.wait_ge(u_lo_done, blocks_done if i is None else i * 4 + blocks_done)
                    for c in range(4):
                        for t in range(T):
                            uh, ul = u_hi[b % 2][:, c, t * P:(t + 1) * P], u_lo[b % 2][:, c, t * P:(t + 1) * P]
                            for half in range(2):
                                dst = bank[4 + 2 * t + half][:, :]
                                cols = slice(half * BLOCK, (half + 1) * BLOCK)
                                a, z_ = begins and c == 0, ends and c == 3
                                pe.matmul(dst, uh, hi[:, c, cols], start=a, stop=False, skip_group_check=True)
                                pe.matmul(dst, uh, lo[:, c, cols], start=False, stop=False, skip_group_check=True)
                                last = pe.matmul(dst, ul, hi[:, c, cols], start=False, stop=z_, skip_group_check=True)
                    last.then_inc(mm_done, 1)

                up(u, 0)
                up(u + 1, 1)
                down(u + 2, 0, begins=True)
                up(u + 3, 2)
                down(u + 4, 1)
                with pe.Fori(0, 2) as i:
                    up(u + 5, 3, i)
                    down(u + 6, 2, i)
                    up(u + 7, 4, i)
                    down(u + 8, 3, i)
                up(u + 13, 7)
                down(u + 14, 6)
                down(u + 15, 7, ends=True)

            mlp(0)
            if upto < 5:
                return
            turn_x(pe, "mla")
            project(first["mla_in_rest"], 2, fresh="mla")
            u = first["q_up"]
            pe.wait_ge(evac_act, act_after[u - 1])
            pe.wait_ge(evac_dve, dve_after[u - 1])
            turn_pe(pe, "latent", z_mla)
            project(u, 2, fresh="latent")
            wait_turned(pe, "latent")
            project(first["kv_up"], 1, chunk0=Q_LORA // P)
            pe.wait_ge(kr_staged, 1)
            looped_attention(PAIRS["L"], latent_value, True)
            pe.wait_ge(heads_out, PAIRS["L"] + 8)
            turn_pe(pe, "mla_mix", mix)
            project(first["mla_out"], 2, fresh="mla_mix")
            if upto < 6:
                return
            mlp(1)

        @block.scalar
        def _(act):
            order = Order(act, act_order)
            act.wait_ge(pos_loaded, 16)
            act.wait_ge(trig_in, 1)
            act.activation(sine[:, :, :], angle[:, :, :], ACT.Sin)
            act.activation(cosine[:, :, :], turns[:, :, :], ACT.Sin).then_inc(trig_ready, 1)
            act.wait_ge(lam_in, 1)
            act.activation(lam_dot[:, :], lam_dot[:, :], ACT.Exp).then_inc(lam_exp, 1)
            split_hi(act, 0)
            act.wait_ge(gains_ready, 1)
            turn_act(act, "even")
            act.wait_ge(x_loaded, 16)
            act.wait_ge(gains_turned, 1)
            x_squares_act(act, 0)
            act.wait_ge(consts, 2)
            guess_act(act, order, 0)

            def project(u0, count, dst, scale, trips=0):
                if trips:
                    with act.Fori(0, trips) as i:
                        for j in range(2):
                            split_hi(act, u0 + j + 1, i, 2)
                            unit_z_act(act, u0 + j, dst, scale, i, 2)
                else:
                    for j in range(count):
                        split_hi(act, u0 + j + 1)
                        unit_z_act(act, u0 + j, dst, scale)

            def project_x(u0):
                for j in range(2):
                    split_hi(act, u0 + j + 1)

            def first_unit(name, r, u, dst):
                turn_act(act, name)
                split_hi(act, u + 1)
                act.wait_ge(*X_READY[name])
                x_squares_act(act, r)
                guess_act(act, order, r)
                act.wait_ge(rstd_ready[r], 1)
                unit_z_act(act, u, dst, rstd[r][:, 0:1])

            def static_attention(kinds, scales):
                pairs = static_pairs(kinds)

                dst, r = (z_even, 0) if kinds == "AB" else (z_odd, 3)
                qk_evac_act(act, pairs[0][2], 0, scales(pairs[0][0]))
                for n, (kind, i, g) in enumerate(pairs):
                    if n in SPLITS[kinds]:
                        split_hi(act, FIRST_FILL[kinds] + SPLITS[kinds][n])
                    probs_act(act, g, g % 2, sink=kind == "C")
                    for u in slot_ends(kinds, n, 0):
                        unit_z_act(act, u, dst, rstd[r][:, 0:1])
                    if n == len(pairs) - 1:
                        tanh_act(kinds, 1)
                    if n + 1 < len(pairs):
                        qk_evac_act(act, g + 1, (g + 1) % 2, scales(pairs[n + 1][0]))
                    if kind != "A":
                        pt_evac_act(act, g, g % 2)
                    for u in slot_ends(kinds, n, 1):
                        unit_z_act(act, u, dst, rstd[r][:, 0:1])
                    beside_act(kinds, n)

            def squares_act(v, c0, n, unit, at):
                act.wait_ge(evac_act, act_after[unit])
                act.wait_ge(evac_dve, dve_after[unit])
                act.activation(mix[:, :, at:at + n], v[:, :, c0:c0 + n], ACT.Square, scale=HD ** -0.5).then_inc(squares_ready, 1)

            def tanh_act(kinds, half):
                v, spots = (z_even, ((1536, 0), (3584, 2048))) if kinds == "AB" else (z_odd, ((768, 0), (2816, 1280)))
                unit = FIRST_FILL[kinds] + (3, 4)[half] - (kinds == "CD")
                src, to = spots[half]
                act.wait_ge(evac_act, act_after[unit])
                act.wait_ge(evac_dve, dve_after[unit])
                act.activation(v[:, :, to:to + 512], v[:, :, src:src + 512], ACT.Tanh, scale=0.5)\
                    .then_inc((tanh_first, tanh_second)[half], 1)

            def beside_act(kinds, n):
                if kinds == "AB":
                    if n == 1:
                        squares_act(z_even, 2048, 512, FIRST_FILL[kinds], 512)
                    if n == 2:
                        act.wait_ge(squares_read, 1)
                        squares_act(z_even, 2560, 512, FIRST_FILL[kinds] + 1, 512)
                        guess_act(act, order, 11)
                    if n == 4:
                        act.wait_ge(heads_out, PAIRS["A"] + 4)
                        act.activation(z_even[:, :, 512:1024], mix[:, :, 0:512], ACT.Square, scale=P ** -0.5).then_inc(squares_ready, 1)
                        guess_act(act, order, 2)
                if kinds == "CD":
                    if n == 0:
                        squares_act(z_odd, 1280, 512, FIRST_FILL[kinds] - 1, 512)
                    if n == 1:
                        act.wait_ge(squares_read, 2)
                        squares_act(z_odd, 1792, 512, FIRST_FILL[kinds], 512)
                        guess_act(act, order, 12)
                if n == 5:
                    tanh_act(kinds, 0)

            act.wait_ge(rstd_ready[0], 1)
            project(0, 1, z_even, rstd[0][:, 0:1])
            act.wait_ge(forget_in, 1)
            order.after(act.activation(logf[:, 2, :, :], logf[:, 1, :, :], ACT.Exp))
            act.activation(logf[:, 2, :, :], logf[:, 2, :, :], ACT.Ln, bias=1.0).then_inc(forget_log, 1)
            project(1, 1, z_even, rstd[0][:, 0:1])
            squares_act(z_even, 0, 512, 1, 0)
            project(2, 1, z_even, rstd[0][:, 0:1])
            squares_act(z_even, 512, 512, 2, 512)
            guess_act(act, order, 1)
            project(3, 1, z_even, rstd[0][:, 0:1])
            act.wait_ge(gains_ready, 2)
            act.wait_ge(consts, 3)
            static_attention("AB", lambda kind: g_qk[:, "ABCD".index(kind):"ABCD".index(kind) + 1])
            turn_act(act, "even_mix")
            project_x(first["even_out"])
            if upto < 2:
                return
            first_unit("odd", 3, first["odd_in"], z_odd)
            project(first["odd_in"] + 1, 1, z_odd, rstd[3][:, 0:1])
            squares_act(z_odd, 0, 640, first["odd_in"] + 1, 0)
            guess_act(act, order, 4)
            project(first["odd_in"] + 2, 1, z_odd, rstd[3][:, 0:1])
            static_attention("CD", lambda kind: g_qk[:, "ABCD".index(kind):"ABCD".index(kind) + 1])
            turn_act(act, "odd_mix")
            project_x(first["odd_out"])
            if upto < 3:
                return
            u = first["dsa_in"]
            first_unit("dsa", 5, u, z_dsa)
            project(u + 1, 1, z_dsa, rstd[5][:, 0:1])
            act.wait_ge(index_turned, 1)
            act.activation(qiT[:, 0:2, :], bank[4][:, :].rearrange("p (i q) -> p i q", i=2), ACT.Copy)
            act.activation(qiT[:, 2:4, :], bank[5][:, :].rearrange("p (i q) -> p i q", i=2), ACT.Copy)
            act.activation(kiT, bank[6][:, 0:256], ACT.Copy).then_inc(index_ready, 1)

            def logits(heads):
                for h in heads:
                    act.wait_ge(logits_done, h + 1)
                    if h >= 2:
                        act.wait_ge(logits_added, h - 1)
                    act.activation(rl[:, h % 2, :], bank[4 + h % 4][:, 0:384], ACT.Relu).then_inc(logits_relu, 1)

            split_hi(act, u + 3)
            unit_z_act(act, u + 2, z_dsa, rstd[5][:, 0:1])
            logits(range(4))
            split_hi(act, u + 4)
            logits(range(4, 8))
            unit_z_act(act, u + 3, z_dsa, rstd[5][:, 0:1])
            project(u + 4, 1, z_dsa, rstd[5][:, 0:1])

            def looped_attention(first_pair, mla, scale):
                evac = (lambda g, p: qk_evac_mla_act(act, g, p)) if mla else (lambda g, p: qk_evac_act(act, g, p, HD ** -0.5))
                evac(first_pair, 0)
                evac(first_pair + 1, 1)
                probs_act(act, first_pair, 0, scale)

                def step(g, p, turns=True, probs=True):
                    pt_evac_act(act, g, p)
                    if turns:
                        evac(plus(g, 2), p)
                    if probs:
                        probs_act(act, plus(g, 1), 1 - p, scale)

                with act.Fori(0, 3) as i:
                    for j in range(2):
                        step(i * 2 + (first_pair + j), j)
                step(first_pair + 6, 0, turns=False)
                step(first_pair + 7, 1, turns=False, probs=False)

            looped_attention(PAIRS["S"], False, 1.0)
            turn_act(act, "dsa_mix")
            project_x(first["dsa_out"])
            if upto < 4:
                return

            def mlp(m):
                r, u = (6, 9)[m], first[f"mlp{m}"]
                turn_act(act, f"mlp{m}")
                act.wait_ge(*X_READY[f"mlp{m}"])
                x_squares_act(act, r)
                guess_act(act, order, r)

                def up(v, b, i=None):
                    split_hi(act, v + 1, i, 4)
                    for j in range(2):
                        act.wait_ge(mm_done, mm_value(v, j, i, 4))
                        act.activation(relu[j][:, :], bank[2 * (b % 2) + j][:, :], ACT.Relu).then_inc(relu_done, 1)
                    for j in range(2):
                        done = 2 * FF_BLOCKS * m + 2 * b + j + 1
                        act.wait_ge(sq_done, done if i is None else i * 4 + done)
                        act.activation(u_hi[b % 2][:, 2 * j:2 * j + 2, :], sq[j][:, :].rearrange("p (f q) -> p f q", f=2),
                                       ACT.Copy).then_inc(u_hi_done, 1)

                up(u, 0)
                up(u + 1, 1)
                split_hi(act, u + 3)
                up(u + 3, 2)
                split_hi(act, u + 5)
                with act.Fori(0, 2) as i:
                    up(u + 5, 3, i)
                    split_hi(act, u + 7, i, 4)
                    up(u + 7, 4, i)
                    split_hi(act, u + 9, i, 4)
                up(u + 13, 7)
                split_hi(act, u + 15)
                split_hi(act, u + 16)

            mlp(0)
            if upto < 5:
                return
            first_unit("mla", 7, first["mla_in_rest"], z_mla)
            project(first["mla_in"], 1, z_mla, rstd[7][:, 0:1])
            act.wait_ge(evac_dve, dve_after[first["q_up"] - 1])
            act.wait_ge(evac_act, act_after[first["q_up"] - 1])
            turn_act(act, "latent")
            split_hi(act, first["q_up"] + 1)
            for t in range(T):
                act.activation(mix[:, t, 0:Q_LORA], z_mla[:, t, 0:Q_LORA], ACT.Square, scale=Q_LORA ** -0.5,
                               accum_out=ms[8][:, t:t + 1])
                ins = act.activation(mix[:, t, Q_LORA:640], z_mla[:, t, Q_LORA:640], ACT.Square, scale=KV_LORA ** -0.5,
                                     accum_out=ms[8][:, 2 + t:3 + t])
            ins.then_inc(ms_ready[8], 1)
            guess_act(act, order, 8)
            act.wait_ge(rstd_ready[8], 1)
            unit_z_act(act, first["q_up"], q_full, rstd[8][:, 0:1])
            project(first["q_up"] + 1, 1, q_full, rstd[8][:, 0:1])
            project(first["kv_up"], 1, kv_full, rstd[8][:, 2:3])
            looped_attention(PAIRS["L"], True, 96 ** -0.5)
            turn_act(act, "mla_mix")
            project_x(first["mla_out"])
            if upto < 6:
                return
            mlp(1)
            act.wait_ge(*X_READY["final"])
            x_squares_act(act, 10)
            guess_act(act, order, 10)

        @block.vector
        def _(dve):
            order = Order(dve, dve_order)
            dve.wait_ge(params_loaded, 16)
            dve.wait_ge(pos_loaded, 16)
            order.after(dve.tensor_copy(pos[:, :], pos_i[:, :]))
            for t in range(T):
                ins = dve.tensor_scalar(angle[:, t, :], rowp[:, R_FREQ:R_FREQ + 24], pos[:, t:t + 1], None, ALU.mult)
            order.after(ins)
            magic = 1.5 * 2.0 ** 23
            order.after(dve.tensor_scalar(turns[:, :, :], angle[:, :, :], 1.0 / (2.0 * math.pi), magic, ALU.mult, ALU.add))
            order.after(dve.tensor_scalar(turns[:, :, :], turns[:, :, :], magic, None, ALU.subtract))
            c1 = 6.28125
            c2 = float(np.float32(round((2 * math.pi - c1) * 2 ** 20) / 2 ** 20))
            c3 = float(np.float32(2 * math.pi - c1 - c2))
            for c in (c1, c2, c3):
                order.after(dve.scalar_tensor_tensor(out=angle[:, :, :], in0=turns[:, :, :], scalar=-c, in1=angle[:, :, :],
                                                     op0=ALU.mult, op1=ALU.add))
            pi_below = 3.1415925
            order.after(dve.tensor_scalar(angle[:, :, :], angle[:, :, :], pi_below, -pi_below, ALU.min, ALU.max))
            order.after(dve.scalar_tensor_tensor(out=turns[:, :, :], in0=angle[:, :, :], scalar=-1.0, in1=angle[:, :, :],
                                                 op0=ALU.mult, op1=ALU.min))
            dve.tensor_scalar(turns[:, :, :], turns[:, :, :], math.pi / 2, None, ALU.add).then_inc(trig_in, 1)
            for j in range(2):
                ins = dve.tensor_tensor_reduce(r_tmp[:, 0:HD], rowp[:, R_LAM + 128 * j:R_LAM + 128 * j + HD],
                                               rowp[:, R_LAM + 128 * j + HD:R_LAM + 128 * j + 2 * HD], 1.0, 0.0,
                                               ALU.mult, ALU.add, lam_dot[:, j:j + 1])
                if j == 0:
                    order.after(ins)
            ins.then_inc(lam_in, 1)
            dve.wait_ge(gains_turned, 1)
            dve.tensor_copy(gcols[:, :], bank[0][:, 0:GAIN_ROWS]).then_inc(gains_ready, 1)
            dve.wait_ge(gains_ready, 1)
            dve.tensor_scalar(g_mix[:, 0:4], gcols[:, G_SUB:G_SUB + 1].to_broadcast([P, 4]), 0.5 * (1.0 - LAM_INIT), None, ALU.mult)
            for j in range(4):
                ins = dve.tensor_scalar(g_qk[:, j:j + 1], gcols[:, G_HEAD + 2 * j:G_HEAD + 2 * j + 1],
                                        gcols[:, G_HEAD + 2 * j + 1:G_HEAD + 2 * j + 2], HD ** -0.5, ALU.mult, ALU.mult)
            ins.then_inc(gains_ready, 1)
            split_lo(dve, 0)
            turn_dve(dve, "even")
            dve.wait_ge(lam_exp, 1)
            order.after(dve.tensor_tensor(lam_diff[:, :], lam_dot[:, 1:2], lam_dot[:, 0:1], ALU.subtract))
            dve.memset(lam4[:, 0:2], 1.0)
            dve.tensor_scalar(lam4[:, 2:4], lam_diff[:, 0:1].to_broadcast([P, 2]), -LAM_INIT, None, ALU.add).then_inc(lam_ready, 1)
            newton_dve(dve, order, 0)

            def project(u0, count, dst, scale, trips=0):
                if trips:
                    with dve.Fori(0, trips) as i:
                        for j in range(2):
                            split_lo(dve, u0 + j + 1, i, 2)
                            unit_z_dve(dve, u0 + j, dst, scale, i, 2)
                else:
                    for j in range(count):
                        split_lo(dve, u0 + j + 1)
                        unit_z_dve(dve, u0 + j, dst, scale)

            def project_x(u0):
                for j in range(2):
                    split_lo(dve, u0 + j + 1)
                    unit_x_dve(dve, u0 + j)

            def first_unit(name, r, u, dst):
                turn_dve(dve, name)
                split_lo(dve, u + 1)
                newton_dve(dve, order, r)
                dve.wait_ge(rstd_ready[r], 1)
                unit_z_dve(dve, u, dst, rstd[r][:, 1:2])

            def static_attention(kinds):
                pairs = static_pairs(kinds)

                def maxima(kind, i, g):
                    sink = None
                    if kind == "C":
                        sink = rowp[:, R_SINK + i:R_SINK + i + 5:4].unsqueeze(2).to_broadcast([P, 2, T])
                    row_max_dve(dve, g, g % 2, static_biases(kind, i), sink=sink)

                def difference(i, g):
                    p = g % 2
                    dve.wait_ge(probs_done, g + 1)
                    order.after(dve.reciprocal(inv_sum[p][:, :], row_sum[p][:, :]))
                    order.after(dve.tensor_tensor(inv_sum[p][:, :], inv_sum[p][:, :], lam4[:, :], ALU.mult))
                    for t, cols in ((1, slice(0, 256)), (0, slice(256, 384))):
                        ins = dve.tensor_scalar(sc[p][1][:, cols], sc[p][1][:, cols], inv_sum[p][:, 2 + t:3 + t], None, ALU.mult)
                    order.after(ins)
                    for t, cols in ((1, slice(0, 256)), (0, slice(256, 384))):
                        ins = dve.scalar_tensor_tensor(out=sc[p][0][:, cols], in0=sc[p][0][:, cols], scalar=inv_sum[p][:, t:t + 1],
                                                       in1=sc[p][1][:, cols], op0=ALU.mult, op1=ALU.add)
                    ins.then_inc(diff_done, 1)

                def probs_out(kind, i, g):
                    if kind == "A":
                        difference(i, g)
                        pt_evac_dve(dve, g, g % 2)
                    else:
                        pt_evac_dve(dve, g, g % 2)
                        inv_sum_dve(dve, g, g % 2, sink=kind == "C")

                def out(kind, i, g):
                    p = g % 2
                    if kind == "A":
                        dve.wait_ge(attended, g + 1)
                        dve.tensor_copy(mix[:, :, 128 * i:128 * (i + 1)],
                                        out_bank(g, p)[:, 0:256].rearrange("p (t e) -> p t e", t=T)).then_inc(heads_out, 1)
                        return
                    heads_out_dve(dve, g, p, static_out(kind, i))

                dst, r = (z_even, 0) if kinds == "AB" else (z_odd, 3)
                for n, (kind, i, g) in enumerate(pairs):
                    maxima(kind, i, g)
                    if n:
                        out(*pairs[n - 1])
                    late = None
                    if n in SPLITS[kinds]:
                        u = FIRST_FILL[kinds] + SPLITS[kinds][n]
                        split_lo_half(dve, u, 0)
                        if any(u == v and e0 == 0 for v, e0, _ in slot_pieces(kinds, n, 1)):
                            split_lo_half(dve, u, 1)
                        else:
                            late = u
                    for u in slot_ends(kinds, n, 0):
                        unit_z_dve(dve, u, dst, rstd[r][:, 1:2])
                    beside_dve(kinds, n, 0)
                    probs_out(kind, i, g)
                    if late is not None:
                        split_lo_half(dve, late, 1)
                    for u in slot_ends(kinds, n, 1):
                        unit_z_dve(dve, u, dst, rstd[r][:, 1:2])
                    beside_dve(kinds, n, 1)
                v, th0, g0 = (z_even, 2048, 3584) if kinds == "AB" else (z_odd, 1280, 2816)
                th = v[:, :, th0:th0 + 512]
                dve.wait_ge(tanh_second, 1 if kinds == "AB" else 2)
                order.after(dve.scalar_tensor_tensor(out=th, in0=th, scalar=1.0, in1=v[:, :, g0:g0 + 512],
                                                     op0=ALU.add, op1=ALU.mult))
                dve.tensor_tensor(mix[:, :, 512:768], mix[:, :, 512:768], th[:, :, 0:256], ALU.mult).then_inc(mix_ready, 1)
                out(*pairs[-1])
                dve.wait_ge(heads_out, pairs[-1][2] + 1)
                dve.tensor_tensor(mix[:, :, 768:1024], mix[:, :, 768:1024], th[:, :, 256:512], ALU.mult).then_inc(mix_ready, 1)

            def group_sums(r, at, src, groups, width, squares):
                dve.wait_ge(squares_ready, squares)
                return dve.tensor_reduce(ms[r][:, :].rearrange("p (t g) -> p t g", t=T)[:, :, at:at + groups],
                                         src.rearrange("p t (g d) -> p t g d", d=width), AX.X, ALU.add)

            def beside_dve(kinds, n, late):
                at = (kinds, n, late)
                if at == ("AB", 2, 0):
                    group_sums(11, 0, mix[:, :, 512:1024], 8, HD, 3).then_inc(squares_read, 1)
                if at == ("AB", 2, 1):
                    group_sums(11, 8, mix[:, :, 512:1024], 8, HD, 4).then_inc(ms_ready[11], 1)
                if at == ("AB", 3, 0):
                    newton_dve(dve, order, 11)
                if at == ("AB", 4, 1):
                    group_sums(2, 0, z_even[:, :, 512:1024], 4, P, 5).then_inc(ms_ready[2], 1)
                if at == ("AB", 5, 0):
                    newton_dve(dve, order, 2)
                if at == ("CD", 0, 1):
                    group_sums(12, 0, mix[:, :, 512:1024], 8, HD, 7).then_inc(squares_read, 1)
                if at == ("CD", 1, 1):
                    group_sums(12, 8, mix[:, :, 512:1024], 8, HD, 8).then_inc(ms_ready[12], 1)
                if at == ("CD", 2, 0):
                    newton_dve(dve, order, 12)

            project(0, 1, z_even, rstd[0][:, 1:2])
            dve.wait_ge(evac_act, act_after[0])
            dve.wait_ge(evac_dve, dve_after[0])
            order.after(dve.tensor_tensor(logf[:, 0, :, :], z_even[:, :, 4096:4104],
                                          rowp[:, R_FB:R_FB + 8].unsqueeze(1).to_broadcast([P, T, 8]), ALU.add))
            dve.scalar_tensor_tensor(out=logf[:, 1, :, :], in0=logf[:, 0, :, :], scalar=-1.0, in1=logf[:, 0, :, :],
                                     op0=ALU.mult, op1=ALU.min).then_inc(forget_in, 1)
            dve.wait_ge(forget_log, 1)
            order.after(dve.scalar_tensor_tensor(out=logf[:, 3, :, :], in0=logf[:, 0, :, :], scalar=0.0, in1=logf[:, 2, :, :],
                                                 op0=ALU.min, op1=ALU.subtract))
            for s in range(T):
                ins = dve.tensor_scalar(qkT[s][:, :].rearrange("p (h m) -> p h m", h=8),
                                        logf[:, 3, s, :].unsqueeze(2).to_broadcast([P, 8, P]), -1.0, None, ALU.mult)
            ins.then_inc(forget_ready, 1)
            project(1, 1, z_even, rstd[0][:, 1:2])
            group_sums(1, 0, mix[:, :, 0:512], 8, HD, 1)
            dve.wait_ge(cum_done, 1)
            dve.tensor_copy(cum[:, :, :], bank[4][:, 0:16].rearrange("p (t h) -> p t h", t=T)).then_inc(cum_ready, 1)
            dve.wait_ge(cum_ready, 1)
            project(2, 1, z_even, rstd[0][:, 1:2])
            group_sums(1, 8, mix[:, :, 512:1024], 8, HD, 2).then_inc(ms_ready[1], 1)
            split_lo(dve, 4)
            newton_dve(dve, order, 1)
            dve.wait_ge(cum_done, 2)
            dve.wait_ge(even_tables, 4)
            for h in range(8):
                b = bank[4 + h // 2][:, (h % 2) * SEQ:(h % 2 + 1) * SEQ]
                dve.scalar_tensor_tensor(out=bias_b[:, h, 0:256], in0=b, scalar=cum[:, 1, h:h + 1], in1=causal,
                                         op0=ALU.add, op1=ALU.add)
                ins = dve.scalar_tensor_tensor(out=bias_b[:, h, 256:384], in0=b[:, 0:P], scalar=cum[:, 0, h:h + 1],
                                               in1=causal[:, P:], op0=ALU.add, op1=ALU.add)
            ins.then_inc(bias_ready, 1)
            unit_z_dve(dve, 3, z_even, rstd[0][:, 1:2])
            dve.wait_ge(lam_ready, 1)
            static_attention("AB")
            turn_dve(dve, "even_mix")
            project_x(first["even_out"])
            if upto < 2:
                return
            first_unit("odd", 3, first["odd_in"], z_odd)
            project(first["odd_in"] + 1, 1, z_odd, rstd[3][:, 1:2])
            group_sums(4, 0, mix[:, :, 0:640], 10, HD, 6).then_inc(ms_ready[4], 1)
            split_lo(dve, first["odd_in"] + 3)
            newton_dve(dve, order, 4)
            unit_z_dve(dve, first["odd_in"] + 2, z_odd, rstd[3][:, 1:2])
            dve.wait_ge(tables, 9)
            static_attention("CD")
            turn_dve(dve, "odd_mix")
            project_x(first["odd_out"])
            if upto < 3:
                return
            u = first["dsa_in"]
            first_unit("dsa", 5, u, z_dsa)
            project(u + 1, 1, z_dsa, rstd[5][:, 1:2])

            def rope(groups):
                parts = []
                for v, f0, half, at in groups:
                    heads = v.shape[2]
                    cos = cosine[:, :, f0:f0 + half].unsqueeze(2).to_broadcast([P, T, heads, half])
                    sin = sine[:, :, f0:f0 + half].unsqueeze(2).to_broadcast([P, T, heads, half])
                    a, b = v[:, :, :, 0:half], v[:, :, :, half:2 * half]
                    n = T * heads * half
                    flat = mix[:, :, :].rearrange("p t n -> p (t n)")
                    tmp = [flat[:, at + n * m:at + n * (m + 1)].rearrange("p (t h d) -> p t h d", t=T, h=heads) for m in range(4)]
                    dve.tensor_tensor(tmp[0], a, cos, ALU.mult)
                    dve.tensor_tensor(tmp[1], b, sin, ALU.mult)
                    dve.tensor_tensor(tmp[2], b, cos, ALU.mult)
                    last = dve.tensor_tensor(tmp[3], a, sin, ALU.mult)
                    parts.append((a, b, tmp))
                order.after(last)
                for a, b, tmp in parts:
                    dve.tensor_tensor(a, tmp[0], tmp[1], ALU.subtract)
                    last = dve.tensor_tensor(b, tmp[2], tmp[3], ALU.add)
                return last

            dve.wait_ge(trig_ready, 1)

            def evacuated(u):
                dve.wait_ge(evac_act, act_after[u])
                dve.wait_ge(evac_dve, dve_after[u])

            def rotated(v, lo, hi, width, at, rot):
                return v[:, :, lo:hi].rearrange("p t (h d) -> p t h d", d=width)[:, :, :, at:at + rot]

            evacuated(u + 1)
            rope([(rotated(z_dsa, 1536, 2112, HD, 0, 16), 0, 8, 0)]).then_inc(roped, 1)
            order.after(dve.tensor_scalar(wi[:, :, :], z_dsa[:, :, 2112:2120], (8 ** -0.5) * (HD ** -0.5), None, ALU.mult))
            split_lo(dve, u + 3)
            unit_z_dve(dve, u + 2, z_dsa, rstd[5][:, 1:2])
            halves = ((1, slice(0, 256)), (0, slice(256, 384)))

            def logits(heads):
                for h in heads:
                    dve.wait_ge(logits_relu, h + 1)
                    for t, cols in halves:
                        if h == 0:
                            ins = dve.tensor_scalar(score[:, cols], rl[:, 0, cols], wi[:, t, 0:1], None, ALU.mult)
                        else:
                            ins = dve.scalar_tensor_tensor(out=score[:, cols], in0=rl[:, h % 2, cols], scalar=wi[:, t, h:h + 1],
                                                           in1=score[:, cols], op0=ALU.mult, op1=ALU.add)
                    ins.then_inc(logits_added, 1)
                    dve.wait_ge(logits_added, h + 1)

            logits(range(4))
            split_lo(dve, u + 4)
            logits(range(4, 8))
            for t, cols in halves:
                ins = dve.scalar_tensor_tensor(out=score[:, cols], in0=chunked[:, SEQ - (cols.stop - cols.start):],
                                               scalar=HIDDEN / MASKED, in1=score[:, cols], op0=ALU.mult, op1=ALU.add)
            order.after(ins)
            for taken in range(TOPK // 8):
                if taken == 2:
                    evacuated(u + 2)
                    rope([(rotated(z_dsa, 1024, 1280, HD, 0, 16), 0, 8, 576)])
                if taken == 5:
                    unit_z_dve(dve, u + 3, z_dsa, rstd[5][:, 1:2])
                    evacuated(u + 3)
                    rope([(rotated(z_dsa, 0, 512, HD, 0, 16), 0, 8, 832)])
                for t, cols in halves:
                    ins = dve.max(best[:, t, :], score[:, cols])
                order.after(ins)
                for t, cols in halves:
                    ins = dve.match_replace(score[:, cols], best[:, t, :], score[:, cols], TAKEN)
                order.after(ins)
            order.after(dve.tensor_scalar(bias_s, score, (HIDDEN + TAKEN) / 2, MASKED, ALU.is_gt, ALU.mult))

            unit_z_dve(dve, u + 4, z_dsa, rstd[5][:, 1:2])
            evacuated(u + 4)
            rope([(rotated(z_dsa, 512, 1024, HD, 0, 16), 0, 8, 1344)]).then_inc(roped, 1)
            split_lo(dve, first["dsa_out"])

            def looped_attention(first_pair, biases, scale, dst):
                row_max_dve(dve, first_pair, 0, biases, scale)

                def step(g, p, dst_before, maxima=True):
                    if maxima:
                        row_max_dve(dve, plus(g, 1), 1 - p, biases, scale)
                    pt_evac_dve(dve, g, p)
                    inv_sum_dve(dve, g, p)
                    if dst_before is not None:
                        heads_out_dve(dve, plus(g, -1), 1 - p, dst_before)

                step(first_pair, 0, None)
                step(first_pair + 1, 1, dst(0))
                with dve.Fori(0, 2) as i:
                    for j in range(2):
                        step(i * 2 + (first_pair + 2 + j), j, dst(i * 2 + (1 + j)))
                step(first_pair + 6, 0, dst(5))
                step(first_pair + 7, 1, dst(6), maxima=False)
                heads_out_dve(dve, first_pair + 7, 1, dst(7))

            def sparse_out(i):
                return mix[:, :, :].rearrange("p t (c s) -> p c t s", c=2)[:, :, :, bass.ds(i * HD, HD)]

            def latent_out(i):
                return mix[:, :, bass.ds(i * P, P)].rearrange("p t (c d) -> p c t d", c=2)

            looped_attention(PAIRS["S"], [(bias_s[:, 0:256], bias_s[:, 256:384])] * 2, 1.0, sparse_out)
            turn_dve(dve, "dsa_mix")
            project_x(first["dsa_out"])
            if upto < 4:
                return

            def mlp(m):
                r, u = (6, 9)[m], first[f"mlp{m}"]
                turn_dve(dve, f"mlp{m}")
                newton_dve(dve, order, r, square=rstd_sq[m][:, :])

                def up(v, b, i=None):
                    split_lo(dve, v + 1, i, 4)
                    base = 2 * FF_BLOCKS * m + 2 * b
                    if base > 0:
                        dve.wait_ge(u_lo_done, base if i is None else i * 4 + base)
                    for j in range(2):
                        dve.wait_ge(relu_done, base + j + 1 if i is None else i * 4 + (base + j + 1))
                        dve.tensor_tensor(sq[j][:, :], relu[j][:, :], relu[j][:, :], ALU.mult).then_inc(sq_done, 1)
                    for j in range(2):
                        dve.wait_ge(u_hi_done, base + j + 1 if i is None else i * 4 + (base + j + 1))
                        dve.tensor_tensor(u_lo[b % 2][:, 2 * j:2 * j + 2, :], sq[j][:, :].rearrange("p (f q) -> p f q", f=2),
                                          u_hi[b % 2][:, 2 * j:2 * j + 2, :].bitcast(F32), ALU.subtract).then_inc(u_lo_done, 1)

                up(u, 0)
                up(u + 1, 1)
                split_lo(dve, u + 3)
                up(u + 3, 2)
                split_lo(dve, u + 5)
                with dve.Fori(0, 2) as i:
                    up(u + 5, 3, i)
                    split_lo(dve, u + 7, i, 4)
                    up(u + 7, 4, i)
                    split_lo(dve, u + 9, i, 4)
                up(u + 13, 7)
                split_lo(dve, u + 15)
                split_lo(dve, u + 16)
                dve.wait_ge(mm_done, mm_after[u + 15])
                dve.wait_ge(rstd_ready[r], 1)
                for t in range(T):
                    for half in range(2):
                        cols = slice(half * BLOCK, (half + 1) * BLOCK)
                        ins = dve.scalar_tensor_tensor(out=x[:, t, cols], in0=bank[4 + 2 * t + half][:, :],
                                                       scalar=rstd_sq[m][:, t:t + 1], in1=x[:, t, cols], op0=ALU.mult, op1=ALU.add)
                ins.then_inc(x_ready, 1)

            mlp(0)
            if upto < 5:
                return
            first_unit("mla", 7, first["mla_in_rest"], z_mla)
            project(first["mla_in"], 1, z_mla, rstd[7][:, 1:2])
            turn_dve(dve, "latent")
            u = first["q_up"]
            split_lo(dve, u + 1)
            newton_dve(dve, order, 8)
            dve.wait_ge(rstd_ready[8], 1)
            evacuated(first["mla_in_rest"])
            order.after(rope([(rotated(z_mla, 640, 672, 32, 0, 32), 8, 16, 1024)]))
            unit_z_dve(dve, u, q_full, rstd[8][:, 1:2])
            q_rope = rotated(q_full, 0, Q_UP, 96, 64, 32)
            split_lo(dve, u + 2)
            evacuated(u)
            rope([(q_rope[:, :, 0:8, :], 8, 16, 0)])
            unit_z_dve(dve, u + 1, q_full, rstd[8][:, 1:2])
            evacuated(u + 1)
            rope([(q_rope[:, :, 8:16, :], 8, 16, 1024)]).then_inc(mla_roped, 1)
            project(first["kv_up"], 1, kv_full, rstd[8][:, 3:4])
            looped_attention(PAIRS["L"], [(chunked[:, :], chunked[:, P:])] * 2, 96 ** -0.5, latent_out)
            turn_dve(dve, "mla_mix")
            project_x(first["mla_out"])
            if upto < 6:
                return
            mlp(1)
            newton_dve(dve, order, 10)
            dve.wait_ge(rstd_ready[10], 1)
            dve.wait_ge(final_loaded, 16)
            for t in range(T):
                dve.scalar_tensor_tensor(out=mix[:, t, :], in0=x[:, t, :], scalar=rstd[10][:, t:t + 1], in1=g_final[:, :],
                                         op0=ALU.mult, op1=ALU.mult).then_inc(final_done, 1)


WEIGHTS = {"even_in": "even_w_in", "even_out": "even_w_out", "odd_in": "odd_w_in", "odd_out": "odd_w_out",
           "dsa_in": "a_w_in_2", "dsa_out": "a_w_out_2", "mla_in": "b_w_in_2", "q_up": "b_w_q_up_2",
           "kv_up": "b_w_kv_up_2", "mla_out": "b_w_out_2"}


def kernel(**inputs):
    import concourse.bacc as bacc
    from concourse.bass_utils import run_bass_kernel_spmd

    a = {k: np.ascontiguousarray(v) for k, v in inputs.items()}
    arrays = {name: a[key][0] for name, key in WEIGHTS.items()}
    for m in range(2):
        arrays[f"up{m}"] = a["mlp_w_up_2"][m]
        arrays[f"down{m}"] = a["mlp_w_down_2"][m]
    rows = [a["even_ln_g"], a["odd_ln_g"], a["attn_norm_2"], a["mlp_norm_2"], a["b_q_norm_2"], a["b_kv_norm_2"], a["a_subln_g"]]
    for k in ("a", "b", "c", "d"):
        for which in ("q", "k"):
            rows += [a[f"{k}_{which}_norm_g"]] * 2
    arrays["gain_rows"] = np.concatenate([r.reshape(-1) for r in rows]).reshape(GAIN_ROWS, P)
    freq = [500000.0 ** (-np.arange(0, rot, 2) / rot) for rot in (16, 32)]
    params = [a["a_lambda_q1"], a["a_lambda_k1"], a["a_lambda_q2"], a["a_lambda_k2"], a["b_forget_bias"], a["c_sinks"]]
    arrays["row_params"] = np.concatenate([r.reshape(-1) for r in params] + [f.astype(np.float32) for f in freq])
    table = a["d_rel_bias"][0]
    entry = np.clip(np.arange(P)[:, None] + P - np.arange(SEQ)[None, :] + 63, 0, table.shape[1] - 1)
    arrays["rel_band"] = np.ascontiguousarray(table[:, entry].transpose(1, 0, 2))
    arrays["x"] = a["x"][0]
    arrays["positions"] = np.ascontiguousarray(a["positions_2"][0].reshape(T, P).T)
    arrays["final_gain"] = a["final_norm_2"]

    nc = bacc.Bacc("TRN2", target_bir_lowering=False, num_devices=1)
    aps = {k: nc.dram_tensor(f"in_{k}", v.shape, mybir.dt.from_np(v.dtype), kind="ExternalInput").ap() for k, v in arrays.items()}
    out = nc.dram_tensor("out", (SEQ, DM), F32, kind="ExternalOutput").ap()
    program(nc, aps, aps["x"], aps["gain_rows"], aps["row_params"], aps["positions"], aps["rel_band"], aps["final_gain"], out)
    r = run_bass_kernel_spmd(nc, [{f"in_{k}": v for k, v in arrays.items()}], core_ids=[0])
    return r.results[0]["out"].reshape(1, SEQ, DM)
```

```python
import math
from contextlib import ExitStack

import numpy as np

import concourse.bass as bass
from concourse import mybir
from concourse.alu_op_type import AluOpType as ALU

F32 = mybir.dt.float32
F32R = mybir.dt.float32r
I32 = mybir.dt.int32
ACT = mybir.ActivationFunctionType
AX = mybir.AxisListType

P = 128
SEQ = 256
T = SEQ // P
DM = 1024
KC = DM // P
HD = 64
EPS = 1e-6
MASKED = -1e30
HIDDEN = -3e38
TAKEN = -3.3e38
N_EVEN, N_ODD, N_DSA, N_MLA = 4104, 3328, 2120, 672
Q_LORA, KV_LORA, ROPE = 384, 256, 32
Q_UP, KV_UP = 1536, 2048
FF_BLOCKS = 8
TOPK = 64
BLOCK = 512
LAM_INIT = 0.8 - 0.6 * math.exp(0.0)
G_EVEN, G_ODD, G_DSA, G_MLA, G_MLP0, G_MLP1, G_QL, G_KVL, G_SUB, G_HEAD = 0, 8, 16, 24, 32, 40, 48, 51, 53, 54
GAIN_ROWS = G_HEAD + 8
R_LAM, R_FB, R_SINK, R_FREQ = 0, 256, 264, 272
ROW_PARAMS = R_FREQ + 24


def weight_units():
    units, first = [], {}

    def columns(stage, matrix, kind, start, end, width, kc=KC, split=1, row=0):
        first.setdefault(stage, len(units))
        for c in range(start, end, width):
            w = min(width, end - c)
            units.append((matrix, kind, row, kc, c, w, [(i * (w // split), w // split) for i in range(split)]))

    for start, end in ((4096, N_EVEN), (0, 512), (512, 1024), (1024, 1536), (2048, 2560), (2560, 3072), (3072, 3584),
                       (1536, 2048), (3584, 4096)):
        columns("even_in", "even_in", "z", start, end, BLOCK)
    columns("even_out", "even_out", "x", 0, DM, BLOCK)
    for start, end in ((512, 768), (0, 512), (1280, 1792), (1792, 2304), (2304, 2816), (768, 1280), (2816, 3328)):
        columns("odd_in", "odd_in", "z", start, end, BLOCK)
    columns("odd_out", "odd_out", "x", 0, DM, BLOCK)
    for start, end in ((2048, N_DSA), (1536, 2048), (1024, 1536), (0, 512), (512, 1024)):
        columns("dsa_in", "dsa_in", "z", start, end, BLOCK)
    columns("dsa_out", "dsa_out", "x", 0, DM, BLOCK)

    def mlp(m):
        first[f"mlp{m}"] = len(units)
        for b in range(FF_BLOCKS + 1):
            if b < FF_BLOCKS:
                units.append((f"up{m}", "up", 0, KC, b * BLOCK, BLOCK, [(0, 256), (256, 256)]))
            if b:
                units.append((f"down{m}", "down", 4 * (b - 1), 4, 0, DM, [(0, DM)]))

    mlp(0)
    for start, end in ((512, N_MLA), (0, 512)):
        columns("mla_in", "mla_in", "z", start, end, BLOCK)
    columns("q_up", "q_up", "z", 0, Q_UP, 768, Q_LORA // P, split=2)
    columns("kv_up", "kv_up", "z", 0, KV_UP, KV_UP, KV_LORA // P, split=4)
    columns("mla_out", "mla_out", "x", 0, DM, BLOCK)
    mlp(1)
    return units, first


def program(nc, w, x_in, gain_rows, row_params, positions, rel_band, final_gain, out):
    units, first = weight_units()
    mm_after, act_after, dve_after, pair_of = [], [], [], []
    mm = act_n = dve_n = blocks = 0
    block_evacs = []
    for _, kind, _, _, _, _, parts in units:
        pair_of.append(blocks)
        if kind == "down":
            mm += 1
        else:
            mm += len(parts)
        if kind in ("z", "x"):
            for _ in parts:
                act_n += kind == "z"
                dve_n += 1
                blocks += 1
                block_evacs.append((act_n, dve_n))
        mm_after.append(mm)
        act_after.append(act_n)
        dve_after.append(dve_n)

    def w_view(u):
        matrix, _, row, kc, c, n, _ = units[u]
        return w[matrix][row * P:(row + kc) * P, c:c + n].rearrange("(k p) n -> p k n", p=P)

    ctx = ExitStack()
    with ctx:
        def sb(name, shape, dt=F32):
            return ctx.enter_context(nc.sbuf_tensor(name, shape, dt))

        def sem(name):
            return ctx.enter_context(nc.semaphore(name))

        x = sb("x", [P, T, DM])
        raw = [sb(f"raw{i}", [P, 4096]) for i in range(2)]
        w_hi = [sb(f"w_hi{i}", [P, 4096], F32R) for i in range(2)]
        w_lo = [sb(f"w_lo{i}", [P, 4096], F32R) for i in range(2)]
        h_hi = sb("h_hi", [P, KC, SEQ], F32R)
        h_lo = sb("h_lo", [P, KC, SEQ], F32R)
        mix = sb("mix", [P, T, DM])
        ident = sb("ident", [P, P])
        chunked = sb("chunked", [P, SEQ])
        gcols = sb("gcols", [P, GAIN_ROWS])
        g_mix = sb("g_mix", [P, KC])
        g_qk = sb("g_qk", [P, 4])
        rowp = sb("rowp", [P, ROW_PARAMS])
        lam4 = sb("lam4", [P, 4])
        wait_carrier = sb("wait_carrier", [P, 1])
        lam_diff = sb("lam_diff", [P, 1])
        lam_dot = sb("lam_dot", [P, 2])
        eps = sb("eps", [P, 1])
        pos_i = sb("pos_i", [P, T], I32)
        pos = sb("pos", [P, T])
        angle = sb("angle", [P, T, 24])
        turns = sb("turns", [P, T, 24])
        cosine = sb("cosine", [P, T, 24])
        sine = sb("sine", [P, T, 24])
        R_WIDTH = [2, 32, 8, 2, 20, 2, 2, 2, 4, 2, 2, 32, 32]
        ms = [sb(f"ms{i}", [P, n]) for i, n in enumerate(R_WIDTH)]
        rstd = [sb(f"rstd{i}", [P, n]) for i, n in enumerate(R_WIDTH)]
        r_tmp = sb("r_tmp", [P, 64])
        r_log = sb("r_log", [P, 64])
        rstd_sq = [sb(f"rstd_sq{i}", [P, T]) for i in range(2)]

        both = ExitStack()
        with both:
            def sa(name, shape, dt=F32):
                return both.enter_context(nc.sbuf_tensor(name, shape, dt))
            z = sa("z", [P, T * N_EVEN])
            tab = sa("tab", [P, 4096])
            qs = [sa(f"qs{i}", [P, 256]) for i in range(2)]
            ks = [sa(f"ks{i}", [P, 256]) for i in range(2)]
            qkT = [sa(f"qkT{i}", [P, 1024]) for i in range(2)]
            sc = [[sa(f"sc{i}{c}", [P, 384]) for c in range(2)] for i in range(2)]
            pT = [sa(f"pT{i}", [P, 2, 384]) for i in range(2)]
            row_max = [sa(f"row_max{i}", [P, 4]) for i in range(2)]
            neg_max = [sa(f"neg_max{i}", [P, 4]) for i in range(2)]
            row_sum = [sa(f"row_sum{i}", [P, 4]) for i in range(2)]
            inv_sum = [sa(f"inv_sum{i}", [P, 4]) for i in range(2)]
            sink_e = [sa(f"sink_e{i}", [P, 4]) for i in range(2)]
            logf = sa("logf", [P, 4, T, 8])
            cum = sa("cum", [P, T, 8])
            wi = sa("wi", [P, T, 8])
            best = sa("best", [P, T, 8])
        upper = pT[0][:, :, 0:SEQ]
        causal = sc[1][0][:, 0:SEQ]
        mlpb = ExitStack()
        with mlpb:
            def sm(name, shape, dt=F32):
                return mlpb.enter_context(nc.sbuf_tensor(name, shape, dt))
            relu = [sm(f"relu{i}", [P, BLOCK]) for i in range(2)]
            sq = [sm(f"sq{i}", [P, BLOCK]) for i in range(2)]
            u_hi = [sm(f"u_hi{i}", [P, 4, SEQ], F32R) for i in range(2)]
            u_lo = [sm(f"u_lo{i}", [P, 4, SEQ], F32R) for i in range(2)]
            g_final = sm("g_final", [P, DM])

        bank = [ctx.enter_context(nc.psum_tensor(f"bank{i}", [P, BLOCK], F32)) for i in range(8)]

        x_loaded, rows_loaded, params_loaded = sem("x_loaded"), sem("rows_loaded"), sem("params_loaded")
        pos_loaded, band_loaded, final_loaded = sem("pos_loaded"), sem("band_loaded"), sem("final_loaded")
        stored = sem("stored")
        raw_loaded = [sem(f"raw_loaded{i}") for i in range(2)]
        hi_split, lo_split = sem("hi_split"), sem("lo_split")
        mm_done, evac_act, evac_dve = sem("mm_done"), sem("evac_act"), sem("evac_dve")
        consts = sem("consts")
        tables, even_tables = sem("tables"), sem("even_tables")
        gains_turned, gains_ready = sem("gains_turned"), sem("gains_ready")
        trig_in, trig_ready = sem("trig_in"), sem("trig_ready")
        lam_in, lam_exp, lam_ready = sem("lam_in"), sem("lam_exp"), sem("lam_ready")
        turned, hi_turned, lo_turned = sem("turned"), sem("hi_turned"), sem("lo_turned")
        x_ready, mix_ready = sem("x_ready"), sem("mix_ready")
        ms_ready = [sem(f"ms_ready{i}") for i in range(13)]
        guess_ready = [sem(f"guess_ready{i}") for i in range(13)]
        rstd_ready = [sem(f"rstd_ready{i}") for i in range(13)]
        squares_ready, squares_read = sem("squares_ready"), sem("squares_read")
        act_order, dve_order, pool_order = sem("act_order"), sem("dve_order"), sem("pool_order")
        relu_done, sq_done, u_hi_done, u_lo_done = sem("relu_done"), sem("sq_done"), sem("u_hi_done"), sem("u_lo_done")
        staged, qk_turned, qk_ready = sem("staged"), sem("qk_turned"), sem("qk_ready")
        scores_done, max_done, probs_done = sem("scores_done"), sem("max_done"), sem("probs_done")
        diff_done, probs_turned, pt_act, pt_dve = sem("diff_done"), sem("probs_turned"), sem("pt_act"), sem("pt_dve")
        attended, heads_out = sem("attended"), sem("heads_out")
        raw_max_done, inv_done = sem("raw_max_done"), sem("inv_done")
        forget_in, forget_log, forget_ready = sem("forget_in"), sem("forget_log"), sem("forget_ready")
        cum_done, cum_ready, bias_ready = sem("cum_done"), sem("cum_ready"), sem("bias_ready")
        tanh_first, tanh_second = sem("tanh_first"), sem("tanh_second")
        first_gated = sem("first_gated")
        roped, ki_staged, index_turned, index_ready = sem("roped"), sem("ki_staged"), sem("index_turned"), sem("index_ready")
        logits_done, logits_relu, logits_added = sem("logits_done"), sem("logits_relu"), sem("logits_added")
        mla_roped, kr_staged = sem("mla_roped"), sem("kr_staged")
        gained, final_act, final_dve = sem("gained"), sem("final_act"), sem("final_dve")

        TURNS = {"even": (8, gcols, G_EVEN), "even_mix": (8, g_mix, 0), "odd": (8, gcols, G_ODD), "odd_mix": (8, 0.5, 0),
                 "dsa": (8, gcols, G_DSA), "dsa_mix": (8, None, 0), "mlp0": (8, gcols, G_MLP0), "mla": (8, gcols, G_MLA),
                 "latent": (5, gcols, G_QL), "mla_mix": (8, None, 0), "mlp1": (8, gcols, G_MLP1)}
        turn_base, n = {}, 0
        for name, (chunks, _, _) in TURNS.items():
            turn_base[name] = n
            n += (chunks + 1) // 2
        X_READY = {"even": (x_loaded, 32), "odd": (evac_dve, dve_after[first["even_out"] + 1]), "dsa": (evac_dve, dve_after[first["odd_out"] + 1]),
                   "mlp0": (evac_dve, dve_after[first["dsa_out"] + 1]), "mla": (x_ready, 2),
                   "mlp1": (evac_dve, dve_after[first["mla_out"] + 1]), "final": (x_ready, 4)}
        STATS = {"A": 1, "B": 11, "C": 4, "D": 12}
        PAIRS = {"A": 0, "B": 4, "C": 8, "D": 12, "S": 16, "L": 24}

        z_even = z[:, 0:T * N_EVEN].rearrange("p (t n) -> p t n", t=T)
        z_odd = z[:, 0:T * N_ODD].rearrange("p (t n) -> p t n", t=T)
        z_dsa = z[:, 0:T * N_DSA].rearrange("p (t n) -> p t n", t=T)
        z_mla = tab[:, 0:T * N_MLA].rearrange("p (t n) -> p t n", t=T)
        q_full = z[:, 0:T * Q_UP].rearrange("p (t n) -> p t n", t=T)
        kv_full = z[:, T * Q_UP:T * (Q_UP + KV_UP)].rearrange("p (t n) -> p t n", t=T)
        qs_mla = [tab[:, 1536 + 768 * i:1920 + 768 * i] for i in range(2)]
        ks_mla = [tab[:, 1920 + 768 * i:2304 + 768 * i] for i in range(2)]
        bias_a = tab[:, 0:1024].rearrange("p (h j) -> p h j", h=4)
        bias_b = tab[:, 1024:4096].rearrange("p (h j) -> p h j", h=8)
        bias_c = tab[:, 0:2048].rearrange("p (h j) -> p h j", h=8)
        bias_d = tab[:, 2048:4096].rearrange("p (h j) -> p h j", h=8)
        bias_s = tab[:, 0:384]
        qiT = tab[:, 512:1536].rearrange("p (i q) -> p i q", i=4)
        kiT = tab[:, 1536:1792]
        score = tab[:, 1792:2176]
        rl = tab[:, 2304:3072].rearrange("p (i q) -> p i q", i=2)

        def wait_from(e, s, value):
            if not isinstance(value, int) or value > 0:
                e.wait_ge(s, value)

        def load_unit(e, u, i=None, per=0):
            matrix, kind, row, kc, c, n, _ = units[u]
            slot = u % 2
            dst = raw[slot][:, 0:kc * n].rearrange("p (k n) -> p k n", k=kc)
            if i is None:
                if u >= 2:
                    e.wait_ge(lo_split, 2 * (u - 1))
                e.dma_start(dst, w_view(u)).then_inc(raw_loaded[slot], 16)
                return
            e.wait_ge(lo_split, i * (2 * per) + 2 * (u - 1))
            if kind == "down":
                rows = w[matrix][bass.ds(i * (per // 2 * 4 * P) + row * P, kc * P), :]
                e.dma_start(dst, rows.rearrange("(k p) n -> p k n", p=P)).then_inc(raw_loaded[slot], 16)
            else:
                step = per // 2 if kind == "up" else per
                cols = w[matrix][:, bass.ds(i * (step * n) + c, n)]
                e.dma_start(dst, cols.rearrange("(k p) n -> p k n", p=P)).then_inc(raw_loaded[slot], 16)

        def split_hi(e, u, i=None, per=0, halves=(0, 1)):
            if u >= len(units):
                return
            slot, size = u % 2, units[u][3] * units[u][5]
            if i is None:
                e.wait_ge(raw_loaded[slot], 16 * (u // 2 + 1))
                if u >= 2:
                    e.wait_ge(mm_done, mm_after[u - 2])
            else:
                e.wait_ge(raw_loaded[slot], i * (8 * per) + 16 * (u // 2 + 1))
                e.wait_ge(mm_done, i * (mm_after[u - 2 + per] - mm_after[u - 2]) + mm_after[u - 2])
            for half in halves:
                cols = slice(half * size // 2, (half + 1) * size // 2)
                e.activation(w_hi[slot][:, cols], raw[slot][:, cols], ACT.Copy).then_inc(hi_split, 1)

        def split_lo_half(e, u, half, i=None, per=0):
            slot, size = u % 2, units[u][3] * units[u][5] // 2
            cols = slice(half * size, (half + 1) * size)
            wait_split(e, hi_split, u, half, i, per)
            e.tensor_tensor(w_lo[slot][:, cols], raw[slot][:, cols], w_hi[slot][:, cols].bitcast(F32),
                            ALU.subtract).then_inc(lo_split, 1)

        def wait_split(e, s, u, half, i=None, per=0):
            value = 2 * u + half + 1
            e.wait_ge(s, value if i is None else i * (2 * per) + value)

        def split_lo(e, u, i=None, per=0):
            if u < len(units):
                for half in range(2):
                    split_lo_half(e, u, half, i, per)

        def turn_scale(gain, column):
            if gain is None:
                return 1.0
            return gain if isinstance(gain, float) else gain[:, column:column + 1]

        def turn_pe(e, name, src, c0=0, c1=None):
            chunks = TURNS[name][0]
            for c in range(c0, chunks if c1 is None else c1):
                for t in range(T):
                    last = e.transpose(bank[4 + c // 2][:, (c % 2) * SEQ + t * P:(c % 2) * SEQ + (t + 1) * P],
                                       src[:, t, c * P:(c + 1) * P], ident[:, :])
                if c % 2 or c == chunks - 1:
                    last.then_inc(turned, 1)

        def x_mm_done(name):
            return mm_after[first[{"odd": "even_out", "dsa": "odd_out", "mlp0": "dsa_out", "mlp1": "mla_out"}[name]] + 1]

        def turn_act(e, name):
            chunks, gain, g0 = TURNS[name]
            if X_READY.get(name, (None,))[0] is evac_dve:
                e.wait_ge(mm_done, x_mm_done(name))
            for c in range(chunks):
                if c % 2 == 0:
                    e.wait_ge(turned, turn_base[name] + c // 2 + 1)
                scale = turn_scale(gain, g0 + c)
                ins = e.activation(h_hi[:, c, :], bank[4 + c // 2][:, (c % 2) * SEQ:(c % 2 + 1) * SEQ], ACT.Copy, scale=scale)
                if c % 2 or c == chunks - 1:
                    ins.then_inc(hi_turned, 1)

        def turn_dve(e, name, c0=0, c1=None):
            chunks, gain, g0 = TURNS[name]
            for c in range(c0, chunks if c1 is None else c1):
                if c % 2 == 0:
                    e.wait_ge(hi_turned, turn_base[name] + c // 2 + 1)
                scale = turn_scale(gain, g0 + c)
                ins = e.scalar_tensor_tensor(out=h_lo[:, c, :], in0=bank[4 + c // 2][:, (c % 2) * SEQ:(c % 2 + 1) * SEQ],
                                             scalar=scale, in1=h_hi[:, c, :].bitcast(F32), op0=ALU.mult, op1=ALU.subtract)
                if c % 2 or c == chunks - 1:
                    ins.then_inc(lo_turned, 1)

        def wait_turned(e, name):
            e.wait_ge(lo_turned, turn_base[name] + (TURNS[name][0] + 1) // 2)

        def unit_pe(e, u, chunk0=0, fresh=None):
            _, kind, _, kc, _, n, parts = units[u]
            slot = u % 2
            hi = w_hi[slot][:, 0:kc * n].rearrange("p (k n) -> p k n", k=kc)
            lo = w_lo[slot][:, 0:kc * n].rearrange("p (k n) -> p k n", k=kc)
            wait_split(e, lo_split, u, 0)
            for b, (c0, cn) in enumerate(parts):
                j = pair_of[u] + b
                if j >= 2:
                    a, d = block_evacs[j - 2]
                    wait_from(e, evac_act, a)
                    wait_from(e, evac_dve, d)
                for t in range(T):
                    dst = bank[2 * (j % 2) + t][:, 0:cn]
                    for k in range(kc):
                        if k == kc // 2 and t == 0 and b == 0:
                            wait_split(e, lo_split, u, 1)
                        if fresh and t == 0 and b == 0:
                            e.wait_ge(lo_turned, turn_base[fresh] + (chunk0 + k) // 2 + 1)
                        h, l = h_hi[:, chunk0 + k, t * P:(t + 1) * P], h_lo[:, chunk0 + k, t * P:(t + 1) * P]
                        e.matmul(dst, h, hi[:, k, c0:c0 + cn], start=(k == 0), stop=False)
                        e.matmul(dst, h, lo[:, k, c0:c0 + cn], start=False, stop=False)
                        last = e.matmul(dst, l, hi[:, k, c0:c0 + cn], start=False, stop=(k == kc - 1))
                last.then_inc(mm_done, 1)

        def first_unit_pe(e, u, name, turn_rest):
            n, j = units[u][5], pair_of[u]
            hi = w_hi[u % 2][:, 0:KC * n].rearrange("p (k n) -> p k n", k=KC)
            lo = w_lo[u % 2][:, 0:KC * n].rearrange("p (k n) -> p k n", k=KC)
            wait_split(e, lo_split, u, 0)
            if j >= 2:
                a, d = block_evacs[j - 2]
                wait_from(e, evac_act, a)
                wait_from(e, evac_dve, d)
            for half in range(2):
                if half:
                    wait_split(e, lo_split, u, 1)
                for t in range(T):
                    if not half and t:
                        turn_rest()
                    dst = bank[2 * (j % 2) + t][:, 0:n]
                    for k in range(4 * half, 4 * half + 4):
                        if t == 0:
                            e.wait_ge(lo_turned, turn_base[name] + k // 2 + 1)
                        h, l = h_hi[:, k, t * P:(t + 1) * P], h_lo[:, k, t * P:(t + 1) * P]
                        e.matmul(dst, h, hi[:, k, :], start=(k == 0), stop=False)
                        e.matmul(dst, h, lo[:, k, :], start=False, stop=False)
                        last = e.matmul(dst, l, hi[:, k, :], start=False, stop=(k == KC - 1))
            last.then_inc(mm_done, 1)

        def unit_eighths_pe(e, u, e0, e1):
            n, j = units[u][5], pair_of[u]
            hi = w_hi[u % 2][:, 0:KC * n].rearrange("p (k n) -> p k n", k=KC)
            lo = w_lo[u % 2][:, 0:KC * n].rearrange("p (k n) -> p k n", k=KC)
            if e0 == 0:
                wait_split(e, lo_split, u, 0)
                a, d = block_evacs[j - 2]
                wait_from(e, evac_act, a)
                wait_from(e, evac_dve, d)
            for piece in range(e0, e1):
                t = piece // 4
                if piece == 2:
                    wait_split(e, lo_split, u, 1)
                dst = bank[2 * (j % 2) + t][:, 0:n]
                for k in range(2 * (piece % 4), 2 * (piece % 4) + 2):
                    h, l = h_hi[:, k, t * P:(t + 1) * P], h_lo[:, k, t * P:(t + 1) * P]
                    e.matmul(dst, h, hi[:, k, :], start=(k == 0), stop=False)
                    e.matmul(dst, h, lo[:, k, :], start=False, stop=False)
                    last = e.matmul(dst, l, hi[:, k, :], start=False, stop=(k == KC - 1))
            if e1 == 8:
                last.then_inc(mm_done, 1)

        def mm_value(u, b, i=None, per=0):
            v = mm_after[u] - len(units[u][6]) + b + 1
            return v if i is None else i * (mm_after[u + per] - mm_after[u]) + v

        def unit_z_act(e, u, dst, scale, blocks=range(4)):
            for b, (c0, cn) in enumerate(units[u][6]):
                if b not in blocks:
                    continue
                j = pair_of[u] + b
                e.wait_ge(mm_done, mm_value(u, b))
                c = units[u][4] + c0
                e.activation(dst[:, 0, c:c + cn], bank[2 * (j % 2)][:, 0:cn], ACT.Copy, scale=scale).then_inc(evac_act, 1)

        def unit_z_dve(e, u, dst, scale, blocks=range(4)):
            for b, (c0, cn) in enumerate(units[u][6]):
                if b not in blocks:
                    continue
                j = pair_of[u] + b
                e.wait_ge(mm_done, mm_value(u, b))
                c = units[u][4] + c0
                e.tensor_scalar(dst[:, 1, c:c + cn], bank[2 * (j % 2) + 1][:, 0:cn], scale, None, ALU.mult).then_inc(evac_dve, 1)

        def unit_x_dve(e, u):
            j, c = pair_of[u], units[u][4]
            e.wait_ge(mm_done, mm_after[u])
            e.tensor_tensor(x[:, 0, c:c + BLOCK], bank[2 * (j % 2)][:, :], x[:, 0, c:c + BLOCK], ALU.add)
            e.tensor_tensor(x[:, 1, c:c + BLOCK], bank[2 * (j % 2) + 1][:, :], x[:, 1, c:c + BLOCK], ALU.add).then_inc(evac_dve, 1)

        def up_bank(m, b, j):
            return bank[2 * ((pair_of[first[f"mlp{m}"] - 1] + 1 + b) % 2) + j]

        class Order:
            def __init__(self, e, s):
                self.e, self.s, self.n = e, s, 0

            def after(self, ins):
                ins.then_inc(self.s, 1)
                self.n += 1
                self.e.wait_ge(self.s, self.n)

        def x_squares_act(e, r):
            for t in range(T):
                ins = e.activation(mix[:, t, :], x[:, t, :], ACT.Square, scale=DM ** -0.5, accum_out=ms[r][:, t:t + 1])
            ins.then_inc(ms_ready[r], 1)

        def guess_act(e, order, r, count=1):
            n = R_WIDTH[r]
            e.wait_ge(ms_ready[r], count)
            order.after(e.activation(r_log[:, 0:n], ms[r][:, :], ACT.Ln, bias=eps[:, 0:1]))
            e.activation(rstd[r][:, :], r_log[:, 0:n], ACT.Exp, scale=-0.5).then_inc(guess_ready[r], 1)

        def newton_dve(e, order, r, square=None):
            n = R_WIDTH[r]
            y, tmp = rstd[r][:, :], r_tmp[:, 0:n]
            e.wait_ge(guess_ready[r], 1)
            order.after(e.tensor_scalar(ms[r][:, :], ms[r][:, :], EPS, None, ALU.add))
            order.after(e.tensor_tensor(tmp, y, y, ALU.mult))
            order.after(e.tensor_tensor(tmp, tmp, ms[r][:, :], ALU.mult))
            order.after(e.tensor_scalar(tmp, tmp, -0.5, 1.5, ALU.mult, ALU.add))
            if square is None:
                e.tensor_tensor(y, y, tmp, ALU.mult).then_inc(rstd_ready[r], 1)
            else:
                order.after(e.tensor_tensor(y, y, tmp, ALU.mult))
                e.tensor_tensor(square, y, y, ALU.mult).then_inc(rstd_ready[r], 1)

        def is_static(g):
            return isinstance(g, int) and g < PAIRS["S"]

        def turn_bank(g, p):
            return bank[4] if is_static(g) else bank[p]

        def score_bank(g, p, c):
            return bank[5 + c] if is_static(g) else bank[2 + 2 * p + c]

        def out_bank(g, p):
            return bank[7] if is_static(g) else bank[6 + p]

        def before(g):
            return g if is_static(g) else g - 1

        def stage_wait_pool(e, g):
            wait_from(e, qk_turned, g - 1)

        def turn_qk_pe(e, g, p):
            e.wait_ge(staged, g + 1)
            wait_from(e, qk_ready, before(g))
            for j, src in enumerate((qs[p], ks[p])):
                for t in range(T):
                    last = e.transpose(turn_bank(g, p)[:, (2 * j + t) * P:(2 * j + t + 1) * P], src[:, t * P:(t + 1) * P], ident[:, :])
            last.then_inc(qk_turned, 1)

        def turn_qk_mla_pe(e, g, p):
            e.wait_ge(staged, g + 1)
            e.wait_ge(qk_ready, g)
            for j, src in enumerate((qs_mla[p], ks_mla[p])):
                for m in range(4):
                    last = e.transpose(bank[j][0:96, m * P:(m + 1) * P], src[:, m * 96:(m + 1) * 96], ident[:, :])
            last.then_inc(qk_turned, 1)

        def qk_evac_act(e, g, p, scale):
            e.wait_ge(qk_turned, g + 1)
            wait_from(e, scores_done, g - 1)
            e.activation(qkT[p][:, 0:256], turn_bank(g, p)[:, 0:256], ACT.Copy, scale=scale)
            e.activation(qkT[p][:, 256:512], turn_bank(g, p)[:, 256:512], ACT.Copy).then_inc(qk_ready, 1)

        def qk_evac_mla_act(e, g, p):
            e.wait_ge(qk_turned, g + 1)
            wait_from(e, scores_done, g - 1)
            e.activation(qkT[p][0:96, 0:512], bank[0][0:96, :], ACT.Copy)
            e.activation(qkT[p][0:96, 512:1024], bank[1][0:96, :], ACT.Copy).then_inc(qk_ready, 1)

        def scores_pe(e, g, p, mla=False):
            e.wait_ge(qk_ready, g + 1)
            wait_from(e, pt_dve, before(g))
            wait_from(e, pt_act, before(g) - PAIRS["B"])
            for c in range(2):
                dst = score_bank(g, p, c)
                if mla:
                    q, k = qkT[p][0:96, c * 256:(c + 1) * 256], qkT[p][0:96, 512 + c * 256:512 + (c + 1) * 256]
                else:
                    q, k = qkT[p][c * HD:(c + 1) * HD, 0:256], qkT[p][c * HD:(c + 1) * HD, 256:512]
                e.matmul(dst[:, 0:256], q[:, P:2 * P], k, start=True, stop=True)
                last = e.matmul(dst[:, 256:384], q[:, 0:P], k[:, 0:P], start=True, stop=True)
            last.then_inc(scores_done, 1)

        def row_max_dve(e, g, p, biases, scale=1.0, sink=None):
            e.wait_ge(scores_done, g + 1)
            wait_from(e, probs_turned, g - 1)
            if not isinstance(g, int):
                e.memset(wait_carrier[:, :], 0.0)
            for c in range(2):
                b1, b0 = biases[c]
                s = score_bank(g, p, c)
                for t, cols, b in ((1, slice(0, 256), b1), (0, slice(256, 384), b0)):
                    last = e.tensor_tensor_reduce(sc[p][c][:, cols], s[:, cols], b, 1.0, MASKED, ALU.add, ALU.max,
                                                  row_max[p][:, 2 * c + t:2 * c + t + 1])
            last.then_inc(raw_max_done, 1)
            e.wait_ge(raw_max_done, g + 1)
            if sink is not None:
                e.scalar_tensor_tensor(out=neg_max[p][:, :].rearrange("p (c t) -> p c t", c=2), in0=row_max[p][:, :].rearrange("p (c t) -> p c t", c=2), scalar=1.0, in1=sink, op0=ALU.mult, op1=ALU.max)\
                    .then_inc(sink_max, 1)
                e.wait_ge(sink_max, 2 * (g - PAIRS["C"]) + 1)
                e.tensor_scalar(neg_max[p][:, :], neg_max[p][:, :], -scale, None, ALU.mult).then_inc(sink_max, 1)
                e.wait_ge(sink_max, 2 * (g - PAIRS["C"]) + 2)
                e.tensor_tensor(sink_e[p][:, :].rearrange("p (c t) -> p c t", c=2), neg_max[p][:, :].rearrange("p (c t) -> p c t", c=2),
                                sink, ALU.add).then_inc(max_done, 1)
            else:
                e.tensor_scalar(neg_max[p][:, :], row_max[p][:, :], -scale, None, ALU.mult).then_inc(max_done, 1)

        def probs_act(e, g, p, scale=1.0, sink=False):
            e.wait_ge(max_done, g + 1)
            if isinstance(g, int) and g < PAIRS["B"] + 2:
                wait_from(e, diff_done, g - 1)
            else:
                e.wait_ge(inv_done, g - 1 - PAIRS["B"])
            for c in range(2):
                for t, cols in ((1, slice(0, 256)), (0, slice(256, 384))):
                    j = 2 * c + t
                    last = e.activation(sc[p][c][:, cols], sc[p][c][:, cols], ACT.Exp, bias=neg_max[p][:, j:j + 1],
                                        scale=scale, accum_out=row_sum[p][:, j:j + 1])
            if sink:
                last = e.activation(sink_e[p][:, :], sink_e[p][:, :], ACT.Exp)
            last.then_inc(probs_done, 1)

        def turn_probs_pe(e, g, p, ready, value, comps=2):
            e.wait_ge(ready, value)
            for c in range(comps):
                for m in range(3):
                    last = e.transpose(score_bank(g, p, c)[:, m * P:(m + 1) * P], sc[p][c][:, m * P:(m + 1) * P], ident[:, :])
            last.then_inc(probs_turned, 1)

        def pt_evac_dve(e, g, p):
            e.wait_ge(probs_turned, g + 1)
            wait_from(e, attended, g - 1)
            e.tensor_copy(pT[p][:, 0, :], score_bank(g, p, 0)[:, 0:384]).then_inc(pt_dve, 1)

        def pt_evac_act(e, g, p):
            e.wait_ge(probs_turned, g + 1)
            wait_from(e, attended, g - 1)
            e.activation(pT[p][:, 1, :], score_bank(g, p, 1)[:, 0:384], ACT.Copy).then_inc(pt_act, 1)

        def attend_pe(e, g, p, value, width=HD, comps=2):
            e.wait_ge(pt_dve, g + 1)
            if comps == 2:
                e.wait_ge(pt_act, g + 1 - PAIRS["B"])
            wait_from(e, heads_out, before(g))
            for c in range(comps):
                for t in range(T):
                    dst = out_bank(g, p)[:, (2 * c + t) * width:(2 * c + t + 1) * width]
                    if t == 0:
                        last = e.matmul(dst, pT[p][:, c, 256:384], value(c, 0), start=True, stop=True)
                    else:
                        e.matmul(dst, pT[p][:, c, 0:P], value(c, 0), start=True, stop=False)
                        last = e.matmul(dst, pT[p][:, c, P:2 * P], value(c, 1), start=False, stop=True)
            last.then_inc(attended, 1)

        def inv_sum_dve(e, g, p, sink=False):
            e.wait_ge(probs_done, g + 1)
            wait_from(e, heads_out, g - 1)
            if sink:
                e.tensor_tensor(row_sum[p][:, :], row_sum[p][:, :], sink_e[p][:, :], ALU.add).then_inc(sink_sum, 1)
                e.wait_ge(sink_sum, g - PAIRS["C"] + 1)
            e.reciprocal(inv_sum[p][:, :], row_sum[p][:, :]).then_inc(inv_done, 1)

        def heads_out_dve(e, g, p, dst):
            e.wait_ge(inv_done, g + 1 - PAIRS["B"])
            e.wait_ge(attended, g + 1)
            e.tensor_tensor(dst, out_bank(g, p)[:, 0:256].rearrange("p (c t d) -> p c t d", c=2, t=T),
                            inv_sum[p][:, :].rearrange("p (c t) -> p c t", c=2).unsqueeze(3).to_broadcast([P, 2, T, HD]),
                            ALU.mult).then_inc(heads_out, 1)

        sink_max, sink_sum = sem("sink_max"), sem("sink_sum")

        def staging(buf):
            return buf[:, 0:256].rearrange("p (t c d) -> p t c d", t=T, c=2)

        def heads2(v, c0, step):
            if step == HD:
                return v[:, :, bass.ds(c0, 2 * HD)].rearrange("p t (c d) -> p t c d", c=2)
            return v[:, :, bass.ds(c0, 2 * step)].rearrange("p t (c s) -> p t c s", c=2)[:, :, :, 0:HD]

        def bcast64(a):
            return a.unsqueeze(3).to_broadcast([P, T, 2, HD])

        def static_pair(kind, i):
            if kind in ("A", "B"):
                o = 0 if kind == "A" else 2048
                st = rstd[STATS[kind]][:, :].rearrange("p (t g) -> p t g", t=T)
                return (heads2(z_even, o + 128 * i, HD), st[:, :, 2 * i:2 * i + 2],
                        heads2(z_even, o + 512 + 128 * i, HD), st[:, :, 8 + 2 * i:10 + 2 * i])
            st = rstd[STATS[kind]][:, :].rearrange("p (t g) -> p t g", t=T)
            if kind == "C":
                return (heads2(z_odd, 64 * i, 256), st[:, :, i:i + 5:4], heads2(z_odd, 512, HD), st[:, :, 8:10])
            return (heads2(z_odd, 1280 + 128 * i, HD), st[:, :, 2 * i:2 * i + 2],
                    heads2(z_odd, 1792 + 128 * i, HD), st[:, :, 8 + 2 * i:10 + 2 * i])

        def static_biases(kind, i):
            if kind == "A":
                return [(bias_a[:, i, :], bias_a[:, i, P:])] * 2
            if kind == "B":
                return [(bias_b[:, 2 * i + c, 0:256], bias_b[:, 2 * i + c, 256:384]) for c in range(2)]
            if kind == "C":
                return [(bias_c[:, i + 4 * c, :], bias_c[:, i + 4 * c, P:]) for c in range(2)]
            return [(bias_d[:, 2 * i + c, :], bias_d[:, 2 * i + c, P:]) for c in range(2)]

        def static_value(kind, i):
            if kind == "A":
                return lambda c, t: z_even[:, t, 1024 + 128 * i:1152 + 128 * i]
            if kind == "B":
                return lambda c, t: z_even[:, t, 3072 + 128 * i + 64 * c:3136 + 128 * i + 64 * c]
            if kind == "C":
                return lambda c, t: z_odd[:, t, 640 + 64 * c:704 + 64 * c]
            return lambda c, t: z_odd[:, t, 2304 + 128 * i + 64 * c:2368 + 128 * i + 64 * c]

        def static_out(kind, i):
            if kind == "B":
                v = mix[:, :, 512 + 128 * i:640 + 128 * i].rearrange("p t (c d) -> p c t d", c=2)
            elif kind == "C":
                v = mix[:, :, 0:512].rearrange("p t (c s) -> p c t s", c=2)[:, :, :, 64 * i:64 * i + 64]
            else:
                v = mix[:, :, 512 + 128 * i:640 + 128 * i].rearrange("p t (c d) -> p c t d", c=2)
            return v

        def static_pairs(kinds):
            return [(k, i, PAIRS[k] + i) for k in kinds for i in range(4)]

        FIRST_FILL = {"AB": first["even_in"] + 4, "CD": first["odd_in"] + 3}
        SLOTS = {"AB": [(4, 2), (4, 1), (4, 2), (5, 2)] + [(3, 1)] * 3 + [(4, 0)], "CD": [(3, 1)] * 7 + [(4, 0)]}
        SPLITS = {"AB": {0: 1, 1: 2, 3: 3, 4: 4, 6: 5}, "CD": {0: 1, 3: 2, 4: 3, 6: 4}}
        LATE = {"AB": (1, 3), "CD": ()}

        def slot_pieces(kinds, n, which):
            at = sum(sum(s) for s in SLOTS[kinds][:n]) + (SLOTS[kinds][n][0] if which else 0)
            end, pieces = at + SLOTS[kinds][n][which], []
            while at < end:
                stop = min(end, (at // 8 + 1) * 8)
                pieces.append((FIRST_FILL[kinds] + at // 8, at % 8, at % 8 + stop - at))
                at = stop
            return pieces

        def slot_ends(kinds, n, which):
            return [u for u, _, e1 in slot_pieces(kinds, n, which) if e1 == 8]

        def sparse_value(i):
            return lambda c, t: z_dsa[:, t, bass.ds((i >> 2) * HD + (1280 + 128 * c), HD)]

        def latent_value(i):
            return lambda c, t: kv_full[:, t, bass.ds(i * 256 + (128 * c + 64), HD)]

        block = ctx.enter_context(nc.Block())

        @block.sync
        def _(sp):
            sp.dma_start(mix[0:GAIN_ROWS, 0, 0:P], gain_rows).then_inc(rows_loaded, 16)
            for t in range(T):
                sp.dma_start(x[:, t, :], x_in[t * P:(t + 1) * P, :]).then_inc(x_loaded, 16)
            load_unit(sp, 0)
            load_unit(sp, 1)
            sp.dma_start(rowp[:, :], row_params.partition_broadcast(P)).then_inc(params_loaded, 16)
            sp.dma_start(pos_i[:, :], positions).then_inc(pos_loaded, 16)

            def stream(u0, count, trips=0, per=2):
                if trips:
                    with sp.Fori(0, trips) as i:
                        for j in range(per):
                            load_unit(sp, u0 + j, i, per)
                else:
                    for j in range(count):
                        load_unit(sp, u0 + j)

            stream(2, first["even_out"])
            stream(first["odd_in"], 2)
            sp.wait_ge(max_done, PAIRS["B"] + 4)
            sp.dma_start(tab[:, 2048:4096], rel_band.rearrange("p h j -> p (h j)")).then_inc(band_loaded, 16)
            stream(first["odd_in"] + 2, 8)
            stream(first["dsa_in"] + 1, 7)
            for m in range(2):
                u = first[f"mlp{m}"]
                stream(u + 1, 12, trips=3, per=4)
                stream(u + 13, 3)
                if m == 0:
                    stream(u + 16, first["mlp1"] + 1 - (u + 16))
            sp.wait_ge(heads_out, PAIRS["L"] + 8)
            sp.dma_start(g_final[:, :], final_gain.partition_broadcast(P)).then_inc(final_loaded, 16)
            for t in range(T):
                sp.wait_ge((final_act, final_dve)[t], 1)
                sp.dma_start(out[t * P:(t + 1) * P, :], mix[:, t, :]).then_inc(stored, 16)
            sp.wait_ge(stored, 32)

        @block.gpsimd
        def _(pool):
            order = Order(pool, pool_order)
            order.after(pool.memset(ident[:, :], 0.0))
            pool.affine_select(out=ident[:, :], in_=ident[:, :], compare_op=ALU.not_equal, fill=1.0, base=0,
                               pattern=[[-1, P]], channel_multiplier=1).then_inc(consts, 1)
            pool.memset(eps[:, :], EPS).then_inc(consts, 1)
            order.after(pool.memset(upper, 1.0))
            for t in range(T):
                order.after(pool.affine_select(out=upper[:, t, :], in_=upper[:, t, :], compare_op=ALU.is_ge, fill=0.0,
                                               base=-P * t, pattern=[[1, SEQ]], channel_multiplier=-1))
            order.after(pool.memset(causal, 0.0))
            order.after(pool.affine_select(out=causal, in_=causal, compare_op=ALU.is_ge, fill=MASKED, base=P,
                                           pattern=[[-1, SEQ]], channel_multiplier=1))
            order.after(pool.memset(chunked[:, :], 0.0))
            order.after(pool.memset(chunked[0:64, 192:256], MASKED))
            nd = sc[0][0][:, 0:256]
            order.after(pool.iota(nd, pattern=[[-1, SEQ]], base=P, channel_multiplier=1, allow_small_or_imprecise_dtypes=True))
            nd2 = sc[0][1][:, 0:256]
            order.after(pool.tensor_scalar(nd2, nd, 0.0, None, ALU.max))
            order.after(pool.tensor_scalar(nd, nd, 0.0, None, ALU.min))
            order.after(pool.tensor_tensor(nd, nd, nd2, ALU.subtract))
            order.after(pool.memset(nd[0:64, 192:256], MASKED))
            for h in range(4):
                pool.tensor_scalar(bias_a[:, h, :], nd, 2.0 ** (-8.0 * (h + 1) / 4), None, ALU.mult).then_inc(even_tables, 1)
            pool.memset(g_mix[:, 4:KC], 0.5).then_inc(consts, 1)

            def stage_static(kinds):
                for kind, i, g in static_pairs(kinds):
                    q, rq, k, rk = static_pair(kind, i)
                    if i == 0:
                        pool.wait_ge(rstd_ready[STATS[kind]], 1)
                    stage_wait_pool(pool, g)
                    pool.tensor_tensor(staging(qs[g % 2]), q, bcast64(rq), ALU.mult)
                    pool.tensor_tensor(staging(ks[g % 2]), k, bcast64(rk), ALU.mult).then_inc(staged, 1)

            def gate_first(v, gate_unit, g0, heads_done, count, gain=None):
                th, gt = v[:, :, 0:512], v[:, :, g0:g0 + 512]
                pool.wait_ge(tanh_first, count)
                pool.wait_ge(evac_dve, dve_after[gate_unit])
                order.after(pool.tensor_scalar(th, th, 1.0, None, ALU.add))
                order.after(pool.tensor_tensor(th, th, gt, ALU.mult))
                if gain is not None:
                    heads = th.rearrange("p t (h d) -> p t h d", h=4)
                    pool.wait_ge(rstd_ready[gain], 1)
                    order.after(pool.tensor_tensor(heads, heads, rstd[gain][:, :].rearrange("p (t h) -> p t h", t=T)
                                                   .unsqueeze(3).to_broadcast([P, T, 4, P]), ALU.mult))
                pool.wait_ge(heads_out, heads_done)
                pool.tensor_tensor(mix[:, :, 0:512], mix[:, :, 0:512], th, ALU.mult).then_inc(first_gated, 1)

            stage_static("AB")
            gate_first(z_even, first["even_in"] + 7, 1536, PAIRS["A"] + 4, 1, gain=2)
            pool.wait_ge(max_done, PAIRS["B"] + 4)
            pool.wait_ge(heads_out, PAIRS["B"] + 4)
            order.after(pool.iota(nd, pattern=[[-1, SEQ]], base=P, channel_multiplier=1, allow_small_or_imprecise_dtypes=True))
            order.after(pool.tensor_scalar(nd2, nd, 0.0, None, ALU.max))
            order.after(pool.tensor_scalar(nd, nd, 0.0, None, ALU.min))
            order.after(pool.tensor_tensor(nd, nd, nd2, ALU.subtract))
            order.after(pool.memset(nd[0:64, 192:256], MASKED))
            order.after(pool.memset(nd[64:128, 0:64], MASKED))
            for h in range(8):
                pool.tensor_scalar(bias_c[:, h, :], nd, 2.0 ** -(h + 1), None, ALU.mult).then_inc(tables, 1)
            pool.wait_ge(band_loaded, 16)
            pool.tensor_tensor(bias_d[:, :, :], bias_d[:, :, :], chunked[:, :].unsqueeze(1).to_broadcast([P, 8, SEQ]),
                               ALU.add).then_inc(tables, 1)
            stage_static("CD")
            gate_first(z_odd, first["odd_in"] + 5, 768, PAIRS["C"] + 4, 2)
            pool.wait_ge(roped, 1)
            pool.wait_ge(qk_turned, PAIRS["S"])
            pool.tensor_copy(staging(ks[0]), z_dsa[:, :, 2048:2112].unsqueeze(2).to_broadcast([P, T, 2, HD])).then_inc(ki_staged, 1)
            pool.wait_ge(index_turned, 1)
            pool.wait_ge(roped, 2)
            for p in range(2):
                pool.tensor_copy(staging(ks[p]), heads2(z_dsa, 1024, P))
            pool.wait_ge(roped, 3)
            for p in range(2):
                pool.tensor_copy(staging(qs[p]), heads2(z_dsa, p * HD, 512)).then_inc(staged, 1)

            def stage_sparse(g, p, i):
                stage_wait_pool(pool, g)
                pool.tensor_copy(staging(qs[p]), heads2(z_dsa, i * HD, 512))
                pool.tensor_copy(staging(ks[p]), heads2(z_dsa, (i >> 2) * HD + 1024, P)).then_inc(staged, 1)

            with pool.Fori(0, 3) as i:
                for j in range(2):
                    stage_sparse(i * 2 + (PAIRS["S"] + 2 + j), j, i * 2 + (2 + j))
            pool.wait_ge(mla_roped, 1)
            for p in range(2):
                kbuf = ks_mla[p].rearrange("p (c t d) -> p c t d", c=2, t=T)
                for c in range(2):
                    ins = pool.tensor_copy(kbuf[:, c, :, HD:96], z_mla[:, :, 640:672])
            ins.then_inc(kr_staged, 1)

            def stage_latent(g, p, i):
                stage_wait_pool(pool, g)
                for buf, full, step, n in ((qs_mla[p], q_full, 96, 96), (ks_mla[p], kv_full, 128, 64)):
                    dst = buf.rearrange("p (c t d) -> p c t d", c=2, t=T)[:, :, :, 0:n]
                    src = full[:, :, bass.ds(i * (2 * step), 2 * step)].rearrange("p t (c s) -> p c t s", c=2)[:, :, :, 0:n]
                    last = pool.tensor_copy(dst, src)
                last.then_inc(staged, 1)

            for blocks, pairs in ((1, (0, 1)), (4, ())):
                pool.wait_ge(evac_act, act_after[first["kv_up"]] - 4 + blocks)
                pool.wait_ge(evac_dve, dve_after[first["kv_up"]] - 4 + blocks)
                for i in pairs:
                    stage_latent(PAIRS["L"] + i, i, i)
            with pool.Fori(0, 3) as i:
                for j in range(2):
                    stage_latent(i * 2 + (PAIRS["L"] + 2 + j), j, i * 2 + (2 + j))

        @block.tensor
        def _(pe):
            pe.wait_ge(consts, 1)
            pe.wait_ge(rows_loaded, 16)
            pe.transpose(bank[0][:, 0:GAIN_ROWS], mix[0:GAIN_ROWS, 0, 0:P], ident[0:GAIN_ROWS, 0:GAIN_ROWS]).then_inc(gains_turned, 1)

            def project(u0, count, chunk0=0, fresh=None):
                for j in range(count):
                    unit_pe(pe, u0 + j, chunk0=chunk0, fresh=None if j else fresh)

            def turn_x(name, half):
                s, value = X_READY[name]
                pe.wait_ge(s, value - (1 - half) if name != "even" else value)
                if s is x_ready and not half:
                    turn_pe(pe, name, x, 0, 2)
                    pe.wait_ge(s, value)
                    turn_pe(pe, name, x, 2, 4)
                else:
                    turn_pe(pe, name, x, 4 * half, 4 * half + 4)

            def first_from_x(u, name):
                turn_x(name, 0)
                first_unit_pe(pe, u, name, lambda: turn_x(name, 1))

            def static_attention(kinds):
                pairs = static_pairs(kinds)

                def turn_probs(kind, i, g):
                    if kind == "A":
                        turn_probs_pe(pe, g, g % 2, diff_done, g + 1, comps=1)
                    else:
                        turn_probs_pe(pe, g, g % 2, probs_done, g + 1)

                def attend(kind, i, g):
                    if kind == "A":
                        attend_pe(pe, g, g % 2, static_value(kind, i), width=P, comps=1)
                    else:
                        attend_pe(pe, g, g % 2, static_value(kind, i))

                def fill(n, which):
                    for u, e0, e1 in slot_pieces(kinds, n, which):
                        unit_eighths_pe(pe, u, e0, e1)

                turn_qk_pe(pe, pairs[0][2], 0)
                for n, (kind, i, g) in enumerate(pairs):
                    scores_pe(pe, g, g % 2)
                    if n:
                        attend(*pairs[n - 1])
                    fill(n, 0)
                    if n + 1 < len(pairs):
                        turn_qk_pe(pe, g + 1, (g + 1) % 2)
                    turn_probs(kind, i, g)
                    fill(n, 1)

                name, g = {"AB": "even_mix", "CD": "odd_mix"}[kinds], pairs[-1][2]
                layer = 1 if kinds == "AB" else 2
                pe.wait_ge(first_gated, layer)
                turn_pe(pe, name, mix, 0, 2)
                attend(*pairs[-1])
                turn_pe(pe, name, mix, 2, 4)

                def turn_rest():
                    pe.wait_ge(mix_ready, 2 * layer - 1)
                    turn_pe(pe, name, mix, 4, 6)
                    pe.wait_ge(mix_ready, 2 * layer)
                    turn_pe(pe, name, mix, 6, 8)

                first_unit_pe(pe, FIRST_FILL[kinds] + len(SPLITS[kinds]), name, turn_rest)

            turn_x("even", 0)
            turn_x("even", 1)
            unit_pe(pe, 0, fresh="even")
            unit_pe(pe, 1)
            pe.wait_ge(forget_ready, 1)
            pe.wait_ge(even_tables, 4)
            for t in range(T):
                for s in range(t + 1):
                    last = pe.matmul(bank[1][:, 256 + 8 * t:264 + 8 * t], upper[:, s, t * P:(t + 1) * P], logf[:, 3, s, :],
                                     start=(s == 0), stop=(s == t))
            last.then_inc(cum_done, 1)
            for h in range(8):
                for t in range(T):
                    for s in range(t + 1):
                        last = pe.matmul(bank[4 + h // 2][:, (h % 2) * SEQ + t * P:(h % 2) * SEQ + (t + 1) * P],
                                         qkT[s][:, h * P:(h + 1) * P], upper[:, s, t * P:(t + 1) * P],
                                         start=(s == 0), stop=(s == t))
            last.then_inc(cum_done, 1)
            unit_eighths_pe(pe, 2, 0, 4)
            pe.wait_ge(cum_ready, 1)
            unit_eighths_pe(pe, 2, 4, 8)
            unit_pe(pe, 3)
            pe.wait_ge(bias_ready, 1)
            static_attention("AB")
            unit_pe(pe, first["even_out"] + 1)
            first_from_x(first["odd_in"], "odd")
            unit_pe(pe, first["odd_in"] + 1)
            unit_pe(pe, first["odd_in"] + 2)
            static_attention("CD")
            unit_pe(pe, first["odd_out"] + 1)
            u = first["dsa_in"]
            first_from_x(u, "dsa")
            project(u + 1, 1)
            unit_eighths_pe(pe, u + 2, 0, 4)
            pe.wait_ge(roped, 1)
            for i in range(4):
                for t in range(T):
                    pe.transpose(bank[4 + i // 2][:, (i % 2) * SEQ + t * P:(i % 2) * SEQ + (t + 1) * P],
                                 z_dsa[:, t, 1536 + P * i:1536 + P * (i + 1)], ident[:, :])
            pe.wait_ge(ki_staged, 1)
            for t in range(T):
                last = pe.transpose(bank[6][:, t * P:(t + 1) * P], ks[0][:, t * P:(t + 1) * P], ident[:, :])
            last.then_inc(index_turned, 1)
            unit_eighths_pe(pe, u + 2, 4, 8)

            def logits(heads):
                for h in heads:
                    if h >= 4:
                        pe.wait_ge(logits_relu, h - 3)
                    q = qiT[(h % 2) * HD:(h % 2 + 1) * HD, h // 2, :]
                    k = kiT[(h % 2) * HD:(h % 2 + 1) * HD, :]
                    pe.matmul(bank[4 + h % 4][:, 0:256], q[:, P:2 * P], k, start=True, stop=True)
                    pe.matmul(bank[4 + h % 4][:, 256:384], q[:, 0:P], k[:, 0:P], start=True, stop=True).then_inc(logits_done, 1)

            pe.wait_ge(index_ready, 1)
            logits(range(4))
            unit_eighths_pe(pe, u + 3, 0, 3)
            logits(range(4, 8))
            unit_eighths_pe(pe, u + 3, 3, 8)
            project(u + 4, 1)
            pe.wait_ge(logits_relu, 8)

            def looped_attention(first_pair, value, mla):
                turn = turn_qk_mla_pe if mla else turn_qk_pe
                turn(pe, first_pair, 0)
                turn(pe, first_pair + 1, 1)
                scores_pe(pe, first_pair, 0, mla)

                def step(g, p, value_before, scores=True, turns=True):
                    if scores:
                        scores_pe(pe, g + 1, 1 - p, mla)
                    turn_probs_pe(pe, g, p, probs_done, g + 1)
                    if turns:
                        turn(pe, g + 2, p)
                    if value_before is not None:
                        attend_pe(pe, g - 1, 1 - p, value_before)

                step(first_pair, 0, None)
                step(first_pair + 1, 1, value(0))
                with pe.Fori(0, 2) as i:
                    for j in range(2):
                        step(i * 2 + (first_pair + 2 + j), j, value(i * 2 + (1 + j)))
                step(first_pair + 6, 0, value(5), turns=False)
                step(first_pair + 7, 1, value(6), scores=False, turns=False)
                attend_pe(pe, first_pair + 7, 1, value(7))

            looped_attention(PAIRS["S"], sparse_value, False)
            pe.wait_ge(heads_out, PAIRS["S"] + 8)
            turn_pe(pe, "dsa_mix", mix)
            project(first["dsa_out"], 2, fresh="dsa_mix")

            def mlp(m):
                name, u = f"mlp{m}", first[f"mlp{m}"]
                turn_x(name, 0)

                def up(v, b, i=None):
                    slot = v % 2
                    hi = w_hi[slot][:, :].rearrange("p (k n) -> p k n", k=KC)
                    lo = w_lo[slot][:, :].rearrange("p (k n) -> p k n", k=KC)
                    wait_split(pe, lo_split, v, 0, i, 4)
                    relus = 2 * FF_BLOCKS * m + 2 * (b - 1)
                    if i is not None or b >= 2:
                        pe.wait_ge(relu_done, relus if i is None else i * 4 + relus)
                    parts = [(f, range(KC)) for f in range(4)]
                    if b == 0:
                        parts = [(0, range(4)), (2, range(4)), (0, range(4, KC)), (2, range(4, KC)), (1, range(KC)), (3, range(KC))]
                    for n, (f, rows) in enumerate(parts):
                        dst = up_bank(m, b, f // 2)[:, (f % 2) * SEQ:(f % 2 + 1) * SEQ]
                        if b == 0 and n == 1:
                            turn_x(name, 1)
                        for k in rows:
                            if k == 4 and n == (2 if b == 0 else 0):
                                wait_split(pe, lo_split, v, 1, i, 4)
                            if b == 0 and n in (0, 2):
                                pe.wait_ge(lo_turned, turn_base[name] + k // 2 + 1)
                            wh, wl = hi[:, k, f * P:(f + 1) * P], lo[:, k, f * P:(f + 1) * P]
                            pe.matmul(dst, wh, h_hi[:, k, :], start=(k == 0), stop=False)
                            pe.matmul(dst, wh, h_lo[:, k, :], start=False, stop=False)
                            last = pe.matmul(dst, wl, h_hi[:, k, :], start=False, stop=(k == KC - 1))
                        if f % 2:
                            last.then_inc(mm_done, 1)

                def down(v, b, i=None, begins=False, ends=False):
                    slot = v % 2
                    hi = w_hi[slot][:, :].rearrange("p (k n) -> p k n", k=4)
                    lo = w_lo[slot][:, :].rearrange("p (k n) -> p k n", k=4)
                    wait_split(pe, lo_split, v, 0, i, 4)
                    blocks_done = 2 * FF_BLOCKS * m + 2 * (b + 1)
                    pe.wait_ge(u_lo_done, blocks_done if i is None else i * 4 + blocks_done)
                    for c in range(4):
                        if c == 2:
                            wait_split(pe, lo_split, v, 1, i, 4)
                        for t in range(T):
                            uh, ul = u_hi[b % 2][:, c, t * P:(t + 1) * P], u_lo[b % 2][:, c, t * P:(t + 1) * P]
                            for half in range(2):
                                dst = bank[4 + 2 * t + half][:, :]
                                cols = slice(half * BLOCK, (half + 1) * BLOCK)
                                a, z_ = begins and c == 0, ends and c == 3
                                pe.matmul(dst, uh, hi[:, c, cols], start=a, stop=False, skip_group_check=True)
                                pe.matmul(dst, uh, lo[:, c, cols], start=False, stop=False, skip_group_check=True)
                                last = pe.matmul(dst, ul, hi[:, c, cols], start=False, stop=z_, skip_group_check=True)
                    last.then_inc(mm_done, 1)

                up(u, 0)
                up(u + 1, 1)
                down(u + 2, 0, begins=True)
                up(u + 3, 2)
                down(u + 4, 1)
                with pe.Fori(0, 2) as i:
                    up(u + 5, 3, i)
                    down(u + 6, 2, i)
                    up(u + 7, 4, i)
                    down(u + 8, 3, i)
                up(u + 13, 7)
                down(u + 14, 6)
                down(u + 15, 7, ends=True)

            mlp(0)
            first_from_x(first["mla_in"], "mla")
            project(first["mla_in"] + 1, 1)
            u = first["q_up"]
            pe.wait_ge(evac_act, act_after[u - 1])
            pe.wait_ge(evac_dve, dve_after[u - 1])
            turn_pe(pe, "latent", z_mla)
            project(u, 2, fresh="latent")
            wait_turned(pe, "latent")
            project(first["kv_up"], 1, chunk0=Q_LORA // P)
            pe.wait_ge(kr_staged, 1)
            pe.wait_ge(evac_act, act_after[first["kv_up"]])
            pe.wait_ge(evac_dve, dve_after[first["kv_up"]])
            looped_attention(PAIRS["L"], latent_value, True)
            pe.wait_ge(heads_out, PAIRS["L"] + 8)
            turn_pe(pe, "mla_mix", mix)
            project(first["mla_out"], 2, fresh="mla_mix")
            mlp(1)

        @block.scalar
        def _(act):
            order = Order(act, act_order)
            split_hi(act, 0)
            act.wait_ge(gains_ready, 1)

            def project(u0, count, dst, scale):
                for j in range(count):
                    split_hi(act, u0 + j + 1)
                    unit_z_act(act, u0 + j, dst, scale)

            def project_x(u0):
                for j in range(2):
                    split_hi(act, u0 + j + 1)

            def first_unit(name, r, u, dst):
                turn_act(act, name)
                split_hi(act, u + 1)
                act.wait_ge(*X_READY[name])
                x_squares_act(act, r)
                guess_act(act, order, r)
                act.wait_ge(rstd_ready[r], 1)
                unit_z_act(act, u, dst, rstd[r][:, 0:1])

            def static_attention(kinds, scales):
                pairs = static_pairs(kinds)

                dst, r = (z_even, 0) if kinds == "AB" else (z_odd, 3)
                qk_evac_act(act, pairs[0][2], 0, scales(pairs[0][0]))
                for n, (kind, i, g) in enumerate(pairs):
                    if n in SPLITS[kinds] and n not in LATE[kinds]:
                        split_hi(act, FIRST_FILL[kinds] + SPLITS[kinds][n])
                    probs_act(act, g, g % 2, sink=kind == "C")
                    for u in slot_ends(kinds, n, 0):
                        unit_z_act(act, u, dst, rstd[r][:, 0:1])
                    if n in LATE[kinds]:
                        split_hi(act, FIRST_FILL[kinds] + SPLITS[kinds][n])
                    if n + 1 < len(pairs):
                        qk_evac_act(act, g + 1, (g + 1) % 2, scales(pairs[n + 1][0]))
                    if kind != "A":
                        pt_evac_act(act, g, g % 2)
                    for u in slot_ends(kinds, n, 1):
                        unit_z_act(act, u, dst, rstd[r][:, 0:1])
                    beside_act(kinds, n)
                tanh_act(kinds, 1)

            def squares_act(v, c0, n, unit, at):
                act.wait_ge(evac_act, act_after[unit])
                act.wait_ge(evac_dve, dve_after[unit])
                act.activation(mix[:, :, at:at + n], v[:, :, c0:c0 + n], ACT.Square, scale=HD ** -0.5).then_inc(squares_ready, 1)

            def tanh_act(kinds, half):
                v, spots = (z_even, ((1536, 0), (3584, 2048))) if kinds == "AB" else (z_odd, ((768, 0), (2816, 1280)))
                unit = FIRST_FILL[kinds] + (3, 4)[half] - (kinds == "CD")
                src, to = spots[half]
                act.wait_ge(evac_act, act_after[unit])
                act.wait_ge(evac_dve, dve_after[unit])
                act.activation(v[:, :, to:to + 512], v[:, :, src:src + 512], ACT.Tanh, scale=0.5)\
                    .then_inc((tanh_first, tanh_second)[half], 1)

            def beside_act(kinds, n):
                if kinds == "AB":
                    if n == 1:
                        squares_act(z_even, 2048, 512, FIRST_FILL[kinds], 512)
                    if n == 2:
                        act.wait_ge(squares_read, 1)
                        squares_act(z_even, 2560, 512, FIRST_FILL[kinds] + 1, 512)
                        guess_act(act, order, 11)
                    if n == 4:
                        act.wait_ge(heads_out, PAIRS["A"] + 4)
                        act.activation(z_even[:, :, 512:1024], mix[:, :, 0:512], ACT.Square, scale=P ** -0.5).then_inc(squares_ready, 1)
                        guess_act(act, order, 2)
                if kinds == "CD":
                    if n == 0:
                        squares_act(z_odd, 1280, 512, FIRST_FILL[kinds] - 1, 512)
                    if n == 1:
                        act.wait_ge(squares_read, 2)
                        squares_act(z_odd, 1792, 512, FIRST_FILL[kinds], 512)
                        guess_act(act, order, 12)
                if n == 5:
                    tanh_act(kinds, 0)

            act.wait_ge(gains_turned, 1)
            act.wait_ge(consts, 2)
            first_unit("even", 0, 0, z_even)
            act.wait_ge(forget_in, 1)
            order.after(act.activation(logf[:, 2, :, :], logf[:, 1, :, :], ACT.Exp))
            act.activation(logf[:, 2, :, :], logf[:, 2, :, :], ACT.Ln, bias=1.0).then_inc(forget_log, 1)
            act.wait_ge(lam_in, 1)
            act.activation(lam_dot[:, :], lam_dot[:, :], ACT.Exp).then_inc(lam_exp, 1)
            project(1, 1, z_even, rstd[0][:, 0:1])
            squares_act(z_even, 0, 512, 1, 0)
            act.wait_ge(trig_in, 1)
            act.activation(sine[:, :, :], angle[:, :, :], ACT.Sin)
            act.activation(cosine[:, :, :], turns[:, :, :], ACT.Sin).then_inc(trig_ready, 1)
            project(2, 1, z_even, rstd[0][:, 0:1])
            squares_act(z_even, 512, 512, 2, 512)
            guess_act(act, order, 1)
            project(3, 1, z_even, rstd[0][:, 0:1])
            act.wait_ge(gains_ready, 2)
            act.wait_ge(consts, 3)
            static_attention("AB", lambda kind: g_qk[:, "ABCD".index(kind):"ABCD".index(kind) + 1])
            turn_act(act, "even_mix")
            project_x(first["even_out"])
            first_unit("odd", 3, first["odd_in"], z_odd)
            project(first["odd_in"] + 1, 1, z_odd, rstd[3][:, 0:1])
            squares_act(z_odd, 0, 640, first["odd_in"] + 1, 0)
            guess_act(act, order, 4)
            project(first["odd_in"] + 2, 1, z_odd, rstd[3][:, 0:1])
            static_attention("CD", lambda kind: g_qk[:, "ABCD".index(kind):"ABCD".index(kind) + 1])
            turn_act(act, "odd_mix")
            project_x(first["odd_out"])
            u = first["dsa_in"]
            first_unit("dsa", 5, u, z_dsa)
            project(u + 1, 1, z_dsa, rstd[5][:, 0:1])
            act.wait_ge(index_turned, 1)
            act.activation(qiT[:, 0:2, :], bank[4][:, :].rearrange("p (i q) -> p i q", i=2), ACT.Copy)
            act.activation(qiT[:, 2:4, :], bank[5][:, :].rearrange("p (i q) -> p i q", i=2), ACT.Copy)
            act.activation(kiT, bank[6][:, 0:256], ACT.Copy).then_inc(index_ready, 1)

            def logits(heads):
                for h in heads:
                    act.wait_ge(logits_done, h + 1)
                    if h >= 2:
                        act.wait_ge(logits_added, h - 1)
                    act.activation(rl[:, h % 2, :], bank[4 + h % 4][:, 0:384], ACT.Relu).then_inc(logits_relu, 1)

            split_hi(act, u + 3)
            unit_z_act(act, u + 2, z_dsa, rstd[5][:, 0:1])
            logits(range(4))
            split_hi(act, u + 4)
            logits(range(4, 8))
            unit_z_act(act, u + 3, z_dsa, rstd[5][:, 0:1])
            project(u + 4, 1, z_dsa, rstd[5][:, 0:1])

            def looped_attention(first_pair, mla, scale):
                evac = (lambda g, p: qk_evac_mla_act(act, g, p)) if mla else (lambda g, p: qk_evac_act(act, g, p, HD ** -0.5))
                evac(first_pair, 0)
                evac(first_pair + 1, 1)
                probs_act(act, first_pair, 0, scale)

                def step(g, p, turns=True, probs=True):
                    pt_evac_act(act, g, p)
                    if turns:
                        evac(g + 2, p)
                    if probs:
                        probs_act(act, g + 1, 1 - p, scale)

                with act.Fori(0, 3) as i:
                    for j in range(2):
                        step(i * 2 + (first_pair + j), j)
                step(first_pair + 6, 0, turns=False)
                step(first_pair + 7, 1, turns=False, probs=False)

            looped_attention(PAIRS["S"], False, 1.0)
            turn_act(act, "dsa_mix")
            project_x(first["dsa_out"])

            def mlp(m):
                r, u = (6, 9)[m], first[f"mlp{m}"]
                turn_act(act, f"mlp{m}")
                split_hi(act, u + 1)
                act.wait_ge(*X_READY[f"mlp{m}"])
                x_squares_act(act, r)
                guess_act(act, order, r)

                def up(v, b, i=None):
                    if b:
                        split_hi(act, v + 1, i, 4)
                    for j in range(2):
                        act.wait_ge(mm_done, mm_value(v, j, i, 4))
                        act.activation(relu[j][:, :], up_bank(m, b, j)[:, :], ACT.Relu).then_inc(relu_done, 1)
                    for j in range(2):
                        done = 2 * FF_BLOCKS * m + 2 * b + j + 1
                        act.wait_ge(sq_done, done if i is None else i * 4 + done)
                        act.activation(u_hi[b % 2][:, 2 * j:2 * j + 2, :], sq[j][:, :].rearrange("p (f q) -> p f q", f=2),
                                       ACT.Copy).then_inc(u_hi_done, 1)

                up(u, 0)
                up(u + 1, 1)
                split_hi(act, u + 3)
                up(u + 3, 2)
                split_hi(act, u + 5)
                with act.Fori(0, 2) as i:
                    up(u + 5, 3, i)
                    split_hi(act, u + 7, i, 4)
                    up(u + 7, 4, i)
                    split_hi(act, u + 9, i, 4)
                up(u + 13, 7)
                split_hi(act, u + 15)
                split_hi(act, u + 16)

            mlp(0)
            first_unit("mla", 7, first["mla_in"], z_mla)
            project(first["mla_in"] + 1, 1, z_mla, rstd[7][:, 0:1])
            act.wait_ge(evac_dve, dve_after[first["q_up"] - 1])
            act.wait_ge(evac_act, act_after[first["q_up"] - 1])
            turn_act(act, "latent")
            for t in range(T):
                act.activation(mix[:, t, 0:Q_LORA], z_mla[:, t, 0:Q_LORA], ACT.Square, scale=Q_LORA ** -0.5,
                               accum_out=ms[8][:, t:t + 1])
                ins = act.activation(mix[:, t, Q_LORA:640], z_mla[:, t, Q_LORA:640], ACT.Square, scale=KV_LORA ** -0.5,
                                     accum_out=ms[8][:, 2 + t:3 + t])
            ins.then_inc(ms_ready[8], 1)
            guess_act(act, order, 8)
            split_hi(act, first["q_up"] + 1)
            act.wait_ge(rstd_ready[8], 1)
            unit_z_act(act, first["q_up"], q_full, rstd[8][:, 0:1])
            project(first["q_up"] + 1, 1, q_full, rstd[8][:, 0:1])
            unit_z_act(act, first["kv_up"], kv_full, rstd[8][:, 2:3], (0, 1))
            split_hi(act, first["mla_out"], halves=(0,))
            unit_z_act(act, first["kv_up"], kv_full, rstd[8][:, 2:3], (2,))
            split_hi(act, first["mla_out"], halves=(1,))
            unit_z_act(act, first["kv_up"], kv_full, rstd[8][:, 2:3], (3,))
            looped_attention(PAIRS["L"], True, 96 ** -0.5)
            turn_act(act, "mla_mix")
            project_x(first["mla_out"])
            mlp(1)
            order.after(act.activation(r_log[:, 0:1], eps[:, 0:1], ACT.Ln))
            act.wait_ge(*X_READY["final"])
            act.activation(h_hi[:, 0:4, :], x[:, 0, :].rearrange("p (k n) -> p k n", k=4), ACT.Square, scale=DM ** -0.5,
                           accum_out=ms[10][:, 0:1]).then_inc(act_order, 1)
            order.n += 1
            act.wait_ge(act_order, order.n)
            guess_act(act, order, 10)
            act.wait_ge(rstd_ready[10], 1)
            act.wait_ge(gained, 1)
            act.activation(mix[:, 0, :], mix[:, 0, :], ACT.Copy, scale=rstd[10][:, 0:1]).then_inc(final_act, 1)

        @block.vector
        def _(dve):
            order = Order(dve, dve_order)
            dve.wait_ge(gains_turned, 1)
            dve.tensor_copy(gcols[:, :], bank[0][:, 0:GAIN_ROWS]).then_inc(gains_ready, 1)
            dve.wait_ge(gains_ready, 1)
            dve.tensor_scalar(g_mix[:, 0:4], gcols[:, G_SUB:G_SUB + 1].to_broadcast([P, 4]), 0.5 * (1.0 - LAM_INIT), None, ALU.mult)
            for j in range(4):
                ins = dve.tensor_scalar(g_qk[:, j:j + 1], gcols[:, G_HEAD + 2 * j:G_HEAD + 2 * j + 1],
                                        gcols[:, G_HEAD + 2 * j + 1:G_HEAD + 2 * j + 2], HD ** -0.5, ALU.mult, ALU.mult)
            ins.then_inc(gains_ready, 1)
            split_lo(dve, 0)
            def project(u0, count, dst, scale):
                for j in range(count):
                    split_lo(dve, u0 + j + 1)
                    unit_z_dve(dve, u0 + j, dst, scale)

            def project_x(u0):
                for j in range(2):
                    split_lo(dve, u0 + j + 1)
                    unit_x_dve(dve, u0 + j)

            def first_unit(name, r, u, dst):
                turn_dve(dve, name)
                split_lo(dve, u + 1)
                newton_dve(dve, order, r)
                dve.wait_ge(rstd_ready[r], 1)
                unit_z_dve(dve, u, dst, rstd[r][:, 1:2])

            def static_attention(kinds):
                pairs = static_pairs(kinds)

                def maxima(kind, i, g):
                    sink = None
                    if kind == "C":
                        sink = rowp[:, R_SINK + i:R_SINK + i + 5:4].unsqueeze(2).to_broadcast([P, 2, T])
                    row_max_dve(dve, g, g % 2, static_biases(kind, i), sink=sink)

                def difference(i, g):
                    p = g % 2
                    dve.wait_ge(probs_done, g + 1)
                    order.after(dve.reciprocal(inv_sum[p][:, :], row_sum[p][:, :]))
                    order.after(dve.tensor_tensor(inv_sum[p][:, :], inv_sum[p][:, :], lam4[:, :], ALU.mult))
                    for t, cols in ((1, slice(0, 256)), (0, slice(256, 384))):
                        ins = dve.tensor_scalar(sc[p][1][:, cols], sc[p][1][:, cols], inv_sum[p][:, 2 + t:3 + t], None, ALU.mult)
                    order.after(ins)
                    for t, cols in ((1, slice(0, 256)), (0, slice(256, 384))):
                        ins = dve.scalar_tensor_tensor(out=sc[p][0][:, cols], in0=sc[p][0][:, cols], scalar=inv_sum[p][:, t:t + 1],
                                                       in1=sc[p][1][:, cols], op0=ALU.mult, op1=ALU.add)
                    ins.then_inc(diff_done, 1)

                def probs_out(kind, i, g):
                    if kind == "A":
                        difference(i, g)
                        pt_evac_dve(dve, g, g % 2)
                    else:
                        pt_evac_dve(dve, g, g % 2)
                        inv_sum_dve(dve, g, g % 2, sink=kind == "C")

                def out(kind, i, g):
                    p = g % 2
                    if kind == "A":
                        dve.wait_ge(attended, g + 1)
                        dve.tensor_copy(mix[:, :, 128 * i:128 * (i + 1)],
                                        out_bank(g, p)[:, 0:256].rearrange("p (t e) -> p t e", t=T)).then_inc(heads_out, 1)
                        return
                    heads_out_dve(dve, g, p, static_out(kind, i))

                dst, r = (z_even, 0) if kinds == "AB" else (z_odd, 3)
                for n, (kind, i, g) in enumerate(pairs):
                    maxima(kind, i, g)
                    if n:
                        out(*pairs[n - 1])
                    u = FIRST_FILL[kinds] + SPLITS[kinds].get(n, 0)
                    early = n in SPLITS[kinds] and n not in LATE[kinds]
                    if early:
                        split_lo_half(dve, u, 0)
                    for v in slot_ends(kinds, n, 0):
                        unit_z_dve(dve, v, dst, rstd[r][:, 1:2])
                    beside_dve(kinds, n, 0)
                    probs_out(kind, i, g)
                    if early:
                        split_lo_half(dve, u, 1)
                    for v in slot_ends(kinds, n, 1):
                        unit_z_dve(dve, v, dst, rstd[r][:, 1:2])
                    if n in LATE[kinds]:
                        split_lo_half(dve, u, 0)
                        split_lo_half(dve, u, 1)
                    beside_dve(kinds, n, 1)
                v, th0, g0 = (z_even, 2048, 3584) if kinds == "AB" else (z_odd, 1280, 2816)
                th = v[:, :, th0:th0 + 512]
                dve.wait_ge(tanh_second, 1 if kinds == "AB" else 2)
                order.after(dve.scalar_tensor_tensor(out=th, in0=th, scalar=1.0, in1=v[:, :, g0:g0 + 512],
                                                     op0=ALU.add, op1=ALU.mult))
                turn_dve(dve, {"AB": "even_mix", "CD": "odd_mix"}[kinds], 0, 4)
                dve.tensor_tensor(mix[:, :, 512:768], mix[:, :, 512:768], th[:, :, 0:256], ALU.mult).then_inc(mix_ready, 1)
                out(*pairs[-1])
                dve.wait_ge(heads_out, pairs[-1][2] + 1)
                dve.tensor_tensor(mix[:, :, 768:1024], mix[:, :, 768:1024], th[:, :, 256:512], ALU.mult).then_inc(mix_ready, 1)

            def group_sums(r, at, src, groups, width, squares):
                dve.wait_ge(squares_ready, squares)
                return dve.tensor_reduce(ms[r][:, :].rearrange("p (t g) -> p t g", t=T)[:, :, at:at + groups],
                                         src.rearrange("p t (g d) -> p t g d", d=width), AX.X, ALU.add)

            def beside_dve(kinds, n, late):
                at = (kinds, n, late)
                if at == ("AB", 2, 1):
                    group_sums(11, 0, mix[:, :, 512:1024], 8, HD, 3).then_inc(squares_read, 1)
                if at == ("AB", 2, 1):
                    group_sums(11, 8, mix[:, :, 512:1024], 8, HD, 4).then_inc(ms_ready[11], 1)
                if at == ("AB", 3, 0):
                    newton_dve(dve, order, 11)
                if at == ("AB", 4, 1):
                    group_sums(2, 0, z_even[:, :, 512:1024], 4, P, 5).then_inc(ms_ready[2], 1)
                if at == ("AB", 5, 0):
                    newton_dve(dve, order, 2)
                if at == ("CD", 0, 1):
                    group_sums(12, 0, mix[:, :, 512:1024], 8, HD, 7).then_inc(squares_read, 1)
                if at == ("CD", 1, 1):
                    group_sums(12, 8, mix[:, :, 512:1024], 8, HD, 8).then_inc(ms_ready[12], 1)
                if at == ("CD", 2, 0):
                    newton_dve(dve, order, 12)

            first_unit("even", 0, 0, z_even)
            dve.wait_ge(params_loaded, 16)
            for j in range(2):
                ins = dve.tensor_tensor_reduce(r_tmp[:, 0:HD], rowp[:, R_LAM + 128 * j:R_LAM + 128 * j + HD],
                                               rowp[:, R_LAM + 128 * j + HD:R_LAM + 128 * j + 2 * HD], 1.0, 0.0,
                                               ALU.mult, ALU.add, lam_dot[:, j:j + 1])
                if j == 0:
                    order.after(ins)
            ins.then_inc(lam_in, 1)
            dve.wait_ge(evac_act, act_after[0])
            dve.wait_ge(evac_dve, dve_after[0])
            order.after(dve.tensor_tensor(logf[:, 0, :, :], z_even[:, :, 4096:4104],
                                          rowp[:, R_FB:R_FB + 8].unsqueeze(1).to_broadcast([P, T, 8]), ALU.add))
            dve.scalar_tensor_tensor(out=logf[:, 1, :, :], in0=logf[:, 0, :, :], scalar=-1.0, in1=logf[:, 0, :, :],
                                     op0=ALU.mult, op1=ALU.min).then_inc(forget_in, 1)
            dve.wait_ge(forget_log, 1)
            order.after(dve.scalar_tensor_tensor(out=logf[:, 3, :, :], in0=logf[:, 0, :, :], scalar=0.0, in1=logf[:, 2, :, :],
                                                 op0=ALU.min, op1=ALU.subtract))
            for s in range(T):
                ins = dve.tensor_scalar(qkT[s][:, :].rearrange("p (h m) -> p h m", h=8),
                                        logf[:, 3, s, :].unsqueeze(2).to_broadcast([P, 8, P]), -1.0, None, ALU.mult)
            ins.then_inc(forget_ready, 1)
            dve.wait_ge(lam_exp, 1)
            order.after(dve.tensor_tensor(lam_diff[:, :], lam_dot[:, 1:2], lam_dot[:, 0:1], ALU.subtract))
            dve.memset(lam4[:, 0:2], 1.0)
            dve.tensor_scalar(lam4[:, 2:4], lam_diff[:, 0:1].to_broadcast([P, 2]), -LAM_INIT, None, ALU.add).then_inc(lam_ready, 1)
            dve.wait_ge(pos_loaded, 16)
            order.after(dve.tensor_copy(pos[:, :], pos_i[:, :]))
            for t in range(T):
                ins = dve.tensor_scalar(angle[:, t, :], rowp[:, R_FREQ:R_FREQ + 24], pos[:, t:t + 1], None, ALU.mult)
            order.after(ins)
            magic = 1.5 * 2.0 ** 23
            order.after(dve.tensor_scalar(turns[:, :, :], angle[:, :, :], 1.0 / (2.0 * math.pi), magic, ALU.mult, ALU.add))
            order.after(dve.tensor_scalar(turns[:, :, :], turns[:, :, :], magic, None, ALU.subtract))
            c1 = 6.28125
            c2 = float(np.float32(round((2 * math.pi - c1) * 2 ** 20) / 2 ** 20))
            c3 = float(np.float32(2 * math.pi - c1 - c2))
            for c in (c1, c2, c3):
                order.after(dve.scalar_tensor_tensor(out=angle[:, :, :], in0=turns[:, :, :], scalar=-c, in1=angle[:, :, :],
                                                     op0=ALU.mult, op1=ALU.add))
            pi_below = 3.1415925
            order.after(dve.tensor_scalar(angle[:, :, :], angle[:, :, :], pi_below, -pi_below, ALU.min, ALU.max))
            order.after(dve.scalar_tensor_tensor(out=turns[:, :, :], in0=angle[:, :, :], scalar=-1.0, in1=angle[:, :, :],
                                                 op0=ALU.mult, op1=ALU.min))
            dve.tensor_scalar(turns[:, :, :], turns[:, :, :], math.pi / 2, None, ALU.add).then_inc(trig_in, 1)
            project(1, 1, z_even, rstd[0][:, 1:2])
            group_sums(1, 0, mix[:, :, 0:512], 8, HD, 1)
            dve.wait_ge(cum_done, 1)
            dve.tensor_copy(cum[:, :, :], bank[1][:, 256:272].rearrange("p (t h) -> p t h", t=T)).then_inc(cum_ready, 1)
            dve.wait_ge(cum_ready, 1)
            dve.wait_ge(cum_done, 2)
            dve.wait_ge(even_tables, 4)

            def forget_biases(heads):
                for h in heads:
                    b = bank[4 + h // 2][:, (h % 2) * SEQ:(h % 2 + 1) * SEQ]
                    dve.scalar_tensor_tensor(out=bias_b[:, h, 0:256], in0=b, scalar=cum[:, 1, h:h + 1], in1=causal,
                                             op0=ALU.add, op1=ALU.add)
                    ins = dve.scalar_tensor_tensor(out=bias_b[:, h, 256:384], in0=b[:, 0:P], scalar=cum[:, 0, h:h + 1],
                                                   in1=causal[:, P:], op0=ALU.add, op1=ALU.add)
                return ins

            forget_biases(range(5))
            split_lo(dve, 3)
            unit_z_dve(dve, 2, z_even, rstd[0][:, 1:2])
            group_sums(1, 8, mix[:, :, 512:1024], 8, HD, 2).then_inc(ms_ready[1], 1)
            forget_biases(range(5, 8)).then_inc(bias_ready, 1)
            newton_dve(dve, order, 1)
            split_lo(dve, 4)
            unit_z_dve(dve, 3, z_even, rstd[0][:, 1:2])
            dve.wait_ge(lam_ready, 1)
            static_attention("AB")
            turn_dve(dve, "even_mix", 4, 8)
            project_x(first["even_out"])
            first_unit("odd", 3, first["odd_in"], z_odd)
            project(first["odd_in"] + 1, 1, z_odd, rstd[3][:, 1:2])
            group_sums(4, 0, mix[:, :, 0:640], 10, HD, 6).then_inc(ms_ready[4], 1)
            newton_dve(dve, order, 4)
            split_lo(dve, first["odd_in"] + 3)
            unit_z_dve(dve, first["odd_in"] + 2, z_odd, rstd[3][:, 1:2])
            dve.wait_ge(tables, 9)
            static_attention("CD")
            turn_dve(dve, "odd_mix", 4, 8)
            project_x(first["odd_out"])
            u = first["dsa_in"]
            first_unit("dsa", 5, u, z_dsa)
            project(u + 1, 1, z_dsa, rstd[5][:, 1:2])

            def rope(groups):
                parts = []
                for v, f0, half, at in groups:
                    heads = v.shape[2]
                    cos = cosine[:, :, f0:f0 + half].unsqueeze(2).to_broadcast([P, T, heads, half])
                    sin = sine[:, :, f0:f0 + half].unsqueeze(2).to_broadcast([P, T, heads, half])
                    a, b = v[:, :, :, 0:half], v[:, :, :, half:2 * half]
                    n = T * heads * half
                    flat = mix[:, :, :].rearrange("p t n -> p (t n)")
                    tmp = [flat[:, at + n * m:at + n * (m + 1)].rearrange("p (t h d) -> p t h d", t=T, h=heads) for m in range(4)]
                    dve.tensor_tensor(tmp[0], a, cos, ALU.mult)
                    dve.tensor_tensor(tmp[1], b, sin, ALU.mult)
                    dve.tensor_tensor(tmp[2], b, cos, ALU.mult)
                    last = dve.tensor_tensor(tmp[3], a, sin, ALU.mult)
                    parts.append((a, b, tmp))
                order.after(last)
                for a, b, tmp in parts:
                    dve.tensor_tensor(a, tmp[0], tmp[1], ALU.subtract)
                    last = dve.tensor_tensor(b, tmp[2], tmp[3], ALU.add)
                return last

            dve.wait_ge(trig_ready, 1)

            def evacuated(u):
                dve.wait_ge(evac_act, act_after[u])
                dve.wait_ge(evac_dve, dve_after[u])

            def rotated(v, lo, hi, width, at, rot):
                return v[:, :, lo:hi].rearrange("p t (h d) -> p t h d", d=width)[:, :, :, at:at + rot]

            evacuated(u + 1)
            rope([(rotated(z_dsa, 1536, 2112, HD, 0, 16), 0, 8, 0)]).then_inc(roped, 1)
            order.after(dve.tensor_scalar(wi[:, :, :], z_dsa[:, :, 2112:2120], (8 ** -0.5) * (HD ** -0.5), None, ALU.mult))
            split_lo(dve, u + 3)
            unit_z_dve(dve, u + 2, z_dsa, rstd[5][:, 1:2])
            halves = ((1, slice(0, 256)), (0, slice(256, 384)))

            def logits(heads):
                for h in heads:
                    dve.wait_ge(logits_relu, h + 1)
                    for t, cols in halves:
                        if h == 0:
                            ins = dve.tensor_scalar(score[:, cols], rl[:, 0, cols], wi[:, t, 0:1], None, ALU.mult)
                        else:
                            ins = dve.scalar_tensor_tensor(out=score[:, cols], in0=rl[:, h % 2, cols], scalar=wi[:, t, h:h + 1],
                                                           in1=score[:, cols], op0=ALU.mult, op1=ALU.add)
                    ins.then_inc(logits_added, 1)
                    dve.wait_ge(logits_added, h + 1)

            logits(range(4))
            split_lo(dve, u + 4)
            logits(range(4, 8))
            for t, cols in halves:
                ins = dve.scalar_tensor_tensor(out=score[:, cols], in0=chunked[:, SEQ - (cols.stop - cols.start):],
                                               scalar=HIDDEN / MASKED, in1=score[:, cols], op0=ALU.mult, op1=ALU.add)
            order.after(ins)
            for taken in range(TOPK // 8):
                if taken == 2:
                    evacuated(u + 2)
                    rope([(rotated(z_dsa, 1024, 1280, HD, 0, 16), 0, 8, 576)]).then_inc(roped, 1)
                if taken == 5:
                    unit_z_dve(dve, u + 3, z_dsa, rstd[5][:, 1:2])
                    evacuated(u + 3)
                    rope([(rotated(z_dsa, 0, 512, HD, 0, 16), 0, 8, 832)])
                if taken == 6:
                    unit_z_dve(dve, u + 4, z_dsa, rstd[5][:, 1:2])
                    evacuated(u + 4)
                    rope([(rotated(z_dsa, 512, 1024, HD, 0, 16), 0, 8, 1344)]).then_inc(roped, 1)
                for t, cols in halves:
                    ins = dve.max(best[:, t, :], score[:, cols])
                order.after(ins)
                for t, cols in halves:
                    ins = dve.match_replace(score[:, cols], best[:, t, :], score[:, cols], TAKEN)
                order.after(ins)
            order.after(dve.tensor_scalar(bias_s, score, (HIDDEN + TAKEN) / 2, MASKED, ALU.is_gt, ALU.mult))


            def looped_attention(first_pair, biases, scale, dst, split=None):
                if split is not None:
                    split_lo_half(dve, split, 0)
                row_max_dve(dve, first_pair, 0, biases, scale)
                if split is not None:
                    split_lo_half(dve, split, 1)

                def step(g, p, dst_before, maxima=True):
                    if maxima:
                        row_max_dve(dve, g + 1, 1 - p, biases, scale)
                    pt_evac_dve(dve, g, p)
                    inv_sum_dve(dve, g, p)
                    if dst_before is not None:
                        heads_out_dve(dve, g - 1, 1 - p, dst_before)

                step(first_pair, 0, None)
                step(first_pair + 1, 1, dst(0))
                with dve.Fori(0, 2) as i:
                    for j in range(2):
                        step(i * 2 + (first_pair + 2 + j), j, dst(i * 2 + (1 + j)))
                step(first_pair + 6, 0, dst(5))
                step(first_pair + 7, 1, dst(6), maxima=False)
                heads_out_dve(dve, first_pair + 7, 1, dst(7))

            def sparse_out(i):
                return mix[:, :, :].rearrange("p t (c s) -> p c t s", c=2)[:, :, :, bass.ds(i * HD, HD)]

            def latent_out(i):
                return mix[:, :, bass.ds(i * P, P)].rearrange("p t (c d) -> p c t d", c=2)

            looped_attention(PAIRS["S"], [(bias_s[:, 0:256], bias_s[:, 256:384])] * 2, 1.0, sparse_out, first["dsa_out"])
            turn_dve(dve, "dsa_mix")
            project_x(first["dsa_out"])

            def mlp(m):
                r, u = (6, 9)[m], first[f"mlp{m}"]
                turn_dve(dve, f"mlp{m}")
                split_lo(dve, u + 1)
                newton_dve(dve, order, r, square=rstd_sq[m][:, :])

                def up(v, b, i=None):
                    if b:
                        split_lo(dve, v + 1, i, 4)
                    base = 2 * FF_BLOCKS * m + 2 * b
                    if base > 0:
                        dve.wait_ge(u_lo_done, base if i is None else i * 4 + base)
                    for j in range(2):
                        dve.wait_ge(relu_done, base + j + 1 if i is None else i * 4 + (base + j + 1))
                        dve.tensor_tensor(sq[j][:, :], relu[j][:, :], relu[j][:, :], ALU.mult).then_inc(sq_done, 1)
                    for j in range(2):
                        dve.wait_ge(u_hi_done, base + j + 1 if i is None else i * 4 + (base + j + 1))
                        dve.tensor_tensor(u_lo[b % 2][:, 2 * j:2 * j + 2, :], sq[j][:, :].rearrange("p (f q) -> p f q", f=2),
                                          u_hi[b % 2][:, 2 * j:2 * j + 2, :].bitcast(F32), ALU.subtract).then_inc(u_lo_done, 1)

                up(u, 0)
                up(u + 1, 1)
                split_lo(dve, u + 3)
                up(u + 3, 2)
                split_lo(dve, u + 5)
                with dve.Fori(0, 2) as i:
                    up(u + 5, 3, i)
                    split_lo(dve, u + 7, i, 4)
                    up(u + 7, 4, i)
                    split_lo(dve, u + 9, i, 4)
                up(u + 13, 7)
                split_lo(dve, u + 15)
                split_lo(dve, u + 16)
                dve.wait_ge(mm_done, mm_after[u + 15])
                dve.wait_ge(rstd_ready[r], 1)
                for half in range(2):
                    for t in range(T):
                        cols = slice(half * BLOCK, (half + 1) * BLOCK)
                        ins = dve.scalar_tensor_tensor(out=x[:, t, cols], in0=bank[4 + 2 * t + half][:, :],
                                                       scalar=rstd_sq[m][:, t:t + 1], in1=x[:, t, cols], op0=ALU.mult, op1=ALU.add)
                    ins.then_inc(x_ready, 1)

            mlp(0)
            first_unit("mla", 7, first["mla_in"], z_mla)
            project(first["mla_in"] + 1, 1, z_mla, rstd[7][:, 1:2])
            turn_dve(dve, "latent")
            u = first["q_up"]
            newton_dve(dve, order, 8)
            split_lo(dve, u + 1)
            dve.wait_ge(rstd_ready[8], 1)
            unit_z_dve(dve, u, q_full, rstd[8][:, 1:2])
            evacuated(first["mla_in"])
            order.after(rope([(rotated(z_mla, 640, 672, 32, 0, 32), 8, 16, 1024)]))
            q_rope = rotated(q_full, 0, Q_UP, 96, 64, 32)
            split_lo(dve, u + 2)
            evacuated(u)
            rope([(q_rope[:, :, 0:8, :], 8, 16, 0)])
            unit_z_dve(dve, u + 1, q_full, rstd[8][:, 1:2])
            evacuated(u + 1)
            rope([(q_rope[:, :, 8:16, :], 8, 16, 1024)]).then_inc(mla_roped, 1)
            unit_z_dve(dve, first["kv_up"], kv_full, rstd[8][:, 3:4], (0, 1, 2))
            split_lo_half(dve, first["mla_out"], 0)
            unit_z_dve(dve, first["kv_up"], kv_full, rstd[8][:, 3:4], (3,))
            split_lo_half(dve, first["mla_out"], 1)
            looped_attention(PAIRS["L"], [(chunked[:, :], chunked[:, P:])] * 2, 96 ** -0.5, latent_out)
            turn_dve(dve, "mla_mix")
            project_x(first["mla_out"])
            mlp(1)
            dve.wait_ge(*X_READY["final"])
            dve.tensor_tensor_reduce(mix[:, 1, :], x[:, 1, :], x[:, 1, :], 1.0 / DM, 0.0, ALU.mult, ALU.add,
                                     ms[10][:, 1:2]).then_inc(ms_ready[10], 1)
            dve.wait_ge(ms_ready[10], 1)
            dve.wait_ge(final_loaded, 16)
            dve.tensor_tensor(mix[:, :, :], x[:, :, :], g_final[:, :].unsqueeze(1).to_broadcast([P, T, DM]), ALU.mult)\
                .then_inc(gained, 1)
            newton_dve(dve, order, 10)
            dve.wait_ge(rstd_ready[10], 1)
            dve.wait_ge(gained, 1)
            dve.tensor_scalar(mix[:, 1, :], mix[:, 1, :], rstd[10][:, 1:2], None, ALU.mult).then_inc(final_dve, 1)


WEIGHTS = {"even_in": "even_w_in", "even_out": "even_w_out", "odd_in": "odd_w_in", "odd_out": "odd_w_out",
           "dsa_in": "a_w_in_2", "dsa_out": "a_w_out_2", "mla_in": "b_w_in_2", "q_up": "b_w_q_up_2",
           "kv_up": "b_w_kv_up_2", "mla_out": "b_w_out_2"}


def kernel(**inputs):
    import concourse.bacc as bacc
    from concourse.bass_utils import run_bass_kernel_spmd

    a = {k: np.ascontiguousarray(v) for k, v in inputs.items()}
    arrays = {name: a[key][0] for name, key in WEIGHTS.items()}
    for m in range(2):
        arrays[f"up{m}"] = a["mlp_w_up_2"][m]
        arrays[f"down{m}"] = a["mlp_w_down_2"][m]
    rows = [a["even_ln_g"], a["odd_ln_g"], a["attn_norm_2"], a["mlp_norm_2"], a["b_q_norm_2"], a["b_kv_norm_2"], a["a_subln_g"]]
    for k in ("a", "b", "c", "d"):
        for which in ("q", "k"):
            rows += [a[f"{k}_{which}_norm_g"]] * 2
    arrays["gain_rows"] = np.concatenate([r.reshape(-1) for r in rows]).reshape(GAIN_ROWS, P)
    freq = [500000.0 ** (-np.arange(0, rot, 2) / rot) for rot in (16, 32)]
    params = [a["a_lambda_q1"], a["a_lambda_k1"], a["a_lambda_q2"], a["a_lambda_k2"], a["b_forget_bias"], a["c_sinks"]]
    arrays["row_params"] = np.concatenate([r.reshape(-1) for r in params] + [f.astype(np.float32) for f in freq])
    table = a["d_rel_bias"][0]
    entry = np.clip(np.arange(P)[:, None] + P - np.arange(SEQ)[None, :] + 63, 0, table.shape[1] - 1)
    arrays["rel_band"] = np.ascontiguousarray(table[:, entry].transpose(1, 0, 2))
    arrays["x"] = a["x"][0]
    arrays["positions"] = np.ascontiguousarray(a["positions_2"][0].reshape(T, P).T)
    arrays["final_gain"] = a["final_norm_2"]

    nc = bacc.Bacc("TRN2", target_bir_lowering=False, num_devices=1)
    aps = {k: nc.dram_tensor(f"in_{k}", v.shape, mybir.dt.from_np(v.dtype), kind="ExternalInput").ap() for k, v in arrays.items()}
    out = nc.dram_tensor("out", (SEQ, DM), F32, kind="ExternalOutput").ap()
    program(nc, aps, aps["x"], aps["gain_rows"], aps["row_params"], aps["positions"], aps["rel_band"], aps["final_gain"], out)
    r = run_bass_kernel_spmd(nc, [{f"in_{k}": v for k, v in arrays.items()}], core_ids=[0])
    return r.results[0]["out"].reshape(1, SEQ, DM)
```
